# Optimizing a Trainium2 kernel written in Bass

```python
import math
import jax, jax.numpy as jnp
from jax import lax
import numpy as np

D_MODEL = 1024
BATCH = 1
SEQ = 1024
DEPTH = 1
DEC_BATCH = 8
DEC_SEQ = 16
PAST_LEN = 1024

CHUNK = 64
Q_BLOCK = 128
ROPE_THETA = 10000.0
EPS = 1e-6
NEG = -1e30
MACARON = 0.5
D_FF = 2816
ATT_HEADS = 4
ATT_DH = 64
ATT_QK_W = ATT_HEADS * 2 * ATT_DH
ATT_V_W = ATT_HEADS * 2 * ATT_DH
RW_HEAD = 64
RW_W = D_MODEL // 2
RW_HEADS = RW_W // RW_HEAD
W_LORA = 64
A_LORA = 64
G_LORA = 128
SHIFT_W = 3 * RW_W + W_LORA + A_LORA + G_LORA
LNX_EPS = 64e-5
GATE_W = 2 * D_MODEL
IN_W = 2 * ATT_QK_W + ATT_V_W + SHIFT_W + GATE_W

kernel_name = 'hybrid_diffattn_rwkv7_macaron_step'

def rms_norm(x, g, eps=EPS):
    xf = x.astype(jnp.float32)
    y = xf * lax.rsqrt(jnp.mean(xf * xf, axis=-1, keepdims=True) + eps)
    return (y * g.astype(jnp.float32)).astype(x.dtype)

def swiglu(x, w_in, w_out):
    gate, up = jnp.split(x @ w_in, 2, axis=-1)
    return (jax.nn.silu(gate) * up) @ w_out

def sandwich_ffn(x, pre_g, w_in, w_out, post_g):
    return x + MACARON * rms_norm(swiglu(rms_norm(x, pre_g), w_in, w_out), post_g)

def rope(x, pos):
    half = ATT_DH // 2
    inv = ROPE_THETA ** (-jnp.arange(half, dtype=jnp.float32) / half)
    ang = pos.astype(jnp.float32)[:, None] * inv[None, :]
    cos = jnp.cos(ang)[None, :, None, None, :]
    sin = jnp.sin(ang)[None, :, None, None, :]
    xf = x.astype(jnp.float32)
    x1, x2 = xf[..., :half], xf[..., half:]
    return jnp.concatenate([x1 * cos - x2 * sin, x1 * sin + x2 * cos], axis=-1).astype(x.dtype)

def diff_core(q, k, v, lam, mask):
    s = jnp.einsum('bqhmd,bkhmd->bhmqk', q, k).astype(jnp.float32) * (ATT_DH ** -0.5)
    if mask is not None:
        s = jnp.where(mask, s, NEG)
    pr = jax.nn.softmax(s, axis=-1)
    a = pr[:, :, 0] - lam * pr[:, :, 1]
    return jnp.einsum('bhqk,bkhe->bqhe', a, v.astype(jnp.float32))

def diff_attention(z_q, z_k, z_v, pos, lam, lam_init, subln_g, cache_k, cache_v):
    B, T, _ = z_q.shape
    q = rope(z_q.reshape(B, T, ATT_HEADS, 2, ATT_DH), pos)
    k = rope(z_k.reshape(B, T, ATT_HEADS, 2, ATT_DH), pos)
    v = z_v.reshape(B, T, ATT_HEADS, 2 * ATT_DH)
    if cache_k is None:
        nb = T // Q_BLOCK
        qb = jnp.moveaxis(q.reshape(B, nb, Q_BLOCK, ATT_HEADS, 2, ATT_DH), 1, 0)
        key_chunk = jnp.arange(T) // CHUNK

        def block(args):
            qi, bi = args
            q_chunk = (bi * Q_BLOCK + jnp.arange(Q_BLOCK)) // CHUNK
            mask = key_chunk[None, :] <= q_chunk[:, None]
            return diff_core(qi, k, v, lam, mask)

        o = lax.map(block, (qb, jnp.arange(nb)))
        o = jnp.moveaxis(o, 0, 1).reshape(B, T, ATT_HEADS, 2 * ATT_DH)
    else:
        keys = jnp.concatenate([cache_k.astype(k.dtype), k], axis=1)
        vals = jnp.concatenate([cache_v.astype(v.dtype), v], axis=1)
        o = diff_core(q, keys, vals, lam, None)
    o = o * lax.rsqrt(jnp.mean(o * o, axis=-1, keepdims=True) + EPS) * subln_g.astype(jnp.float32) * (1.0 - lam_init)
    return o.reshape(B, T, ATT_V_W).astype(z_v.dtype), k, v

def wkv7_scan(r, decay, k, v, kk, a, S0):
    def step(S, inp):
        r_t, w_t, k_t, v_t, kk_t, a_t = inp
        sa = jnp.einsum('bhij,bhj->bhi', S, -kk_t)
        S = S * w_t[:, :, None, :] + sa[..., None] * (kk_t * a_t)[:, :, None, :] + v_t[..., None] * k_t[:, :, None, :]
        y = jnp.einsum('bhij,bhj->bhi', S, r_t)
        return S, y

    xs = tuple(jnp.moveaxis(t, 1, 0) for t in (r, decay, k, v, kk, a))
    S, ys = lax.scan(step, S0, xs)
    return jnp.moveaxis(ys, 0, 1), S

def rwkv7_branch(z_rw, S0, shift0, p):
    B, T, _ = z_rw.shape
    prev = jnp.concatenate([shift0.astype(z_rw.dtype), z_rw[:, :-1]], axis=1)
    zs = (z_rw + (prev - z_rw) * p['rwkv_mu']).astype(jnp.float32)
    r, k, v, zw, za, zg = jnp.split(zs, [RW_W, 2 * RW_W, 3 * RW_W, 3 * RW_W + W_LORA, 3 * RW_W + W_LORA + A_LORA], axis=-1)
    w = -jax.nn.softplus(-(p['rwkv_w0'].astype(jnp.float32) + jnp.tanh(zw) @ p['rwkv_w2'].astype(jnp.float32))) - 0.5
    decay = jnp.exp(-jnp.exp(w))
    a = jax.nn.sigmoid(p['rwkv_a0'].astype(jnp.float32) + za @ p['rwkv_a2'].astype(jnp.float32))
    g = jax.nn.sigmoid(zg) @ p['rwkv_g2'].astype(jnp.float32)
    heads = lambda t: t.reshape(B, T, RW_HEADS, RW_HEAD)
    kk = heads(k * p['rwkv_k_k'].astype(jnp.float32))
    kk = kk / jnp.maximum(jnp.sqrt(jnp.sum(kk * kk, axis=-1, keepdims=True)), 1e-12)
    k = k * (1.0 + (a - 1.0) * p['rwkv_k_a'].astype(jnp.float32))
    rh, kh, vh, ah, dh = heads(r), heads(k), heads(v), heads(a), heads(decay)
    y, S = wkv7_scan(rh, dh, kh, vh, kk, ah, S0.astype(jnp.float32))
    mu = jnp.mean(y, axis=-1, keepdims=True)
    var = jnp.mean(jnp.square(y - mu), axis=-1, keepdims=True)
    y = ((y - mu) * lax.rsqrt(var + LNX_EPS)).reshape(B, T, RW_W)
    y = y * p['rwkv_lnx_g'].astype(jnp.float32) + p['rwkv_lnx_b'].astype(jnp.float32)
    bonus = jnp.sum(rh * kh * p['rwkv_r_k'].astype(jnp.float32), axis=-1, keepdims=True) * vh
    out = (y + bonus.reshape(B, T, RW_W)) * g
    return out.astype(z_rw.dtype), S, z_rw[:, -1:]

def layer(x, pos, l, p, cache_k, cache_v, S0, shift0):
    h = sandwich_ffn(x, p['ffn1_pre_g'], p['ffn1_w_in'], p['ffn1_w_out'], p['ffn1_post_g'])
    u = rms_norm(h, p['mix_pre_g'])
    z = u @ p['w_in']
    o1 = ATT_QK_W
    o2 = 2 * ATT_QK_W
    o3 = o2 + ATT_V_W
    o4 = o3 + SHIFT_W
    z_q, z_k, z_v, z_rw, z_g = jnp.split(z, [o1, o2, o3, o4], axis=-1)
    lam_init = 0.8 - 0.6 * math.exp(-0.3 * l)
    f32 = lambda t: t.astype(jnp.float32)
    lam = (jnp.exp(jnp.sum(f32(p['att_lambda_q1']) * f32(p['att_lambda_k1'])))
           - jnp.exp(jnp.sum(f32(p['att_lambda_q2']) * f32(p['att_lambda_k2']))) + lam_init)
    o_att, k_rows, v_rows = diff_attention(z_q, z_k, z_v, pos, lam, lam_init, p['att_subln_g'], cache_k, cache_v)
    o_rw, S, shift = rwkv7_branch(z_rw, S0, shift0, p)
    gate_att, gate_rw = jnp.split(jax.nn.sigmoid(z_g), 2, axis=-1)
    merged = gate_att * (o_att @ p['w_o_att']) + gate_rw * (o_rw @ p['w_o_rwkv'])
    h = h + rms_norm(merged @ p['w_out'], p['mix_post_g'])
    y = sandwich_ffn(h, p['ffn2_pre_g'], p['ffn2_w_in'], p['ffn2_w_out'], p['ffn2_post_g'])
    return y, k_rows, v_rows, S, shift

def setup_inputs(seed: int = 0) -> dict:
    key = jax.random.key(seed)
    ks = iter(jax.random.split(key, 48))
    L = DEPTH

    def nrm(shape, scale):
        return scale * jax.random.normal(next(ks), shape, jnp.float32)

    def gain(n):
        return 1.0 + nrm((L, n), 0.05)

    return {
        'x_prompt': nrm((BATCH, SEQ, D_MODEL), 1.0),
        'x_sample': nrm((DEC_BATCH, DEC_SEQ, D_MODEL), 1.0),
        'cache_att_k': nrm((L, DEC_BATCH, PAST_LEN, ATT_HEADS, 2, ATT_DH), 1.0),
        'cache_att_v': nrm((L, DEC_BATCH, PAST_LEN, ATT_HEADS, 2 * ATT_DH), 1.0),
        'state_rwkv': nrm((L, DEC_BATCH, RW_HEADS, RW_HEAD, RW_HEAD), 0.3),
        'state_shift': nrm((L, DEC_BATCH, 1, SHIFT_W), 1.0),
        'ffn1_pre_g': gain(D_MODEL),
        'ffn1_w_in': nrm((L, D_MODEL, 2 * D_FF), D_MODEL ** -0.5),
        'ffn1_w_out': nrm((L, D_FF, D_MODEL), D_FF ** -0.5),
        'ffn1_post_g': gain(D_MODEL),
        'mix_pre_g': gain(D_MODEL),
        'w_in': nrm((L, D_MODEL, IN_W), D_MODEL ** -0.5),
        'att_lambda_q1': nrm((L, ATT_DH), 0.1),
        'att_lambda_k1': nrm((L, ATT_DH), 0.1),
        'att_lambda_q2': nrm((L, ATT_DH), 0.1),
        'att_lambda_k2': nrm((L, ATT_DH), 0.1),
        'att_subln_g': gain(2 * ATT_DH),
        'rwkv_mu': jax.random.uniform(next(ks), (L, SHIFT_W), jnp.float32),
        'rwkv_w0': jax.random.uniform(next(ks), (L, RW_W), jnp.float32, minval=-6.0, maxval=0.0),
        'rwkv_w2': nrm((L, W_LORA, RW_W), 0.5 * W_LORA ** -0.5),
        'rwkv_a0': nrm((L, RW_W), 0.1),
        'rwkv_a2': nrm((L, A_LORA, RW_W), 0.5 * A_LORA ** -0.5),
        'rwkv_g2': nrm((L, G_LORA, RW_W), G_LORA ** -0.5),
        'rwkv_k_k': 0.85 + nrm((L, RW_W), 0.05),
        'rwkv_k_a': 1.0 + nrm((L, RW_W), 0.05),
        'rwkv_r_k': nrm((L, RW_HEADS, RW_HEAD), 0.1),
        'rwkv_lnx_g': gain(RW_W),
        'rwkv_lnx_b': nrm((L, RW_W), 0.02),
        'w_o_att': nrm((L, ATT_V_W, D_MODEL), ATT_V_W ** -0.5),
        'w_o_rwkv': nrm((L, RW_W, D_MODEL), RW_W ** -0.5),
        'w_out': nrm((L, D_MODEL, D_MODEL), D_MODEL ** -0.5),
        'mix_post_g': gain(D_MODEL),
        'ffn2_pre_g': gain(D_MODEL),
        'ffn2_w_in': nrm((L, D_MODEL, 2 * D_FF), D_MODEL ** -0.5),
        'ffn2_w_out': nrm((L, D_FF, D_MODEL), D_FF ** -0.5),
        'ffn2_post_g': gain(D_MODEL),
    }

def reference(x_prompt, x_sample, cache_att_k, cache_att_v, state_rwkv, state_shift,
              ffn1_pre_g, ffn1_w_in, ffn1_w_out, ffn1_post_g, mix_pre_g, w_in,
              att_lambda_q1, att_lambda_k1, att_lambda_q2, att_lambda_k2, att_subln_g,
              rwkv_mu, rwkv_w0, rwkv_w2, rwkv_a0, rwkv_a2, rwkv_g2, rwkv_k_k, rwkv_k_a,
              rwkv_r_k, rwkv_lnx_g, rwkv_lnx_b, w_o_att, w_o_rwkv, w_out, mix_post_g,
              ffn2_pre_g, ffn2_w_in, ffn2_w_out, ffn2_post_g):
    Bp, Tp, _ = x_prompt.shape
    Bs, Ts, _ = x_sample.shape
    past = cache_att_k.shape[2]
    pos_p = jnp.arange(Tp)
    pos_s = past + jnp.arange(Ts)
    xp, xs = x_prompt, x_sample
    kp_l, vp_l, sp_l, shp_l = [], [], [], []
    ks_l, vs_l, ss_l, shs_l = [], [], [], []
    for l in range(DEPTH):
        p = dict(
            ffn1_pre_g=ffn1_pre_g[l], ffn1_w_in=ffn1_w_in[l], ffn1_w_out=ffn1_w_out[l], ffn1_post_g=ffn1_post_g[l],
            mix_pre_g=mix_pre_g[l], w_in=w_in[l],
            att_lambda_q1=att_lambda_q1[l], att_lambda_k1=att_lambda_k1[l],
            att_lambda_q2=att_lambda_q2[l], att_lambda_k2=att_lambda_k2[l], att_subln_g=att_subln_g[l],
            rwkv_mu=rwkv_mu[l], rwkv_w0=rwkv_w0[l], rwkv_w2=rwkv_w2[l], rwkv_a0=rwkv_a0[l], rwkv_a2=rwkv_a2[l],
            rwkv_g2=rwkv_g2[l], rwkv_k_k=rwkv_k_k[l], rwkv_k_a=rwkv_k_a[l], rwkv_r_k=rwkv_r_k[l],
            rwkv_lnx_g=rwkv_lnx_g[l], rwkv_lnx_b=rwkv_lnx_b[l],
            w_o_att=w_o_att[l], w_o_rwkv=w_o_rwkv[l], w_out=w_out[l], mix_post_g=mix_post_g[l],
            ffn2_pre_g=ffn2_pre_g[l], ffn2_w_in=ffn2_w_in[l], ffn2_w_out=ffn2_w_out[l], ffn2_post_g=ffn2_post_g[l],
        )
        S0p = jnp.zeros((Bp, RW_HEADS, RW_HEAD, RW_HEAD), jnp.float32)
        sh0p = jnp.zeros((Bp, 1, SHIFT_W), xp.dtype)
        xp, kp, vp, Sp, shp = layer(xp, pos_p, l, p, None, None, S0p, sh0p)
        xs, kn, vn, Sn, shn = layer(xs, pos_s, l, p, cache_att_k[l], cache_att_v[l], state_rwkv[l], state_shift[l])
        kp_l.append(kp); vp_l.append(vp); sp_l.append(Sp); shp_l.append(shp)
        ks_l.append(kn); vs_l.append(vn); ss_l.append(Sn); shs_l.append(shn)
    new_k_prompt = jnp.stack(kp_l, 0)
    new_v_prompt = jnp.stack(vp_l, 0)
    new_rwkv_prompt = jnp.stack(sp_l, 0)
    new_shift_prompt = jnp.stack(shp_l, 0)
    new_k_sample = jnp.stack(ks_l, 0)
    new_v_sample = jnp.stack(vs_l, 0)
    new_rwkv_sample = jnp.stack(ss_l, 0)
    new_shift_sample = jnp.stack(shs_l, 0)
    return (xp, xs, new_k_prompt, new_v_prompt, new_rwkv_prompt, new_shift_prompt,
            new_k_sample, new_v_sample, new_rwkv_sample, new_shift_sample)


_drawn_inputs = setup_inputs


def setup_inputs(seed=0):
    import zlib

    import numpy as np

    out = dict(_drawn_inputs(seed))
    spreads = {}
    factors = {'att_lambda_q2': 200.0,
     'rwkv_lnx_g': 3.213,
     'rwkv_lnx_b': 7.838,
     'ffn2_post_g': 3.72,
     'att_subln_g': 3.045}
    for name, (base, spread) in spreads.items():
        noise = np.random.default_rng([zlib.crc32(name.encode()), seed]).standard_normal(out[name].shape)
        drawn = base * np.exp(spread * noise) if base else spread * noise
        out[name] = __import__('jax').numpy.asarray(drawn.astype(out[name].dtype))
    for name, factor in factors.items():
        out[name] = (out[name] * factor).astype(out[name].dtype)
    return out
```

```python
from contextlib import ExitStack, contextmanager

import numpy as np

import concourse.bass as bass
from concourse import mybir

F32 = mybir.dt.float32
F32R = mybir.dt.float32r
ALU = mybir.AluOpType
ACT = mybir.ActivationFunctionType
AX = mybir.AxisListType.X

P = 128
D = 1024
DT = D // P
SEQ = 1024
NB = 8
NQ = 16
TOK = SEQ + NB * NQ
HALF = TOK // 2
NN = HALF // 2
FF = 2816
FT = FF // P
KS = 4
EPS = 1e-6
Z_TILES = 42
Z_GATES = 16
ZQ, ZK, ZV, ZR = 0, 4, 8, 12
HEADS = 4
SCALE = 64 ** -0.5
CHUNK = 64
RT = 4
ZRT = 14
KAPPA = float(np.exp(-0.5))
LAM_INIT = 0.8 - 0.6
PAST = 1024

VECS = [("ffn1_pre_g", 8), ("ffn1_post_g", 8), ("mix_pre_g", 8), ("mix_post_g", 8), ("ffn2_pre_g", 8),
        ("ffn2_post_g", 8), ("rwkv_mu", 14), ("rwkv_w0", 4), ("rwkv_a0", 4), ("rwkv_k_k", 4),
        ("rwkv_k_a", 4), ("rwkv_r_k", 4), ("rwkv_lnx_g", 4), ("rwkv_lnx_b", 4), ("att_subln_g", 1)]
VEC_AT = {}
_at = 0
for _n, _k in VECS:
    VEC_AT[_n] = _at
    _at += _k
NVEC = _at


class Chain:

    def __init__(self, eng, sem):
        self.eng, self.sem, self.n = eng, sem, 0

    def mark(self, ins):
        ins.then_inc(self.sem, 1)
        self.n += 1

    def wait(self):
        self.eng.wait_ge(self.sem, self.n)

    def do(self, ins):
        self.mark(ins)
        self.wait()


@contextmanager
def stage(nc, tag):
    used = []
    with ExitStack() as buffers:
        sb = lambda n, s, d=F32: buffers.enter_context(nc.sbuf_tensor(tag + n, s, d))

        def sem(n):
            used.append(nc.alloc_semaphore(tag + n))
            return used[-1]

        with ExitStack() as ctx:
            yield ctx, sb, sem
        nc.clear_and_free_semaphores(used)
        nc.all_engine_barrier()


def feature_tiles(dram, t0, t1):
    return dram.rearrange("(k p) t -> p k t", p=P)[:, :, t0:t1]


def load_inputs(nc, t, S):
    with stage(nc, "li_") as (ctx, sb, sem):
        ps = S["ps"]
        rows = sb("rows", [NVEC, P])
        xtok = sb("xtok", [P, TOK // P, D])
        xfeat = sb("xfeat", [P, DT, TOK])
        consts_in, rows_in, x_in, stored = sem("consts_in"), sem("rows_in"), sem("x_in"), sem("stored")
        vec_t, vec_done, half_t, copied_a, copied_v = (sem(n) for n in ("vec_t", "vec_done", "half_t", "copied_a", "copied_v"))
        ones_set = sem("ones_set")
        block = ctx.enter_context(nc.Block())
        NT = TOK // P
        units = [(m, f) for m in range(NT) for f in range(2)]

        @block.sync
        def _(sp):
            sp.dma_start(S["ident"][:, :], t["c_ident"]).then_inc(consts_in, 16)
            at = 0
            for name, k in VECS:
                src = t[name].rearrange("a b c -> (a b c)") if len(t[name].shape) == 3 else t[name].rearrange("a b -> (a b)")
                sp.dma_start(rows[at:at + k, :], src.rearrange("(k p) -> k p", p=P)).then_inc(rows_in, 16)
                at += k
            sp.dma_start(xtok[:, 0:SEQ // P, :], t["x_prompt"].rearrange("b (n p) d -> p (b n) d", p=P)).then_inc(x_in, 16)
            sp.dma_start(xtok[:, SEQ // P, :], t["x_sample"].rearrange("b s d -> (b s) d")).then_inc(x_in, 16)
            sp.wait_ge(copied_a, len(units) // 2)
            sp.wait_ge(copied_v, len(units) // 2)
            sp.dma_start(feature_tiles(t["res0"], 0, TOK), xfeat[:, :, :]).then_inc(stored, 16)
            sp.wait_ge(stored, 16)

        @block.tensor
        def _(pe):
            pe.wait_ge(consts_in, 16)
            pe.wait_ge(rows_in, 16 * len(VECS))
            pe.transpose(ps[:, 7, 0:NVEC], rows[:, :], S["ident"][0:NVEC, 0:NVEC]).then_inc(vec_t, 1)
            pe.wait_ge(x_in, 32)
            for n, (m, f) in enumerate(units):
                if n >= 4:
                    pe.wait_ge(copied_a if n % 2 == 0 else copied_v, (n - 4) // 2 + 1)
                for i in range(4):
                    ins = pe.transpose(ps[:, n % 4, i * P:(i + 1) * P], xtok[:, m, (4 * f + i) * P:(4 * f + i + 1) * P], S["ident"][:, :])
                ins.then_inc(half_t, 1)

        def copy_out(n, m, f):
            return xfeat[:, 4 * f:4 * f + 4, m * P:(m + 1) * P], ps[:, n % 4, :].rearrange("p (i q) -> p i q", i=4)

        @block.scalar
        def _(act):
            for n, (m, f) in enumerate(units):
                if n % 2 == 0:
                    act.wait_ge(half_t, n + 1)
                    act.activation(*copy_out(n, m, f), ACT.Copy).then_inc(copied_a, 1)

        @block.vector
        def _(dve):
            dve.memset(S["ones"][:, :], 1.0).then_inc(ones_set, 1)
            dve.memset(S["eps"][:, :], EPS).then_inc(ones_set, 1)
            dve.memset(S["lnx_eps"][:, :], 64e-5).then_inc(ones_set, 1)
            dve.wait_ge(vec_t, 1)
            dve.tensor_copy(S["vec"][:, :], ps[:, 7, 0:NVEC]).then_inc(vec_done, 1)
            dve.wait_ge(vec_done, 1)
            for n in ("ffn1_post_g", "ffn2_post_g"):
                g = S["vec"][:, VEC_AT[n]:VEC_AT[n] + 8]
                dve.tensor_scalar(g, g, 0.5, None, ALU.mult).then_inc(vec_done, 1)
            for n, (m, f) in enumerate(units):
                if n % 2 == 1:
                    dve.wait_ge(half_t, n + 1)
                    dve.tensor_copy(*copy_out(n, m, f)).then_inc(copied_v, 1)


def ffn_half(nc, t, S, tag, half, res_in, res_out, w_in, w_out, pre, post):
    t0, t1 = half * HALF, (half + 1) * HALF
    with stage(nc, tag) as (ctx, sb, sem):
        ps = S["ps"]
        xn = {h: sb("xn" + h, [P, DT, HALF], F32R) for h in ("hi", "lo")}
        hid = {h: sb("hid" + h, [P, FT, HALF], F32R) for h in ("hi", "lo")}
        work = sb("work", [P, DT, HALF])
        tmp = sb("tmp", [P, 4, HALF])
        raw = sb("raw", [P, 4, KS, P])
        w = {h: sb("w" + h, [P, 4, KS, P], F32R) for h in ("hi", "lo")}
        sq, ssum, rstd = tmp[:, 0:2], tmp[:, 2], tmp[:, 3]
        x_in, squared, summed, sum_mm, rooted, scaled, xhi, xlo = (sem(n) for n in
            ("x_in", "squared", "summed", "sum_mm", "rooted", "scaled", "xhi", "xlo"))
        raw_in = [sem(f"raw_in{q}") for q in range(4)]
        whi, wlo, used, silu_done, prod_done, hhi, hlo, y_done, ysq, yadd, stored, dchain = (sem(n) for n in
            ("whi", "wlo", "used", "silu_done", "prod_done", "hhi", "hlo", "y_done", "ysq", "yadd", "stored", "dchain"))
        back_in = [sem(f"back_in{q}") for q in range(2)]
        block = ctx.enter_context(nc.Block())
        w_in_v = w_in.rearrange("(k p) n -> p k n", p=P)
        w_out_v = w_out.rearrange("(k p) n -> p k n", p=P)
        UP = 4
        N_UP = UP * FT
        DOWN = [(k, min(KS, FT - k)) for k in range(0, FT, KS)]
        ND = len(DOWN)
        vec = lambda name, k: S["vec"][:, VEC_AT[name] + k:VEC_AT[name] + k + 1]
        flat = lambda a: a.rearrange("p (n t) -> p n t", n=2)
        bank = lambda b: ps[:, b:b + 2, 0:NN]

        @block.sync
        def _(sp):
            for k in range(DT):
                sp.dma_start(work[:, k], feature_tiles(res_in, t0, t1)[:, k]).then_inc(x_in, 16)

            def up(j, r):
                for q in range(UP):
                    if not (isinstance(j, int) and 2 * j + r == 0):
                        sp.wait_ge(wlo, (2 * j + r - 1) * UP + q + 1)
                    col = (2 * j + r) * P + (q // 2) * FF
                    sp.dma_start(raw[:, q], w_in_v[:, (q % 2) * KS:(q % 2) * KS + KS, bass.ds(col, P)]).then_inc(raw_in[q], 16)

            up(0, 0)
            up(0, 1)
            with sp.Fori(1, FT // 2) as j:
                up(j, 0)
                up(j, 1)

            def down(j, first):
                for r in range(2):
                    for i, (k, n) in enumerate(DOWN):
                        s = r * ND + i
                        sp.wait_ge(wlo, N_UP + j * 2 * ND + s - 4 + 1)
                        sp.dma_start(raw[:, s % 4, 0:n], w_out_v[:, k:k + n, bass.ds((2 * j + r) * P, P)]).then_inc(raw_in[s % 4], 16)

            with sp.Fori(0, DT // 2) as j:
                down(j, False)
            for k in range(DT):
                sp.wait_ge(yadd, DT if k < 2 else DT + k - 1)
                sp.dma_start(tmp[:, k % 2], feature_tiles(res_in, t0, t1)[:, k]).then_inc(back_in[k % 2], 16)
                if k >= 1:
                    sp.wait_ge(yadd, DT + k)
                    sp.dma_start(feature_tiles(res_out, t0, t1)[:, k - 1], work[:, k - 1]).then_inc(stored, 16)
            sp.wait_ge(yadd, 2 * DT)
            sp.dma_start(feature_tiles(res_out, t0, t1)[:, DT - 1], work[:, DT - 1]).then_inc(stored, 16)
            sp.wait_ge(stored, 16 * DT)

        @block.scalar
        def _(act):
            for k in range(DT):
                act.wait_ge(x_in, 16 * DT)
                if k >= 2:
                    act.wait_ge(summed, k - 1)
                act.activation(sq[:, k % 2], work[:, k], ACT.Square).then_inc(squared, 1)
            act.wait_ge(sum_mm, 1)
            act.activation(flat(rstd), bank(0), ACT.Sqrt, bias=S["eps"][:, 0:1], scale=1.0 / D).then_inc(rooted, 1)
            for k in range(DT):
                act.wait_ge(scaled, k + 1)
                act.activation(xn["hi"][:, k], work[:, k], ACT.Copy).then_inc(xhi, 1)

            def split(j, r, first=False):
                for q in range(UP):
                    act.wait_ge(raw_in[q], 16 * (2 * j + r + 1))
                    if not first:
                        act.wait_ge(used, (2 * j + r - 1) * UP + q + 1)
                    act.activation(w["hi"][:, q], raw[:, q], ACT.Copy).then_inc(whi, 1)

            def finish(j, r):
                act.wait_ge(used, (2 * j + r) * UP + 2)
                act.activation(flat(work[:, r]), bank(4 * r), ACT.Silu).then_inc(silu_done, 1)
                act.wait_ge(prod_done, 2 * j + r + 1)
                act.activation(hid["hi"][:, bass.ds(2 * j + r, 1)], work[:, 2 + r:3 + r], ACT.Copy).then_inc(hhi, 1)

            def split_down(j, s, n):
                i = 2 * ND * j + s
                act.wait_ge(raw_in[s % 4], 16 * (FT + 2 * ND // 4 * j + s // 4 + 1))
                act.wait_ge(used, N_UP + i - 4 + 1)
                act.activation(w["hi"][:, s % 4, 0:n], raw[:, s % 4, 0:n], ACT.Copy).then_inc(whi, 1)

            def finish_down(j, r):
                act.wait_ge(used, N_UP + (2 * j + r + 1) * ND)
                act.activation(flat2(work[:, bass.ds(2 * j + r, 1)]), bank(4 * r), ACT.Copy).then_inc(y_done, 1)
                if not (isinstance(j, int) and j == 0):
                    act.wait_ge(yadd, 2 * j + r - 1)
                act.activation(flat(sq[:, r]), bank(4 * r), ACT.Square).then_inc(ysq, 1)

            flat2 = lambda a: a.rearrange("p o (n t) -> p (o n) t", n=2)
            split(0, 0, True)
            split(0, 1)
            finish(0, 0)
            with act.Fori(1, FT // 2) as j:
                split(j, 0)
                finish(j - 1, 1)
                split(j, 1)
                finish(j, 0)
            for i in range(4):
                split_down(0, i, DOWN[i][1])
            finish(FT // 2 - 1, 1)
            for i in range(4, 8):
                split_down(0, i, DOWN[i % ND][1])
            for s in range(8, 2 * ND):
                split_down(0, s, DOWN[s % ND][1])
            finish_down(0, 0)
            with act.Fori(1, DT // 2) as j:
                for s in range(4):
                    split_down(j, s, DOWN[s % ND][1])
                finish_down(j - 1, 1)
                for s in range(4, 2 * ND):
                    split_down(j, s, DOWN[s % ND][1])
                finish_down(j, 0)
            finish_down(DT // 2 - 1, 1)
            act.wait_ge(sum_mm, 2)
            act.activation(flat(rstd), bank(0), ACT.Sqrt, bias=S["eps"][:, 0:1], scale=1.0 / D).then_inc(rooted, 1)

        @block.vector
        def _(dve):
            own = Chain(dve, dchain)
            dve.wait_ge(squared, 2)
            dve.tensor_tensor(ssum, sq[:, 0], sq[:, 1], ALU.add).then_inc(summed, 2)
            dve.wait_ge(summed, 2)
            for k in range(2, DT):
                dve.wait_ge(squared, k + 1)
                dve.tensor_tensor(ssum, ssum, sq[:, k % 2], ALU.add).then_inc(summed, 1)
                dve.wait_ge(summed, k + 1)
            dve.wait_ge(rooted, 1)
            own.do(dve.reciprocal(rstd, rstd))
            for k in range(DT):
                dve.scalar_tensor_tensor(work[:, k], work[:, k], vec(pre, k), rstd, ALU.mult, ALU.mult).then_inc(scaled, 1)
            for k in range(DT):
                dve.wait_ge(xhi, k + 1)
                dve.tensor_tensor(xn["lo"][:, k], work[:, k], xn["hi"][:, k].bitcast(F32), ALU.subtract).then_inc(xlo, 1)
            dve.wait_ge(xlo, DT)

            def split(j, r):
                for q in range(UP):
                    dve.wait_ge(whi, (2 * j + r) * UP + q + 1)
                    dve.tensor_tensor(w["lo"][:, q], raw[:, q], w["hi"][:, q].bitcast(F32), ALU.subtract).then_inc(wlo, 1)

            def finish(j, r):
                dve.wait_ge(silu_done, 2 * j + r + 1)
                dve.wait_ge(used, (2 * j + r + 1) * UP)
                if not (isinstance(j, int) and j == 0):
                    dve.wait_ge(hlo, 2 * j + r - 1)
                dve.tensor_tensor(flat(work[:, 2 + r]), flat(work[:, r]), bank(4 * r + 2), ALU.mult).then_inc(prod_done, 1)
                dve.wait_ge(hhi, 2 * j + r + 1)
                dve.tensor_tensor(hid["lo"][:, bass.ds(2 * j + r, 1)], work[:, 2 + r:3 + r],
                                  hid["hi"][:, bass.ds(2 * j + r, 1)].bitcast(F32), ALU.subtract).then_inc(hlo, 1)

            def split_down(j, s, n):
                dve.wait_ge(whi, N_UP + 2 * ND * j + s + 1)
                dve.tensor_tensor(w["lo"][:, s % 4, 0:n], raw[:, s % 4, 0:n], w["hi"][:, s % 4, 0:n].bitcast(F32), ALU.subtract).then_inc(wlo, 1)

            def finish_down(j, r):
                dve.wait_ge(ysq, 2 * j + r + 1)
                if isinstance(j, int) and 2 * j + r == 0:
                    dve.tensor_copy(ssum, sq[:, 0]).then_inc(yadd, 1)
                else:
                    dve.wait_ge(yadd, 2 * j + r)
                    dve.tensor_tensor(ssum, ssum, sq[:, r], ALU.add).then_inc(yadd, 1)

            split(0, 0)
            split(0, 1)
            finish(0, 0)
            with dve.Fori(1, FT // 2) as j:
                split(j, 0)
                finish(j - 1, 1)
                split(j, 1)
                finish(j, 0)
            for s in range(4):
                split_down(0, s, DOWN[s][1])
            finish(FT // 2 - 1, 1)
            for s in range(4, 2 * ND):
                split_down(0, s, DOWN[s % ND][1])
            finish_down(0, 0)
            with dve.Fori(1, DT // 2) as j:
                for s in range(4):
                    split_down(j, s, DOWN[s % ND][1])
                finish_down(j - 1, 1)
                for s in range(4, 2 * ND):
                    split_down(j, s, DOWN[s % ND][1])
                finish_down(j, 0)
            finish_down(DT // 2 - 1, 1)
            dve.wait_ge(rooted, 2)
            own.do(dve.reciprocal(rstd, rstd))
            dve.wait_ge(y_done, DT)
            for k in range(DT):
                own.do(dve.scalar_tensor_tensor(work[:, k], work[:, k], vec(post, k), rstd, ALU.mult, ALU.mult))
                dve.wait_ge(back_in[k % 2], 16 * (k // 2 + 1))
                dve.tensor_tensor(work[:, k], work[:, k], tmp[:, k % 2], ALU.add).then_inc(yadd, 1)

        @block.tensor
        def _(pe):
            def sum_features(n):
                for b in range(2):
                    ins = pe.matmul(ps[:, b, 0:NN], S["ones"][:, :], ssum[:, b * NN:(b + 1) * NN], start=True, stop=True)
                ins.then_inc(sum_mm, 1)

            def slab(slot, n, act_hi, act_lo, bank0, first, last):
                for k in range(n):
                    for wt, xt, f, l in (("hi", act_hi, first and k == 0, False), ("hi", act_lo, False, False),
                                         ("lo", act_hi, False, last and k == n - 1)):
                        for b in range(2):
                            ins = pe.matmul(ps[:, bank0 + b, 0:NN], w[wt][:, slot, k], xt[k][:, b * NN:(b + 1) * NN], start=f, stop=l)
                return ins

            pe.wait_ge(summed, DT)
            sum_features(1)
            pe.wait_ge(xlo, DT)
            pe.wait_ge(rooted, 1)

            def up(j, first=False):
                for r in range(2):
                    if not first:
                        pe.wait_ge(prod_done, 2 * j + r - 1)
                    for q in range(UP):
                        pe.wait_ge(wlo, (2 * j + r) * UP + q + 1)
                        ks = [(q % 2) * KS + k for k in range(KS)]
                        slab(q, KS, [xn["hi"][:, k] for k in ks], [xn["lo"][:, k] for k in ks],
                             4 * r + 2 * (q // 2), q % 2 == 0, q % 2 == 1).then_inc(used, 1)

            def down(j, first=False):
                for r in range(2):
                    if first:
                        pe.wait_ge(prod_done, FT - 1 + r)
                    else:
                        pe.wait_ge(ysq, 2 * j + r - 1)
                    for i, (k, n) in enumerate(DOWN):
                        s = r * ND + i
                        if first:
                            pe.wait_ge(hlo, k + n)
                        pe.wait_ge(wlo, N_UP + 2 * ND * j + s + 1)
                        slab(s % 4, n, [hid["hi"][:, k + x] for x in range(n)], [hid["lo"][:, k + x] for x in range(n)],
                             4 * r, i == 0, i == ND - 1).then_inc(used, 1)

            up(0, True)
            with pe.Fori(1, FT // 2) as j:
                up(j)
            down(0, True)
            with pe.Fori(1, DT // 2) as j:
                down(j)
            pe.wait_ge(yadd, DT)
            pe.wait_ge(ysq, DT)
            sum_features(2)


def in_projection(nc, t, S):
    with stage(nc, "ip_") as (ctx, sb, sem):
        ps = S["ps"]
        xn = {h: sb("xn" + h, [P, DT, TOK], F32R) for h in ("hi", "lo")}
        work = sb("work", [P, DT, TOK])
        sq, ssum, rstd = sb("sq", [P, 2, TOK]), sb("ssum", [P, TOK]), sb("rstd", [P, TOK])
        out = sq
        raw = sb("raw", [P, 4, KS, P])
        w = {h: sb("w" + h, [P, 4, KS, P], F32R) for h in ("hi", "lo")}
        x_in, squared, summed, sum_mm, rooted, scaled, xhi, xlo, inv = (sem(n) for n in
            ("x_in", "squared", "summed", "sum_mm", "rooted", "scaled", "xhi", "xlo", "inv"))
        raw_in = [sem(f"raw_in{q}") for q in range(4)]
        z_out = [sem(f"z_out{q}") for q in range(2)]
        whi, wlo, used, out_a, out_v = (sem(n) for n in ("whi", "wlo", "used", "out_a", "out_v"))
        block = ctx.enter_context(nc.Block())
        w_in_v = t["w_in"].rearrange("(k p) n -> p k n", p=P)
        z_v = t["zT"].rearrange("(m p) t -> p m t", p=P)
        UP = 2
        NJ, NG = Z_TILES // 2, Z_GATES // 2
        vec = lambda k: S["vec"][:, VEC_AT["mix_pre_g"] + k:VEC_AT["mix_pre_g"] + k + 1]
        rows = lambda a, n0, n1: a.rearrange("p (n t) -> p n t", t=NN)[:, n0:n1]
        zero = lambda j: isinstance(j, int) and j == 0

        @block.sync
        def _(sp):
            for k in range(DT):
                sp.dma_start(work[:, k], feature_tiles(t["res1"], 0, TOK)[:, k]).then_inc(x_in, 16)

            def load(j, r):
                for q in range(UP):
                    slot = UP * r + q
                    if not zero(j):
                        sp.wait_ge(wlo, 4 * (j - 1) + slot + 1)
                    sp.dma_start(raw[:, slot], w_in_v[:, q * KS:(q + 1) * KS, bass.ds((2 * j + r) * P, P)]).then_inc(raw_in[slot], 16)

            load(0, 0)
            load(0, 1)
            with sp.Fori(1, NJ) as j:
                load(j, 0)
                load(j, 1)

        @block.gpsimd
        def _(pool):
            def store(j, r, by_both):
                pool.wait_ge(out_a, 2 * j + r + 1)
                if by_both:
                    pool.wait_ge(out_v, 2 * j + r + 1)
                pool.dma_start(z_v[:, bass.ds(2 * j + r, 1)], out[:, r:r + 1]).then_inc(z_out[r], 16)

            with pool.Fori(0, NJ - NG) as j:
                store(j, 0, True)
                store(j, 1, True)
            with pool.Fori(NJ - NG, NJ) as j:
                store(j, 0, False)
                store(j, 1, False)
            for r in range(2):
                pool.wait_ge(z_out[r], 16 * NJ)

        @block.scalar
        def _(act):
            act.wait_ge(x_in, 16 * DT)
            for k in range(DT):
                if k >= 2:
                    act.wait_ge(summed, k - 1)
                act.activation(sq[:, k % 2], work[:, k], ACT.Square).then_inc(squared, 1)
            act.wait_ge(sum_mm, 1)
            act.activation(rows(rstd, 0, 4), ps[:, 0:4, 0:NN], ACT.Sqrt, bias=S["eps"][:, 0:1], scale=1.0 / D).then_inc(rooted, 1)

            def split(j, r):
                for q in range(UP):
                    slot = UP * r + q
                    act.wait_ge(raw_in[slot], 16 * (j + 1))
                    if not zero(j):
                        act.wait_ge(used, 4 * (j - 1) + slot + 1)
                    act.activation(w["hi"][:, slot], raw[:, slot], ACT.Copy).then_inc(whi, 1)

            def finish(j, r, func):
                act.wait_ge(used, (2 * j + r + 1) * UP)
                if not zero(j):
                    act.wait_ge(z_out[r], 16 * j)
                n = 2 if func == ACT.Copy else 4
                act.activation(rows(out[:, r], 0, n), ps[:, 4 * r:4 * r + n, 0:NN], func).then_inc(out_a, 1)

            split(0, 0)
            split(0, 1)
            for k in range(DT):
                act.wait_ge(scaled, k + 1)
                act.activation(xn["hi"][:, k], work[:, k], ACT.Copy).then_inc(xhi, 1)
            finish(0, 0, ACT.Copy)
            with act.Fori(1, NJ - NG) as j:
                split(j, 0)
                finish(j - 1, 1, ACT.Copy)
                split(j, 1)
                finish(j, 0, ACT.Copy)
            split(NJ - NG, 0)
            finish(NJ - NG - 1, 1, ACT.Copy)
            split(NJ - NG, 1)
            finish(NJ - NG, 0, ACT.Sigmoid)
            with act.Fori(NJ - NG + 1, NJ) as j:
                split(j, 0)
                finish(j - 1, 1, ACT.Sigmoid)
                split(j, 1)
                finish(j, 0, ACT.Sigmoid)
            finish(NJ - 1, 1, ACT.Sigmoid)

        @block.vector
        def _(dve):
            dve.wait_ge(squared, 2)
            dve.tensor_tensor(ssum[:, :], sq[:, 0], sq[:, 1], ALU.add).then_inc(summed, 2)
            dve.wait_ge(summed, 2)
            for k in range(2, DT):
                dve.wait_ge(squared, k + 1)
                dve.tensor_tensor(ssum[:, :], ssum[:, :], sq[:, k % 2], ALU.add).then_inc(summed, 1)
                dve.wait_ge(summed, k + 1)
            dve.wait_ge(rooted, 1)
            dve.reciprocal(rstd[:, :], rstd[:, :]).then_inc(inv, 1)
            dve.wait_ge(inv, 1)

            def split(j, r):
                for q in range(UP):
                    slot = UP * r + q
                    dve.wait_ge(whi, 4 * j + slot + 1)
                    dve.tensor_tensor(w["lo"][:, slot], raw[:, slot], w["hi"][:, slot].bitcast(F32), ALU.subtract).then_inc(wlo, 1)

            def finish(j, r):
                dve.wait_ge(used, (2 * j + r + 1) * UP)
                if not zero(j):
                    dve.wait_ge(z_out[r], 16 * j)
                dve.tensor_copy(rows(out[:, r], 2, 4), ps[:, 4 * r + 2:4 * r + 4, 0:NN]).then_inc(out_v, 1)

            split(0, 0)
            split(0, 1)
            for k in range(DT):
                dve.scalar_tensor_tensor(work[:, k], work[:, k], vec(k), rstd[:, :], ALU.mult, ALU.mult).then_inc(scaled, 1)
                if k >= 1:
                    dve.wait_ge(xhi, k)
                    dve.tensor_tensor(xn["lo"][:, k - 1], work[:, k - 1], xn["hi"][:, k - 1].bitcast(F32), ALU.subtract).then_inc(xlo, 1)
            dve.wait_ge(xhi, DT)
            dve.tensor_tensor(xn["lo"][:, DT - 1], work[:, DT - 1], xn["hi"][:, DT - 1].bitcast(F32), ALU.subtract).then_inc(xlo, 1)
            finish(0, 0)
            with dve.Fori(1, NJ - NG) as j:
                split(j, 0)
                finish(j - 1, 1)
                split(j, 1)
                finish(j, 0)
            split(NJ - NG, 0)
            finish(NJ - NG - 1, 1)
            split(NJ - NG, 1)
            with dve.Fori(NJ - NG + 1, NJ) as j:
                split(j, 0)
                split(j, 1)

        @block.tensor
        def _(pe):
            pe.wait_ge(summed, DT)
            for b in range(4):
                ins = pe.matmul(ps[:, b, 0:NN], S["ones"][:, :], ssum[:, b * NN:(b + 1) * NN], start=True, stop=True)
            ins.then_inc(sum_mm, 1)
            pe.wait_ge(rooted, 1)

            def tile(j, first=False, by_both=True):
                for r in range(2):
                    if not first:
                        pe.wait_ge(out_a, 2 * j + r - 1)
                        if by_both:
                            pe.wait_ge(out_v, 2 * j + r - 1)
                    for q in range(UP):
                        slot = UP * r + q
                        pe.wait_ge(wlo, 4 * j + slot + 1)
                        for k in range(KS):
                            x = q * KS + k
                            if first and r == 0:
                                pe.wait_ge(xlo, x + 1)
                            for wt, xt, f, l in (("hi", "hi", x == 0, False), ("hi", "lo", False, False), ("lo", "hi", False, x == DT - 1)):
                                for b in range(4):
                                    ins = pe.matmul(ps[:, 4 * r + b, 0:NN], w[wt][:, slot, k], xn[xt][:, x, b * NN:(b + 1) * NN], start=f, stop=l)
                        ins.then_inc(used, 1)

            tile(0, True)
            with pe.Fori(1, NJ - NG + 1) as j:
                tile(j)
            with pe.Fori(NJ - NG + 1, NJ) as j:
                tile(j, by_both=False)


def out_projection_half(nc, t, S, tag, half):
    t0, t1 = half * HALF, (half + 1) * HALF
    with stage(nc, tag) as (ctx, sb, sem):
        ps = S["ps"]
        o_raw = sb("o_raw", [P, 2, KS, HALF])
        o = {h: sb("o" + h, [P, 2, KS, HALF], F32R) for h in ("hi", "lo")}
        m = {h: sb("m" + h, [P, DT, HALF], F32R) for h in ("hi", "lo")}
        y = sb("y", [P, DT, HALF])
        gate = sb("gate", [P, 2, 2, HALF])
        prod = sb("prod", [P, 2, 2, HALF])
        tmp = sb("tmp", [P, 4, HALF])
        sq, ssum, rstd = tmp[:, 0:2], tmp[:, 2], tmp[:, 3]
        raw = sb("raw", [P, 4, KS, P])
        w = {h: sb("w" + h, [P, 4, KS, P], F32R) for h in ("hi", "lo")}
        raw_in = [sem(f"raw_in{q}") for q in range(4)]
        gate_in = [sem(f"gate_in{q}") for q in range(2)]
        back_in = [sem(f"back_in{q}") for q in range(2)]
        o_in, ohi, olo, whi, wlo, used, gated, merged, mhi, mlo, y_done, ysq, yadd, sum_mm, rooted, inv, normed, stored = (sem(n) for n in
            ("o_in", "ohi", "olo", "whi", "wlo", "used", "gated", "merged", "mhi", "mlo", "y_done", "ysq", "yadd", "sum_mm", "rooted", "inv", "normed", "stored"))
        block = ctx.enter_context(nc.Block())
        w_att = t["w_o_att"].rearrange("(k p) n -> p k n", p=P)
        w_rw = t["w_o_rwkv"].rearrange("(k p) n -> p k n", p=P)
        w_out = t["w_out"].rearrange("(k p) n -> p k n", p=P)
        z_v = t["zT"].rearrange("(m p) t -> p m t", p=P)
        vec = lambda k: S["vec"][:, VEC_AT["mix_post_g"] + k:VEC_AT["mix_post_g"] + k + 1]
        flat = lambda a: a.rearrange("p (n t) -> p n t", n=2)
        bank = lambda b: ps[:, b:b + 2, 0:NN]
        G0 = Z_TILES - Z_GATES

        @block.sync
        def _(sp):
            for i, src in enumerate(("attT", "rwT")):
                sp.dma_start(o_raw[:, i], feature_tiles(t[src], t0, t1)).then_inc(o_in, 16)
            for s in range(4 * DT):
                u, q = s % (2 * DT) // 2, s % 2
                if s >= 4:
                    sp.wait_ge(wlo, s - 3)
                cols = slice(u * P, (u + 1) * P)
                src = (w_att[:, :, cols], w_rw[:, :, cols])[q] if s < 2 * DT else w_out[:, q * KS:(q + 1) * KS, cols]
                sp.dma_start(raw[:, s % 4], src).then_inc(raw_in[s % 4], 16)
            for k in range(DT):
                sp.wait_ge(yadd, DT)
                if k >= 2:
                    sp.wait_ge(normed, k - 1)
                sp.dma_start(tmp[:, k % 2], feature_tiles(t["res1"], t0, t1)[:, k]).then_inc(back_in[k % 2], 16)
                if k >= 1:
                    sp.wait_ge(normed, k)
                    sp.dma_start(feature_tiles(t["res2"], t0, t1)[:, k - 1], y[:, k - 1]).then_inc(stored, 16)
            sp.wait_ge(normed, DT)
            sp.dma_start(feature_tiles(t["res2"], t0, t1)[:, DT - 1], y[:, DT - 1]).then_inc(stored, 16)
            sp.wait_ge(stored, 16 * DT)

        @block.gpsimd
        def _(pool):
            for u in range(DT):
                if u >= 2:
                    pool.wait_ge(merged, u - 1)
                pool.dma_start(gate[:, u % 2], z_v[:, G0 + u:Z_TILES:DT, t0:t1]).then_inc(gate_in[u % 2], 16)

        @block.scalar
        def _(act):
            act.wait_ge(o_in, 32)
            for i in range(2):
                act.activation(o["hi"][:, i], o_raw[:, i], ACT.Copy).then_inc(ohi, 1)

            def split(s):
                act.wait_ge(raw_in[s % 4], 16 * (s // 4 + 1))
                if s >= 4:
                    act.wait_ge(used, s - 3)
                act.activation(w["hi"][:, s % 4], raw[:, s % 4], ACT.Copy).then_inc(whi, 1)

            for s in range(2):
                split(s)
            for u in range(DT):
                for s in (2 * u + 2, 2 * u + 3):
                    split(s)
                act.wait_ge(merged, u + 1)
                act.activation(m["hi"][:, u], prod[:, u % 2, 0], ACT.Copy).then_inc(mhi, 1)
            for u in range(DT):
                if u < DT - 1:
                    for s in (2 * (DT + u) + 2, 2 * (DT + u) + 3):
                        split(s)
                act.wait_ge(used, 2 * (DT + u + 1))
                act.activation(flat(y[:, u]), bank(4 * (u % 2)), ACT.Copy).then_inc(y_done, 1)
                if u >= 2:
                    act.wait_ge(yadd, u - 1)
                act.activation(flat(sq[:, u % 2]), bank(4 * (u % 2)), ACT.Square).then_inc(ysq, 1)
            act.wait_ge(sum_mm, 1)
            act.activation(flat(rstd), bank(0), ACT.Sqrt, bias=S["eps"][:, 0:1], scale=1.0 / D).then_inc(rooted, 1)

        @block.vector
        def _(dve):
            for i in range(2):
                dve.wait_ge(ohi, i + 1)
                dve.tensor_tensor(o["lo"][:, i], o_raw[:, i], o["hi"][:, i].bitcast(F32), ALU.subtract).then_inc(olo, 1)

            def split(s):
                dve.wait_ge(whi, s + 1)
                dve.tensor_tensor(w["lo"][:, s % 4], raw[:, s % 4], w["hi"][:, s % 4].bitcast(F32), ALU.subtract).then_inc(wlo, 1)

            for s in range(2):
                split(s)
            for u in range(DT):
                for s in (2 * u + 2, 2 * u + 3):
                    split(s)
                dve.wait_ge(used, 2 * u + 2)
                dve.wait_ge(gate_in[u % 2], 16 * (u // 2 + 1))
                if u >= 2:
                    dve.wait_ge(mlo, u - 1)
                for i in range(2):
                    dve.tensor_tensor(flat(prod[:, u % 2, i]), flat(gate[:, u % 2, i]), bank(4 * (u % 2) + 2 * i), ALU.mult).then_inc(gated, 1)
                dve.wait_ge(gated, 2 * u + 2)
                dve.tensor_tensor(prod[:, u % 2, 0], prod[:, u % 2, 0], prod[:, u % 2, 1], ALU.add).then_inc(merged, 1)
                dve.wait_ge(mhi, u + 1)
                dve.tensor_tensor(m["lo"][:, u], prod[:, u % 2, 0], m["hi"][:, u].bitcast(F32), ALU.subtract).then_inc(mlo, 1)
            for u in range(DT):
                if u < DT - 1:
                    for s in (2 * (DT + u) + 2, 2 * (DT + u) + 3):
                        split(s)
                dve.wait_ge(ysq, u + 1)
                if u == 0:
                    dve.tensor_copy(ssum, sq[:, 0]).then_inc(yadd, 1)
                else:
                    dve.wait_ge(yadd, u)
                    dve.tensor_tensor(ssum, ssum, sq[:, u % 2], ALU.add).then_inc(yadd, 1)
            dve.wait_ge(rooted, 1)
            dve.reciprocal(rstd, rstd).then_inc(inv, 1)
            dve.wait_ge(inv, 1)
            for k in range(DT):
                dve.scalar_tensor_tensor(y[:, k], y[:, k], vec(k), rstd, ALU.mult, ALU.mult).then_inc(inv, 1)
                dve.wait_ge(inv, k + 2)
                dve.wait_ge(back_in[k % 2], 16 * (k // 2 + 1))
                dve.tensor_tensor(y[:, k], y[:, k], tmp[:, k % 2], ALU.add).then_inc(normed, 1)

        @block.tensor
        def _(pe):
            def slab(slot, xt, bank0, first, last):
                for k in range(KS):
                    for wt, h, f, l in (("hi", "hi", first and k == 0, False), ("hi", "lo", False, False), ("lo", "hi", False, last and k == KS - 1)):
                        for b in range(2):
                            ins = pe.matmul(ps[:, bank0 + b, 0:NN], w[wt][:, slot, k], xt(h, k)[:, b * NN:(b + 1) * NN], start=f, stop=l)
                ins.then_inc(used, 1)

            for u in range(DT):
                if u >= 2:
                    pe.wait_ge(gated, 2 * (u - 1))
                for i in range(2):
                    if u == 0:
                        pe.wait_ge(olo, i + 1)
                    pe.wait_ge(wlo, 2 * u + i + 1)
                    slab((2 * u + i) % 4, lambda h, k: o[h][:, i, k], 4 * (u % 2) + 2 * i, True, True)
            for u in range(DT):
                if u < 2:
                    pe.wait_ge(gated, 2 * (DT - 1 + u))
                else:
                    pe.wait_ge(ysq, u - 1)
                for i in range(2):
                    s = 2 * (DT + u) + i
                    if u == 0:
                        pe.wait_ge(mlo, 4 * i + 4)
                    pe.wait_ge(wlo, s + 1)
                    slab(s % 4, lambda h, k: m[h][:, 4 * i + k], 4 * (u % 2), i == 0, i == 1)
            pe.wait_ge(yadd, DT)
            for b in range(2):
                ins = pe.matmul(ps[:, b, 0:NN], S["ones"][:, :], ssum[:, b * NN:(b + 1) * NN], start=True, stop=True)
            ins.then_inc(sum_mm, 1)


def prompt_attention(nc, t, S):
    with stage(nc, "pa_") as (ctx, sb, sem):
        ps = S["ps"]
        qk = sb("qk", [P, 8, TOK])
        vf = sb("vf", [P, HEADS, TOK])
        ktok, vtok = sb("ktok", [P, TOK // P, HEADS * P]), sb("vtok", [P, TOK // P, HEADS * P])
        cos, sin, rot = sb("cos", [P, TOK]), sb("sin", [P, TOK]), sb("rot", [P, P])
        turn = sb("turn", [P, TOK])
        mask = sb("mask", [1, P + CHUNK])
        lamr, lamc = sb("lamr", [1, 4, 64]), sb("lamc", [1, 8])
        ex = sb("ex", [P, 2, SEQ])
        aw = sb("aw", [P, SEQ])
        awT = sb("awT", [P, SEQ // P, P])
        stat = sb("stat", [P, 8])
        z_in = [sem(f"z_in{i}") for i in range(4)]
        c_in, turned, cosed, roped, sined = (sem(n) for n in ("c_in", "turned", "cosed", "roped", "sined"))
        moved, moved_a, stored, lam_s, lam_e, lam_mm, chain = (sem(n) for n in ("moved", "moved_a", "stored", "lam_s", "lam_e", "lam_mm", "chain"))
        scored, maxed, exped, mixed, flipped, flipped_out, valued, out_done = (sem(n) for n in
            ("scored", "maxed", "exped", "mixed", "flipped", "flipped_out", "valued", "out_done"))
        osq, osum, oroot, onorm = (sem(n) for n in ("osq", "osum", "oroot", "onorm"))
        block = ctx.enter_context(nc.Block())
        NK = SEQ // P
        units = [(h, b) for h in range(HEADS) for b in range(NK)]
        z_v = t["zT"].rearrange("(m p) t -> p m t", p=P)
        NT = TOK // P
        flips = [("v", m) for m in range(NT)] + [("k", m) for m in range(NT)]
        third = lambda a: a.rearrange("p (n t) -> p n t", n=3)
        three = lambda b: ps[:, b:b + 3, 0:TOK // 3]
        halves = [(0, 512), (512, 1024)]
        cols = lambda b: [(a, min(e, (b + 1) * P)) for a, e in halves if a < (b + 1) * P]

        @block.sync
        def _(sp):
            for k, n in (("q1", 0), ("k1", 1), ("q2", 2), ("k2", 3)):
                sp.dma_start(lamr[:, n], t["att_lambda_" + k]).then_inc(c_in, 16)
            for dst, n in ((rot, "c_rot"), (cos, "c_cos"), (sin, "c_sin"), (mask, "c_mask")):
                sp.dma_start(dst[:, :], t[n]).then_inc(c_in, 16)
            for i in range(4):
                dst = vf[:, :, :] if i == 1 else qk[:, 4 * (i // 2):4 * (i // 2) + 4]
                if i < 3:
                    sp.dma_start(dst, z_v[:, {0: ZQ, 1: ZV, 2: ZK}[i]:{0: ZQ, 1: ZV, 2: ZK}[i] + 4]).then_inc(z_in[i], 16)
            sp.wait_ge(moved, NT)
            sp.dma_start(t["new_v_prompt"].rearrange("(m p) c -> p m c", p=P), vtok[:, 0:NK]).then_inc(stored, 16)
            sp.dma_start(t["new_v_sample"], vtok[:, NK]).then_inc(stored, 16)
            sp.wait_ge(moved, 2 * NT)
            sp.dma_start(t["new_k_prompt"].rearrange("(m p) c -> p m c", p=P), ktok[:, 0:NK]).then_inc(stored, 16)
            sp.dma_start(t["new_k_sample"], ktok[:, NK]).then_inc(stored, 16)
            sp.wait_ge(onorm, 2 * HEADS)
            sp.dma_start(feature_tiles(t["attT"], 0, SEQ), vf[:, :, 0:SEQ]).then_inc(stored, 16)
            sp.wait_ge(stored, 16 * 5)

        @block.gpsimd
        def _(pool):
            pool.wait_ge(c_in, 16 * 8)
            for i in range(8):
                pool.wait_ge(turned, i + 1)
                pool.tensor_tensor(qk[:, i], qk[:, i], cos[:, :], ALU.mult).then_inc(cosed, 1)

        @block.scalar
        def _(act):
            act.wait_ge(lam_s, 2)
            act.activation(lamc[:, 2:4], lamc[:, 0:2], ACT.Exp).then_inc(lam_e, 1)
            for n, (h, b) in enumerate(units):
                N = (b + 1) * P
                for m in range(2):
                    act.wait_ge(maxed, 2 * n + m + 1)
                    if n >= 1:
                        act.wait_ge(mixed, 2 * n)
                    act.activation(ex[:, m, 0:N], ps[:, 2 * m:2 * m + 2, :].rearrange("p b c -> p (b c)")[:, 0:N], ACT.Exp,
                                   bias=stat[:, 4 * m + 1:4 * m + 2], scale=SCALE, accum_out=stat[:, 4 * m + 2:4 * m + 3]).then_inc(exped, 1)
                for g in range(len(cols(b))):
                    act.wait_ge(flipped, sum(len(cols(bb)) for _, bb in units[:n]) + g + 1)
                    if n >= 1:
                        act.wait_ge(valued, n)
                    k = min(4, b + 1 - 4 * g)
                    act.activation(awT[:, 4 * g:4 * g + k], ps[:, 4 + g, 0:k * P].rearrange("p (k q) -> p k q", k=k), ACT.Copy).then_inc(flipped_out, 1)
            for h in range(HEADS):
                if h == 0:
                    act.wait_ge(out_done, len(units))
                else:
                    act.wait_ge(oroot, h)
                    act.wait_ge(osum, h)
                act.activation(turn[:, 0:SEQ], vf[:, h, 0:SEQ], ACT.Square).then_inc(osq, 1)
                act.wait_ge(osum, h + 1)
                if h >= 1:
                    act.wait_ge(onorm, 2 * h)
                act.activation(sin[:, 0:SEQ], ps[:, 0:2, :].rearrange("p b c -> p (b c)"), ACT.Sqrt, bias=S["eps"][:, 0:1], scale=1.0 / P).then_inc(oroot, 1)

        def take_out(dve, n):
            h, b = units[n]
            dve.wait_ge(valued, n + 1)
            dve.tensor_copy(vf[:, h, b * P:(b + 1) * P], ps[:, 6 + n % 2, 0:P]).then_inc(out_done, 1)

        @block.vector
        def _(dve):
            own = Chain(dve, chain)
            dve.wait_ge(c_in, 16 * 8)
            for i in range(2):
                dve.tensor_tensor_reduce(out=lamr[:, 2 * i], in0=lamr[:, 2 * i], in1=lamr[:, 2 * i + 1], scale=1.0, scalar=0.0,
                                         op0=ALU.mult, op1=ALU.add, accum_out=lamc[:, i:i + 1]).then_inc(lam_s, 1)
            dve.wait_ge(lam_e, 1)
            own.do(dve.tensor_tensor(lamc[:, 4:5], lamc[:, 3:4], lamc[:, 2:3], ALU.subtract))
            own.do(dve.tensor_scalar(lamc[:, 5:6], lamc[:, 4:5], -LAM_INIT, None, ALU.add))
            dve.tensor_copy(lamc[:, 6:7], lamc[:, 5:6]).then_inc(lam_s, 1)
            dve.wait_ge(lam_mm, 1)
            own.do(dve.tensor_copy(S["neg_lam"][:, :], ps[:, 7, 0:1]))

            def rope(i):
                dve.wait_ge(turned, i + 1)
                if i >= 1:
                    dve.wait_ge(roped, i)
                dve.tensor_tensor(third(turn[:, :]), three(3 * (i % 2)), third(sin[:, :]), ALU.mult).then_inc(sined, 1)
                dve.wait_ge(sined, i + 1)
                dve.wait_ge(cosed, i + 1)
                dve.tensor_tensor(qk[:, i], qk[:, i], turn[:, :], ALU.add).then_inc(roped, 1)

            for i in range(8):
                rope(i)
            dve.wait_ge(roped, 8)
            dve.tensor_copy(S["qk_sample"][:, :, :], qk[:, :, SEQ:TOK]).then_inc(chain, 1)
            own.n += 1
            for n, (what, m) in enumerate(flips):
                dve.wait_ge(moved_a, n + 1)
                dve.tensor_copy((vtok if what == "v" else ktok)[:, m], ps[:, 6 + n % 2, :]).then_inc(moved, 1)
            for n, (h, b) in enumerate(units):
                N = (b + 1) * P
                for m in range(2):
                    dve.wait_ge(scored, n + 1)
                    own.do(dve.tensor_reduce(stat[:, 4 * m:4 * m + 1], ps[:, 2 * m:2 * m + 2, :].rearrange("p b c -> p (b c)")[:, 0:N], AX, ALU.max, negate=True))
                    dve.tensor_scalar(stat[:, 4 * m + 1:4 * m + 2], stat[:, 4 * m:4 * m + 1], SCALE, None, ALU.mult).then_inc(maxed, 1)
                for m in range(2):
                    dve.wait_ge(exped, 2 * n + m + 1)
                    own.do(dve.reciprocal(stat[:, 4 * m + 3:4 * m + 4], stat[:, 4 * m + 2:4 * m + 3]))
                    if m == 0:
                        if n >= 1:
                            dve.wait_ge(flipped, sum(len(cols(bb)) for _, bb in units[:n]))
                        dve.tensor_scalar(aw[:, 0:N], ex[:, 0, 0:N], stat[:, 3:4], None, ALU.mult).then_inc(mixed, 1)
                    else:
                        own.do(dve.tensor_tensor(stat[:, 7:8], stat[:, 7:8], S["neg_lam"][:, :], ALU.mult))
                        dve.wait_ge(mixed, 2 * n + 1)
                        dve.scalar_tensor_tensor(aw[:, 0:N], ex[:, 1, 0:N], stat[:, 7:8], aw[:, 0:N], ALU.mult, ALU.add).then_inc(mixed, 1)
                if n >= 1:
                    take_out(dve, n - 1)
            take_out(dve, len(units) - 1)
            for h in range(HEADS):
                dve.wait_ge(oroot, h + 1)
                own.do(dve.reciprocal(sin[:, 0:SEQ], sin[:, 0:SEQ]))
                dve.scalar_tensor_tensor(vf[:, h, 0:SEQ], vf[:, h, 0:SEQ], S["vec"][:, NVEC - 1:NVEC], sin[:, 0:SEQ], ALU.mult, ALU.mult).then_inc(onorm, 1)
                dve.wait_ge(onorm, 2 * h + 1)
                dve.tensor_scalar(vf[:, h, 0:SEQ], vf[:, h, 0:SEQ], 1.0 - LAM_INIT, None, ALU.mult).then_inc(onorm, 1)

        @block.tensor
        def _(pe):
            pe.wait_ge(c_in, 16 * 8)
            pe.wait_ge(lam_s, 3)
            pe.matmul(ps[:, 7, 0:1], S["ones"][0:1, :], lamc[:, 6:7], start=True, stop=True).then_inc(lam_mm, 1)
            for i in range(8):
                pe.wait_ge(z_in[0 if i < 4 else 2], 16)
                if i >= 2:
                    pe.wait_ge(sined, i - 1)
                for b in range(3):
                    ins = pe.matmul(ps[:, 3 * (i % 2) + b, 0:TOK // 3], rot[:, :], qk[:, i, b * (TOK // 3):(b + 1) * (TOK // 3)], start=True, stop=True)
                ins.then_inc(turned, 1)
            pe.wait_ge(z_in[1], 16)
            pe.wait_ge(roped, 8)
            pe.wait_ge(chain, 3)
            for n, (what, m) in enumerate(flips):
                if n >= 2:
                    pe.wait_ge(moved, n - 1)
                for h in range(HEADS):
                    src = vf[:, h, m * P:(m + 1) * P] if what == "v" else qk[:, 4 + h, m * P:(m + 1) * P]
                    ins = pe.transpose(ps[:, 6 + n % 2, h * P:(h + 1) * P], src, S["ident"][:, :])
                ins.then_inc(moved_a, 1)

            def scores(n):
                h, b = units[n]
                N = (b + 1) * P
                if n >= 1:
                    pe.wait_ge(exped, 2 * n)
                for i, (a, e) in enumerate(cols(b)):
                    last = e == N
                    for m in range(2):
                        rows = slice(64 * m, 64 * m + 64)
                        pe.matmul(ps[:, 2 * m + i, 0:e - a], qk[rows, h, b * P:(b + 1) * P], qk[rows, 4 + h, a:e], start=True, stop=not last)
                    if last:
                        for m in range(2):
                            ins = pe.matmul(ps[:, 2 * m + i, e - a - CHUNK:e - a], mask[:, 0:P], mask[:, P:P + CHUNK], start=False, stop=True)
                ins.then_inc(scored, 1)

            def flip(n):
                h, b = units[n]
                pe.wait_ge(mixed, 2 * n + 2)
                for g in range(len(cols(b))):
                    if n >= 1:
                        pe.wait_ge(flipped_out, sum(len(cols(bb)) for _, bb in units[:n]))
                    for k in range(min(4, b + 1 - 4 * g)):
                        ins = pe.transpose(ps[:, 4 + g, k * P:(k + 1) * P], aw[:, (4 * g + k) * P:(4 * g + k + 1) * P], S["ident"][:, :])
                    ins.then_inc(flipped, 1)

            def values(n):
                h, b = units[n]
                if n >= 2:
                    pe.wait_ge(out_done, n - 1)
                for k in range(b + 1):
                    if k % 4 == 0:
                        pe.wait_ge(flipped_out, sum(len(cols(bb)) for _, bb in units[:n]) + k // 4 + 1)
                    ins = pe.matmul(ps[:, 6 + n % 2, 0:P], vtok[:, k, h * P:(h + 1) * P], awT[:, k], start=k == 0, stop=k == b)
                ins.then_inc(valued, 1)

            pe.wait_ge(moved, 2 * NT)
            scores(0)
            for n in range(len(units)):
                if n + 1 < len(units):
                    scores(n + 1)
                flip(n)
                values(n)
            for h in range(HEADS):
                pe.wait_ge(osq, h + 1)
                if h >= 1:
                    pe.wait_ge(oroot, h)
                for b in range(2):
                    ins = pe.matmul(ps[:, b, :], S["ones"][:, :], turn[:, b * 512:(b + 1) * 512], start=True, stop=True)
                ins.then_inc(osum, 1)


def sample_attention(nc, t, S):
    with stage(nc, "sa_") as (ctx, sb, sem):
        ps = S["ps"]
        CK = 1024 // P
        NS = 1024 + NQ
        kc, vc = sb("kc", [P, 2, CK, HEADS * P]), sb("vc", [P, 2, CK, HEADS * P])
        vnew = sb("vnew", [NQ, 2, HEADS * P])
        kT = sb("kT", [P, HEADS, CK * P])
        qbd = sb("qbd", [P, 2, HEADS, 2 * NQ])
        knew = sb("knew", [P, 2, HEADS, NQ])
        ex = sb("ex", [P, NS])
        pick, coef, sign = sb("pick", [P, 64]), sb("coef", [P, 64]), sb("sign", [P, 2])
        stat = sb("stat", [P, 8])
        awT = sb("awT", [P, CK + 1, 64])
        out, sq, root = sb("out", [P, HEADS, P]), sb("sq", [P, HEADS * P]), sb("root", [P, HEADS * P])
        k_in, v_in = [sem(f"k_in{i}") for i in range(2)], [sem(f"v_in{i}") for i in range(2)]
        c_in, qset, flipped, out_a, out_v, scored, maxed, exped, weighed, mixed, mixed_out, valued, out_done, chain = (sem(n) for n in
            ("c_in", "qset", "flipped", "out_a", "out_v", "scored", "maxed", "exped", "weighed", "mixed", "mixed_out", "valued", "out_done", "chain"))
        osq, osum, oroot, onorm, stored = (sem(n) for n in ("osq", "osum", "oroot", "onorm", "stored"))
        block = ctx.enter_context(nc.Block())
        k_v = t["cache_att_k"].rearrange("b (p k) c -> b p k c", k=CK)
        v_v = t["cache_att_v"].rearrange("b (p k) c -> b p k c", k=CK)
        vn_v = t["new_v_sample"].rearrange("(b q) c -> b q c", b=NB)
        zero = lambda j: isinstance(j, int) and j == 0
        GROUPS = [(h, g) for h in range(HEADS) for g in range(2)]
        flat3 = ps[:, 0:3, :].rearrange("p b c -> p (b c)")
        one = lambda a: a.rearrange("b p k c -> p (b k) c")

        @block.sync
        def _(sp):
            sp.dma_start(pick[:, :], t["c_pick"]).then_inc(c_in, 16)
            sp.dma_start(sign[:, :], t["c_sign"]).then_inc(c_in, 16)

            def load(j, r):
                if not zero(j):
                    sp.wait_ge(flipped, 8 * (2 * j + r - 1))
                sp.dma_start(kc[:, r], one(k_v[bass.ds(2 * j + r, 1)])).then_inc(k_in[r], 16)
                if not zero(j):
                    sp.wait_ge(valued, 2 * j + r - 1)
                sp.dma_start(vc[:, r], one(v_v[bass.ds(2 * j + r, 1)])).then_inc(v_in[r], 16)
                sp.dma_start(vnew[:, r], vn_v[bass.ds(2 * j + r, 1)].rearrange("b q c -> q (b c)")).then_inc(v_in[r], 16)

            load(0, 0)
            load(0, 1)
            with sp.Fori(1, NB // 2) as j:
                load(j, 0)
                load(j, 1)
            sp.wait_ge(onorm, 2)
            sp.dma_start(feature_tiles(t["attT"], SEQ, TOK), out[:, :, :]).then_inc(stored, 16)
            sp.wait_ge(stored, 16)

        def copy_group(r, g):
            h, half = GROUPS[g]
            return kT[:, h, half * 512:half * 512 + 512], ps[:, 3 + g % 2, :]

        @block.scalar
        def _(act):
            def seq(j, r):
                n = 2 * j + r
                for g in range(0, 8, 2):
                    act.wait_ge(flipped, 8 * n + g + 1)
                    if not (zero(j) and r == 0):
                        act.wait_ge(scored, n)
                    act.activation(*copy_group(r, g), ACT.Copy).then_inc(out_a, 1)
                act.wait_ge(maxed, n + 1)
                if not (zero(j) and r == 0):
                    act.wait_ge(mixed, n)
                act.activation(ex[:, :], flat3[:, 0:NS], ACT.Exp, bias=stat[:, 1:2], scale=SCALE, accum_out=stat[:, 2:3]).then_inc(exped, 1)

            seq(0, 0)
            seq(0, 1)
            with act.Fori(1, NB // 2) as j:
                seq(j, 0)
                seq(j, 1)
            act.wait_ge(out_done, NB)
            act.activation(sq[:, :], out[:, :, :].rearrange("p h t -> p (h t)"), ACT.Square).then_inc(osq, 1)
            act.wait_ge(osum, 1)
            act.activation(root[:, :], ps[:, 0, :], ACT.Sqrt, bias=S["eps"][:, 0:1], scale=1.0 / P).then_inc(oroot, 1)

        @block.vector
        def _(dve):
            dve.memset(qbd[:, :, :, :], 0.0).then_inc(chain, 1)
            dve.wait_ge(c_in, 32)
            dve.tensor_tensor(stat[:, 4:5], sign[:, 1:2], S["neg_lam"][:, :], ALU.mult).then_inc(chain, 1)
            dve.wait_ge(chain, 2)
            dve.tensor_tensor(stat[:, 5:6], stat[:, 4:5], sign[:, 0:1], ALU.add).then_inc(chain, 1)
            dve.wait_ge(chain, 3)

            def seq(j, r):
                n = 2 * j + r
                first = zero(j) and r == 0
                if not zero(j):
                    dve.wait_ge(scored, n - 1)
                for m in range(2):
                    rows = slice(64 * m, 64 * m + 64)
                    dve.tensor_copy(qbd[rows, r, :, m * NQ:(m + 1) * NQ], S["qk_sample"][rows, 0:HEADS, bass.ds(n * NQ, NQ)]).then_inc(qset, 1)
                dve.tensor_copy(knew[:, r], S["qk_sample"][:, HEADS:8, bass.ds(n * NQ, NQ)]).then_inc(qset, 1)
                for g in range(1, 8, 2):
                    dve.wait_ge(flipped, 8 * n + g + 1)
                    if not first:
                        dve.wait_ge(scored, n)
                    dve.tensor_copy(*copy_group(r, g)).then_inc(out_v, 1)
                dve.wait_ge(scored, n + 1)
                if not first:
                    dve.wait_ge(exped, n)
                dve.tensor_reduce(stat[:, 0:1], flat3[:, 0:NS], AX, ALU.max, negate=True).then_inc(chain, 1)
                dve.wait_ge(chain, 3 + 3 * n + 1)
                dve.tensor_scalar(stat[:, 1:2], stat[:, 0:1], SCALE, None, ALU.mult).then_inc(maxed, 1)
                dve.wait_ge(exped, n + 1)
                dve.reciprocal(stat[:, 3:4], stat[:, 2:3]).then_inc(chain, 1)
                dve.wait_ge(chain, 3 + 3 * n + 2)
                dve.tensor_tensor(stat[:, 6:7], stat[:, 3:4], stat[:, 5:6], ALU.mult).then_inc(chain, 1)
                dve.wait_ge(chain, 3 + 3 * n + 3)
                dve.tensor_scalar(coef[:, :], pick[:, :], stat[:, 6:7], None, ALU.mult).then_inc(weighed, 1)
                dve.wait_ge(mixed, n + 1)
                dve.tensor_copy(awT[:, 0:CK], ps[:, 5, :].rearrange("p (k c) -> p k c", k=CK)).then_inc(mixed_out, 1)
                dve.tensor_copy(awT[0:NQ, CK], ps[0:NQ, 6, 0:64]).then_inc(mixed_out, 1)
                dve.wait_ge(valued, n + 1)
                dve.tensor_copy(out[:, :, bass.ds(n * NQ, NQ)], ps[:, 7, 0:64].rearrange("p (h q) -> p h q", h=HEADS)).then_inc(out_done, 1)

            seq(0, 0)
            seq(0, 1)
            with dve.Fori(1, NB // 2) as j:
                seq(j, 0)
                seq(j, 1)
            dve.wait_ge(oroot, 1)
            dve.reciprocal(root[:, :], root[:, :]).then_inc(chain, 1)
            dve.wait_ge(chain, 3 + 3 * NB + 1)
            o = out[:, :, :].rearrange("p h t -> p (h t)")
            dve.scalar_tensor_tensor(o, o, S["vec"][:, NVEC - 1:NVEC], root[:, :], ALU.mult, ALU.mult).then_inc(onorm, 1)
            dve.wait_ge(onorm, 1)
            dve.tensor_scalar(o, o, 1.0 - LAM_INIT, None, ALU.mult).then_inc(onorm, 1)

        @block.tensor
        def _(pe):
            def seq(j, r):
                n = 2 * j + r
                first = zero(j) and r == 0
                pe.wait_ge(k_in[r], 16 * (j + 1))
                for g, (h, half) in enumerate(GROUPS):
                    if g >= 2 or not first:
                        pe.wait_ge(out_v if g % 2 else out_a, 4 * n + g // 2)
                    for k in range(4):
                        ins = pe.transpose(ps[:, 3 + g % 2, k * P:(k + 1) * P], kc[:, r, 4 * half + k, h * P:(h + 1) * P], S["ident"][:, :])
                    ins.then_inc(flipped, 1)
                pe.wait_ge(qset, 3 * n + 3)
                pe.wait_ge(out_a, 4 * n + 4)
                pe.wait_ge(out_v, 4 * n + 4)
                if not first:
                    pe.wait_ge(exped, n)
                for c in range(2):
                    for h in range(HEADS):
                        pe.matmul(ps[32 * h:32 * h + 32, c, :], qbd[:, r, h], kT[:, h, c * 512:(c + 1) * 512], start=True, stop=True, tile_position=(0, 32 * h))
                for h in range(HEADS):
                    ins = pe.matmul(ps[32 * h:32 * h + 32, 2, 0:NQ], qbd[:, r, h], knew[:, r, h], start=True, stop=True, tile_position=(0, 32 * h))
                ins.then_inc(scored, 1)
                pe.wait_ge(weighed, n + 1)
                if not first:
                    pe.wait_ge(mixed_out, 2 * n)
                for k in range(CK):
                    pe.matmul(ps[:, 5, k * 64:(k + 1) * 64], ex[:, k * P:(k + 1) * P], coef[:, :], start=True, stop=True)
                pe.matmul(ps[0:NQ, 6, 0:64], ex[:, CK * P:NS], coef[:, :], start=True, stop=True).then_inc(mixed, 1)
                pe.wait_ge(mixed_out, 2 * n + 2)
                pe.wait_ge(v_in[r], 32 * (j + 1))
                if not first:
                    pe.wait_ge(out_done, n)
                for h in range(HEADS):
                    for k in range(CK):
                        pe.matmul(ps[:, 7, h * NQ:(h + 1) * NQ], vc[:, r, k, h * P:(h + 1) * P], awT[:, k, h * NQ:(h + 1) * NQ], start=k == 0, stop=False)
                    ins = pe.matmul(ps[:, 7, h * NQ:(h + 1) * NQ], vnew[:, r, h * P:(h + 1) * P], awT[0:NQ, CK, h * NQ:(h + 1) * NQ], start=False, stop=True)
                ins.then_inc(valued, 1)

            seq(0, 0)
            seq(0, 1)
            with pe.Fori(1, NB // 2) as j:
                seq(j, 0)
                seq(j, 1)
            pe.wait_ge(osq, 1)
            pe.matmul(ps[:, 0, :], S["ones"][:, :], sq[:, :], start=True, stop=True).then_inc(osum, 1)


def rwkv_prepare(nc, t, S, R):
    with stage(nc, "rp_") as (ctx, sb, sem):
        ps = S["ps"]
        lora = sb("lora", [P, 2, TOK])
        diff = sb("diff", [P, 2, TOK])
        sw, aa = sb("sw", [P, RT, TOK]), sb("aa", [P, RT, TOK])
        gg = sb("gg", [P, RT, TOK])
        cum = sb("cum", [P, TOK])
        e = [sb(f"e{i}", [P, TOK]) for i in range(2)]
        starts = sb("starts", [P, TOK])
        wl, g2 = sb("wl", [P, RT * P]), sb("g2", [P, RT * P])
        rows = sb("rows", [NB + 1, ZRT * P])
        shift_cols = sb("shift_cols", [P, ZRT, NB])
        last_cols = sb("last_cols", [P, ZRT, NB + 1])
        tri = [R["r"], R["k"], R["v"]]
        z = lambda i: tri[i // RT][:, i % RT] if i < 3 * RT else lora[:, i - 3 * RT]
        z_in = [sem(f"z_in{i}") for i in range(4)]
        c_in, flip, flipped, diffed, shifted, stored, chain, cols_kept, rows_kept, rows_mm = (sem(n) for n in
            ("c_in", "flip", "flipped", "diffed", "shifted", "stored", "chain", "cols_kept", "rows_kept", "rows_mm"))
        acts, lora_mm, lora_out, sum_mm, sum_out, expd, used, pooled = (sem(n) for n in
            ("acts", "lora_mm", "lora_out", "sum_mm", "sum_out", "expd", "used", "pooled"))
        block = ctx.enter_context(nc.Block())
        z_v = t["zT"].rearrange("(m p) t -> p m t", p=P)
        vec = lambda name, k: S["vec"][:, VEC_AT[name] + k:VEC_AT[name] + k + 1]
        third = lambda a: a.rearrange("p (n t) -> p n t", n=3)
        three = lambda b: ps[:, b:b + 3, 0:TOK // 3]
        C3 = [(b, b * (TOK // 3), (b + 1) * (TOK // 3)) for b in range(3)]
        order = [12, 13] + list(range(12))
        sample = lambda a: a[:, SEQ:TOK].rearrange("p (b q) -> p b q", b=NB)

        @block.sync
        def _(sp):
            sp.dma_start(rows[0:NB, :], t["state_shift"].rearrange("a b c d -> (a b c) d")).then_inc(c_in, 16)
            sp.dma_start(starts[:, :], t["c_starts"]).then_inc(c_in, 16)
            sp.dma_start(R["block"][:, :], t["c_block"]).then_inc(c_in, 16)
            sp.dma_start(wl[0:64, :], t["rwkv_w2"]).then_inc(c_in, 16)
            sp.dma_start(wl[64:P, :], t["rwkv_a2"]).then_inc(c_in, 16)
            sp.dma_start(g2[:, :], t["rwkv_g2"]).then_inc(c_in, 16)
            sp.dma_start(lora[:, :, :], z_v[:, ZR + 12:ZR + 14]).then_inc(z_in[3], 16)
            for i in range(3):
                sp.dma_start(tri[i][:, :, :], z_v[:, ZR + RT * i:ZR + RT * (i + 1)]).then_inc(z_in[i], 16)
            sp.wait_ge(rows_kept, 4)
            sp.dma_start(t["new_shift_prompt"], rows[0:1, :]).then_inc(stored, 16)
            sp.dma_start(t["new_shift_sample"], rows[1:NB + 1, :]).then_inc(stored, 16)
            sp.wait_ge(lora_out, 3 * RT)
            sp.dma_start(feature_tiles(t["gT"], 0, TOK), gg[:, :, :]).then_inc(stored, 16)
            sp.wait_ge(chain, R_DONE[RT - 1])
            sp.dma_start(feature_tiles(t["bonusT"], 0, TOK), sw[:, :, :]).then_inc(stored, 16)
            sp.wait_ge(stored, 16 * 4)

        @block.gpsimd
        def _(pool):
            pool.wait_ge(flipped, 1)
            for n, i in enumerate(order):
                pool.wait_ge(z_in[i // RT if i < 12 else 3], 16)
                if n >= 2:
                    pool.wait_ge(shifted, n - 1)
                d, x = diff[:, n % 2], z(i)
                pool.tensor_tensor(d[:, 1:TOK], x[:, 0:TOK - 1], x[:, 1:TOK], ALU.subtract).then_inc(pooled, 1)
                pool.tensor_copy(last_cols[:, i, 0:1], x[:, SEQ - 1:SEQ]).then_inc(cols_kept, 1)
                pool.tensor_copy(last_cols[:, i, 1:NB + 1], sample(x)[:, :, NQ - 1]).then_inc(cols_kept, 1)
                pool.tensor_scalar(d[:, 0:1], x[:, 0:1], -1.0, None, ALU.mult).then_inc(diffed, 1)
                pool.wait_ge(pooled, n + 1)
                pool.tensor_tensor(sample(d)[:, :, 0], shift_cols[:, i], sample(x)[:, :, 0], ALU.subtract).then_inc(diffed, 1)

        @block.scalar
        def _(act):
            act.wait_ge(shifted, 2)
            act.activation(lora[0:64, 0], lora[0:64, 0], ACT.Tanh).then_inc(acts, 1)
            act.activation(lora[:, 1], lora[:, 1], ACT.Sigmoid).then_inc(acts, 1)
            for c in range(RT):
                for n, (dst, bias) in enumerate(((sw[:, c], "rwkv_w0"), (aa[:, c], "rwkv_a0"), (gg[:, c], None))):
                    act.wait_ge(lora_mm, 3 * c + n + 1)
                    src = three(3 * ((3 * c + n) % 2))
                    if bias:
                        act.activation(third(dst), src, ACT.Sigmoid, bias=vec(bias, c)).then_inc(lora_out, 1)
                    else:
                        act.activation(third(dst), src, ACT.Copy).then_inc(lora_out, 1)
            for c in range(RT):
                act.wait_ge(used, c + 1)
                act.activation(e[1][:, :], R["a"][:, c], ACT.Square).then_inc(acts, 1)
                act.wait_ge(sum_mm, c + 1)
                act.activation(third(R["b"][:, c]), three(3 * (c % 2)), ACT.Sqrt).then_inc(sum_out, 1)
            for c in range(RT):
                act.wait_ge(chain, R_CUM[c])
                act.activation(e[0][:, :], cum[:, :], ACT.Exp, scale=KAPPA).then_inc(expd, 1)
                act.activation(e[1][:, :], cum[:, :], ACT.Exp, scale=-KAPPA).then_inc(expd, 1)
                act.wait_ge(chain, R_PREV[c])
                act.activation(diff[:, 0], diff[:, 0], ACT.Exp, scale=-KAPPA).then_inc(expd, 1)

        @block.vector
        def _(dve):
            own = Chain(dve, chain)
            dve.wait_ge(flip, 1)
            dve.tensor_copy(shift_cols[:, :, :], ps[:, 7, 0:ZRT * NB].rearrange("p (i b) -> p i b", b=NB)).then_inc(flipped, 1)
            for n, i in enumerate(order):
                dve.wait_ge(diffed, 2 * n + 2)
                dve.wait_ge(cols_kept, 2 * n + 2)
                dve.scalar_tensor_tensor(z(i), diff[:, n % 2], vec("rwkv_mu", i), z(i), ALU.mult, ALU.add).then_inc(shifted, 1)
            for b in range(4):
                dve.wait_ge(rows_mm, b + 1)
                n = min(4, ZRT - 4 * b)
                dve.tensor_copy(rows[:, 4 * b * P:(4 * b + n) * P], ps[0:NB + 1, 6 + b % 2, 0:n * P]).then_inc(rows_kept, 1)
            dve.wait_ge(shifted, ZRT)
            for c in range(RT):
                dve.tensor_scalar(R["a"][:, c], R["k"][:, c], vec("rwkv_k_k", c), None, ALU.mult).then_inc(used, 1)
            for c in range(RT):
                dve.wait_ge(lora_out, 3 * c + 2)
                own.do(dve.tensor_scalar(diff[:, 1], aa[:, c], -1.0, vec("rwkv_k_a", c), ALU.add, ALU.mult))
                own.do(dve.scalar_tensor_tensor(R["k"][:, c], diff[:, 1], 1.0, R["k"][:, c], ALU.add, ALU.mult))
            for c in range(RT):
                dve.wait_ge(sum_out, c + 1)
                own.do(dve.tensor_scalar(R["b"][:, c], R["b"][:, c], 1e-12, None, ALU.max))
                own.do(dve.reciprocal(R["b"][:, c], R["b"][:, c]))
                own.do(dve.tensor_tensor(R["a"][:, c], R["a"][:, c], R["b"][:, c], ALU.mult))
                own.do(dve.tensor_tensor(R["b"][:, c], R["a"][:, c], aa[:, c], ALU.mult))
                own.do(dve.scalar_tensor_tensor(aa[:, c], R["r"][:, c], vec("rwkv_r_k", c), R["k"][:, c], ALU.mult, ALU.mult))
            for c in range(RT):
                own.do(dve.tensor_tensor_scan(cum[:, :], starts[:, :], sw[:, c], 0.0, ALU.mult, ALU.add))
                assert own.n == R_CUM[c]
                own.do(dve.tensor_tensor(diff[:, 0], cum[:, :], sw[:, c], ALU.subtract))
                assert own.n == R_PREV[c]
                dve.wait_ge(expd, 3 * c + 1)
                own.do(dve.tensor_tensor(R["b"][:, c], R["b"][:, c], e[0][:, :], ALU.mult))
                own.do(dve.tensor_tensor(R["k"][:, c], R["k"][:, c], e[0][:, :], ALU.mult))
                dve.wait_ge(expd, 3 * c + 2)
                own.do(dve.tensor_tensor(R["r"][:, c], R["r"][:, c], e[1][:, :], ALU.mult))
                own.do(dve.tensor_copy(R["pend"][:, c, 0:SEQ // CHUNK], e[1][:, CHUNK - 1:SEQ:CHUNK]))
                own.do(dve.tensor_copy(R["pend"][:, c, SEQ // CHUNK:], e[1][:, SEQ + NQ - 1:TOK:NQ]))
                dve.wait_ge(expd, 3 * c + 3)
                own.do(dve.scalar_tensor_tensor(R["a"][:, c], R["a"][:, c], -1.0, diff[:, 0], ALU.mult, ALU.mult))
                dve.wait_ge(sum_mm, RT + c + 1)
                own.do(dve.tensor_tensor(third(sw[:, c]), third(R["v"][:, c]), three(3 * (c % 2)), ALU.mult))
                assert own.n == R_DONE[c]

        @block.tensor
        def _(pe):
            pe.wait_ge(c_in, 16 * 6)
            for i in range(ZRT):
                ins = pe.transpose(ps[:, 7, i * NB:(i + 1) * NB], rows[0:NB, i * P:(i + 1) * P], S["ident"][0:NB, 0:NB])
            ins.then_inc(flip, 1)
            pe.wait_ge(acts, 2)
            for c in range(RT):
                for n in range(3):
                    i = 3 * c + n
                    if i >= 2:
                        pe.wait_ge(lora_out, i - 1)
                    for b, c0, c1 in C3:
                        w = (wl[0:64, c * P:(c + 1) * P], wl[64:P, c * P:(c + 1) * P], g2[:, c * P:(c + 1) * P])[n]
                        x = (lora[0:64, 0, c0:c1], lora[64:P, 0, c0:c1], lora[:, 1, c0:c1])[n]
                        ins = pe.matmul(ps[:, 3 * (i % 2) + b, 0:TOK // 3], w, x, start=True, stop=True)
                    ins.then_inc(lora_mm, 1)
            pe.wait_ge(cols_kept, 2 * ZRT)
            pe.wait_ge(flipped, 1)
            for b in range(4):
                if b >= 2:
                    pe.wait_ge(rows_kept, b - 1)
                for n in range(min(4, ZRT - 4 * b)):
                    ins = pe.transpose(ps[0:NB + 1, 6 + b % 2, n * P:(n + 1) * P], last_cols[:, 4 * b + n], S["ident"][:, :])
                ins.then_inc(rows_mm, 1)
            for c in range(RT):
                pe.wait_ge(acts, 2 + c + 1)
                if c < 2:
                    pe.wait_ge(lora_out, 3 * RT)
                else:
                    pe.wait_ge(sum_out, c - 1)
                for b, c0, c1 in C3:
                    ins = pe.matmul(ps[:, 3 * (c % 2) + b, 0:TOK // 3], R["block"][:, :], e[1][:, c0:c1], start=True, stop=True)
                ins.then_inc(sum_mm, 1)
            for c in range(RT):
                if c < 2:
                    pe.wait_ge(sum_out, RT)
                    pe.wait_ge(chain, R_CUM[0] - 1)
                else:
                    pe.wait_ge(chain, R_DONE[c - 2])
                for b, c0, c1 in C3:
                    ins = pe.matmul(ps[:, 3 * (c % 2) + b, 0:TOK // 3], R["block"][:, :], aa[:, c, c0:c1], start=True, stop=True)
                ins.then_inc(sum_mm, 1)


R_CUM = [7 * RT + 9 * c + 1 for c in range(RT)]
R_PREV = [n + 1 for n in R_CUM]
R_DONE = [n + 8 for n in R_CUM]


def rwkv_chunks(nc, t, S, R):
    with stage(nc, "rc_") as (ctx, sb, sem):
        ps = S["ps"]
        two = range(2)
        G = [P, RT, CHUNK]
        xin = [sb(f"xin{s}", [P, 5, RT, CHUNK]) for s in two]
        tok = [sb(f"tok{s}", [P, 4, RT, CHUNK]) for s in two]
        dg = [sb(f"dg{s}", [P, 2, RT, CHUNK]) for s in two]
        od = [sb(f"od{s}", [P, 2, RT, CHUNK]) for s in two]
        qm = [sb(f"qm{s}", [P, 3, RT, CHUNK]) for s in two]
        sq2, sq4 = ([sb(f"{n}{s}", [P, 2, RT, CHUNK]) for s in two] for n in ("sqa", "sqb"))
        m8 = [sb(f"m8{s}", G) for s in two]
        x = [sb(f"x{s}", G) for s in two]
        r = [sb(f"r{s}", G) for s in two]
        hty = [sb(f"hty{s}", [P, 2, RT, CHUNK]) for s in two]
        w = [sb(f"w{s}", G) for s in two]
        mv = [sb(f"mv{s}", G) for s in two]
        va = [sb(f"va{s}", [P, 2, RT, CHUNK]) for s in two]
        u = [sb(f"u{s}", G) for s in two]
        st = [sb(f"st{s}", G) for s in two]
        eye = sb("eye", G)
        masks = sb("masks", [P, 2, 6, RT, CHUNK])
        c_in, zeroed = sem("c_in"), sem("zeroed")
        fed, prod, kept_v, kept_a = ([sem(f"{n}{s}") for s in two] for n in ("fed", "prod", "kept_v", "kept_a"))
        NC = SEQ // CHUNK
        NJ = NC // 2
        src = [R["a"], R["b"], R["k"], R["v"], R["r"]]
        bank = lambda s, b: ps[:, 4 * s + b, :].rearrange("p (x c t) -> p x c t", x=2, c=RT)
        zero = lambda j: isinstance(j, int) and j == 0
        NP, NA, NV = 21, 10, 14
        (TAB, TKV, MAB, QAR, QKR, SQ2, X2, SQ4, X3, SQ8, X4, HH, HTY, R2, R3, WW, MV, VA, UU, SS, YY) = range(NP)
        UD, UO, US, UI = 0, 2, 4, 5

        with nc.Block() as block:
            @block.sync
            def _(sp):
                sp.dma_start(masks[:, :, :, :, :], t["c_masks"].rearrange("p (a b c d) -> p a b c d", a=2, b=6, c=RT)).then_inc(c_in, 16)
                sp.dma_start(eye[:, :, :], t["c_eye"].rearrange("p (c d) -> p c d", c=RT)).then_inc(c_in, 16)

            @block.gpsimd
            def _(pool):
                def feed(j, s):
                    for i in range(5):
                        if not zero(j):
                            pool.wait_ge(prod[s], NP * (j - 1) + QKR + 1 if i < 4 else NP * j)
                        pool.tensor_copy(xin[s][:, i], src[i][:, :, bass.ds((2 * j + s) * CHUNK, CHUNK)]).then_inc(fed[s], 1)

                feed(0, 0)
                feed(0, 1)
                with pool.Fori(1, NJ + 1) as j:
                    feed(j, 0)
                    feed(j, 1)

            @block.scalar
            def _(act):
                def keep(j, s, p, dst, frm):
                    act.wait_ge(prod[s], NP * j + p + 1)
                    act.activation(dst, frm, ACT.Copy).then_inc(kept_a[s], 1)

                def chunks(j):
                    for s in two:
                        keep(j, s, TAB, tok[s][:, 0:2], bank(s, 0))
                    for s in two:
                        keep(j, s, TKV, tok[s][:, 2:4], bank(s, 1))
                    for s in two:
                        keep(j, s, SQ2, sq2[s][:, :], bank(s, 1))
                    for s in two:
                        keep(j, s, SQ4, sq4[s][:, :], bank(s, 3))
                    for s in two:
                        keep(j, s, SQ8, m8[s][:, :], bank(s, 1)[:, 0])
                    for s in two:
                        keep(j, s, HTY, hty[s][:, :], bank(s, 0))
                    for s in two:
                        keep(j, s, WW, w[s][:, :], bank(s, 3)[:, 0])
                    for s in two:
                        keep(j, s, MV, mv[s][:, :], bank(s, 0)[:, 0])
                    for s in two:
                        keep(j, s, VA, va[s][:, :], bank(s, 1))

                with act.Fori(0, NJ) as j:
                    chunks(j)
                    for s in two:
                        keep(j, s, YY, R["a"][:, :, bass.ds((2 * j + s) * CHUNK, CHUNK)], bank(s, 0)[:, 0])
                chunks(NJ)

            @block.vector
            def _(dve):
                def chunks(j, kind):
                    mk = masks[:, kind]
                    for s in two:
                        dve.wait_ge(prod[s], NP * j + MAB + 1)
                        dve.tensor_tensor(dg[s][:, :], bank(s, 2), mk[:, UD:UD + 2], ALU.mult).then_inc(kept_v[s], 1)
                        dve.tensor_tensor(od[s][:, :], bank(s, 2), mk[:, UO:UO + 2], ALU.mult).then_inc(kept_v[s], 1)
                    for s in two:
                        dve.wait_ge(prod[s], NP * j + QAR + 1)
                        dve.tensor_tensor(qm[s][:, 0:2], bank(s, 3), mk[:, US:US + 2], ALU.mult).then_inc(kept_v[s], 1)
                    for s in two:
                        dve.wait_ge(prod[s], NP * j + QKR + 1)
                        dve.tensor_tensor(qm[s][:, 2], bank(s, 0)[:, 0], mk[:, UI], ALU.mult).then_inc(kept_v[s], 1)
                        dve.wait_ge(kept_v[s], NV * j + 1)
                        dve.tensor_tensor(x[s][:, :], dg[s][:, 0], eye[:, :], ALU.add).then_inc(kept_v[s], 1)
                    for n, (p, b) in enumerate(((X2, 2), (X3, 0), (X4, 2))):
                        for s in two:
                            dve.wait_ge(prod[s], NP * j + p + 1)
                            dve.wait_ge(kept_v[s], NV * j + 5 + n)
                            dve.tensor_tensor(x[s][:, :], bank(s, b)[:, 0], x[s][:, :], ALU.add).then_inc(kept_v[s], 1)
                    for p, b in ((HH, 3), (R2, 1), (R3, 2)):
                        for s in two:
                            dve.wait_ge(prod[s], NP * j + p + 1)
                            dve.tensor_tensor(r[s][:, :], bank(s, b)[:, 0], eye[:, :], ALU.add).then_inc(kept_v[s], 1)

                def states(j):
                    for s in two:
                        dve.wait_ge(prod[s], NP * j + UU + 1)
                        dve.wait_ge(kept_a[s], NA * j + 9)
                        dve.tensor_tensor(u[s][:, :], bank(s, 2)[:, 0], va[s][:, 0], ALU.add).then_inc(kept_v[s], 1)
                        dve.wait_ge(prod[s], NP * j + SS + 1)
                        if s == 1:
                            dve.wait_ge(prod[0], NP * (j + 1))
                        elif not zero(j):
                            dve.wait_ge(prod[1], NP * j)
                        nxt = st[1 - s]
                        dve.tensor_tensor(nxt[:, :], bank(s, 3)[:, 0], st[s][:, :], ALU.add).then_inc(kept_v[s], 1)
                        dve.wait_ge(kept_v[s], NV * j + 13)
                        dve.tensor_tensor(nxt[:, :], nxt[:, :], R["pend"][:, :, bass.ds(2 * j + s, 1)].broadcast_to([P, RT, CHUNK]), ALU.mult).then_inc(kept_v[s], 1)
                        dve.wait_ge(kept_v[s], NV * j + 14)

                dve.wait_ge(c_in, 32)
                dve.memset(st[0][:, :, :], 0.0).then_inc(zeroed, 1)
                dve.wait_ge(zeroed, 1)
                chunks(0, 0)
                states(0)
                with dve.Fori(1, NJ) as j:
                    chunks(j, 0)
                    states(j)
                chunks(NJ, 1)

            @block.tensor
            def _(pe):
                def each(s, b, g, *terms, inc=False):
                    for c in range(RT):
                        for h in range(2):
                            rows = slice(64 * h, 64 * h + 64)
                            for n, (lhs, rhs) in enumerate(terms):
                                ins = pe.matmul(bank(s, b)[rows, g, c], lhs[rows, c], rhs[rows, c] if rhs is not eye else eye[rows, 0],
                                                start=n == 0, stop=n == len(terms) - 1)
                    if inc:
                        ins.then_inc(prod[s], 1)

                awaited = pe.alloc_register("awaited")

                def wait_count(sem, count):
                    if isinstance(count, int):
                        pe.wait_ge(sem, count)
                    else:
                        pe.reg_mov(awaited, count)
                        pe.wait_ge(c_in, 32)
                        pe.wait_ge(sem, awaited)

                def after(s, j, v=0, a=0, before_v=0, before_a=0, first=False):
                    if v:
                        wait_count(kept_v[s], NV * j + v)
                    if a:
                        wait_count(kept_a[s], NA * j + a)
                    if before_v and not first:
                        wait_count(kept_v[s], NV * (j - 1) + before_v)
                    if before_a and not first:
                        wait_count(kept_a[s], NA * (j - 1) + before_a)

                def chunks(j, first=False):
                    for s in two:
                        wait_count(fed[s], 5 * j + 2)
                        after(s, j, before_a=10, first=first)
                        each(s, 0, 0, (xin[s][:, 0], eye))
                        each(s, 0, 1, (xin[s][:, 1], eye), inc=True)
                    for s in two:
                        wait_count(fed[s], 5 * j + 4)
                        after(s, j, before_a=9, first=first)
                        each(s, 1, 0, (xin[s][:, 2], eye))
                        each(s, 1, 1, (xin[s][:, 3], eye), inc=True)
                    for s in two:
                        after(s, j, before_v=12, first=first)
                        each(s, 2, 0, (xin[s][:, 1], xin[s][:, 0]))
                        each(s, 2, 1, (xin[s][:, 0], xin[s][:, 1]), inc=True)
                    for s in two:
                        wait_count(fed[s], 5 * j + 5)
                        after(s, j, before_v=13, first=first)
                        each(s, 3, 0, (xin[s][:, 2], xin[s][:, 0]))
                        each(s, 3, 1, (xin[s][:, 1], xin[s][:, 4]), inc=True)
                    for s in two:
                        after(s, j, a=1)
                        each(s, 0, 0, (xin[s][:, 2], xin[s][:, 4]), inc=True)
                    up, low = 0, 1
                    for s in two:
                        after(s, j, v=1, a=2)
                        each(s, 1, 0, (dg[s][:, low], dg[s][:, up]))
                        each(s, 1, 1, (dg[s][:, up], dg[s][:, low]), inc=True)
                    for s in two:
                        after(s, j, v=5, a=3)
                        each(s, 2, 0, (sq2[s][:, low], x[s]), inc=True)
                    for s in two:
                        each(s, 3, 0, (sq2[s][:, low], sq2[s][:, up]))
                        each(s, 3, 1, (sq2[s][:, up], sq2[s][:, low]), inc=True)
                    for s in two:
                        after(s, j, v=6, a=4)
                        each(s, 0, 0, (sq4[s][:, low], x[s]), inc=True)
                    for s in two:
                        each(s, 1, 0, (sq4[s][:, up], sq4[s][:, low]), inc=True)
                    for s in two:
                        after(s, j, v=7, a=5)
                        each(s, 2, 0, (m8[s], x[s]), inc=True)
                    for s in two:
                        after(s, j, v=8)
                        each(s, 3, 0, (od[s][:, low], x[s]), inc=True)
                    for s in two:
                        each(s, 0, 0, (x[s], od[s][:, low]))
                        each(s, 0, 1, (x[s], eye), inc=True)
                    for s in two:
                        after(s, j, v=9, a=6)
                        each(s, 1, 0, (hty[s][:, 0], r[s]), inc=True)
                    for s in two:
                        after(s, j, v=10)
                        each(s, 2, 0, (hty[s][:, 0], r[s]), inc=True)
                    for s in two:
                        after(s, j, v=11)
                        each(s, 3, 0, (hty[s][:, 1], r[s]), inc=True)
                    for s in two:
                        each(s, 0, 0, (qm[s][:, 0], tok[s][:, 3]), inc=True)
                    for s in two:
                        after(s, j, a=8)
                        each(s, 1, 0, (w[s], mv[s]))
                        each(s, 1, 1, (tok[s][:, 0], w[s]), inc=True)

                def states(j, first=False):
                    for s in two:
                        after(s, j, a=9)
                        if s == 1:
                            wait_count(kept_v[0], NV * (j + 1))
                        elif not first:
                            wait_count(kept_v[1], NV * j)
                        each(s, 2, 0, (va[s][:, 1], st[s]), inc=True)
                        after(s, j, v=12)
                        each(s, 3, 0, (tok[s][:, 1], u[s]), (tok[s][:, 2], tok[s][:, 3]), inc=True)
                        each(s, 0, 0, (st[s], xin[s][:, 4]), (u[s], qm[s][:, 1]), (tok[s][:, 3], qm[s][:, 2]), inc=True)

                pe.wait_ge(c_in, 32)
                pe.wait_ge(zeroed, 1)
                chunks(0, True)
                states(0, True)
                with pe.Fori(1, NJ) as j:
                    chunks(j)
                    states(j)
                chunks(NJ)

        rwkv_states(nc, t, S, R, sb, sem, eye, xin, tok, qm, va, u, st)


def rwkv_states(nc, t, S, R, sb, sem, eye, xin, tok, qm, va, u, st):
    ps = S["ps"]
    two = range(2)
    sst = sb("sst", [P, NB, RT, CHUNK])
    stT = sb("stT", [P, NB, RT, CHUNK])
    ut = [sb(f"ut{s}", [P, RT, CHUNK]) for s in two]
    bk = [sb(f"bk{s}", [P, 2, RT, CHUNK]) for s in two]
    fin = sb("fin", [P, RT, CHUNK])
    rmask = sb("rmask", [P, 4])
    c_in, stored, turned, turned_a, turned_v, fin_mm, fin_out, ut_mm, ut_out, u_mm, u_out, y_mm, y_out = (sem(n) for n in
        ("s_c_in", "s_stored", "turned", "turned_a", "turned_v", "fin_mm", "fin_out", "ut_mm", "ut_out", "u_mm", "u_out", "y_mm", "y_out"))
    masked, new_mm, new_sum, new_done, back_mm, back_out = (sem(n) for n in ("masked", "new_mm", "new_sum", "new_done", "back_mm", "back_out"))
    bank = lambda b: ps[:, b, :].rearrange("p (x c t) -> p x c t", x=2, c=RT)
    heads_of = lambda a: a.rearrange("(c h) i j -> h i c j", h=2)
    with nc.Block() as block:
        @block.sync
        def _(sp):
            sp.dma_start(rmask[:, :], t["c_rmask"]).then_inc(c_in, 16)
            for b in range(NB):
                for h in range(2):
                    sp.dma_start(sst[64 * h:64 * h + 64, b], heads_of(t["state_rwkv"][b])[h]).then_inc(c_in, 16)
            sp.wait_ge(fin_out, 1)
            for h in range(2):
                sp.dma_start(heads_of(t["new_rwkv_prompt"])[h], fin[64 * h:64 * h + 64]).then_inc(stored, 16)
            for b in range(NB):
                sp.wait_ge(back_out, b + 1)
                for h in range(2):
                    sp.dma_start(heads_of(t["new_rwkv_sample"][b])[h], sst[64 * h:64 * h + 64, b]).then_inc(stored, 16)
            sp.wait_ge(stored, 16 * 2 * (NB + 1))

        @block.scalar
        def _(act):
            for g in (0, 2):
                act.wait_ge(turned, g + 1)
                act.activation(stT[:, 2 * g:2 * g + 2], bank(g), ACT.Copy).then_inc(turned_a, 1)
            for s in two:
                act.wait_ge(ut_mm, s + 1)
                act.activation(ut[s][:, :], bank(6 + s)[:, 0], ACT.Copy).then_inc(ut_out, 1)
            for s in two:
                act.wait_ge(y_mm, s + 1)
                act.activation(R["a"][:, :, SEQ + s * CHUNK:SEQ + (s + 1) * CHUNK], bank(6 + s)[:, 0], ACT.Copy).then_inc(y_out, 1)
            for b in range(NB):
                act.wait_ge(back_mm, b + 1)
                act.activation(sst[:, b], bank(4 + b % 2)[:, 0], ACT.Copy).then_inc(back_out, 1)

        @block.vector
        def _(dve):
            def update(b):
                dve.wait_ge(new_mm, b + 1)
                dve.tensor_tensor(stT[:, b], bank(b % 4)[:, 0], stT[:, b], ALU.add).then_inc(new_sum, 1)
                dve.wait_ge(new_sum, b + 1)
                pend = R["pend"][:, :, SEQ // CHUNK + b:SEQ // CHUNK + b + 1]
                dve.tensor_tensor(stT[:, b], stT[:, b], pend.broadcast_to([P, RT, CHUNK]), ALU.mult).then_inc(new_done, 1)

            for n, g in enumerate((1, 3)):
                dve.wait_ge(turned, g + 1)
                dve.tensor_copy(stT[:, 2 * g:2 * g + 2], bank(g)).then_inc(turned_v, 1)
            dve.wait_ge(fin_mm, 1)
            dve.tensor_copy(fin[:, :], bank(4)[:, 0]).then_inc(fin_out, 1)
            for s in two:
                dve.wait_ge(u_mm, s + 1)
                dve.tensor_tensor(u[s][:, :], bank(4 + s)[:, 0], va[s][:, 0], ALU.add).then_inc(u_out, 1)
            for b in range(NB):
                dve.wait_ge(c_in, 16 * (2 * NB + 1))
                if b >= 2:
                    dve.wait_ge(new_mm, b - 1)
                dve.tensor_scalar(bk[b % 2][:, :], tok[b // 4][:, 1:3], rmask[:, b % 4:b % 4 + 1], None, ALU.mult).then_inc(masked, 1)
                if b >= 1:
                    update(b - 1)
            update(NB - 1)

        @block.tensor
        def _(pe):
            def each(out, *terms, more=()):
                for c in range(RT):
                    for h in range(2):
                        rows = slice(64 * h, 64 * h + 64)
                        for n, (lhs, rhs) in enumerate(terms):
                            ins = pe.matmul(out[rows, c], lhs[rows, c], rhs[rows, c] if rhs is not eye else eye[rows, 0],
                                            start=n == 0, stop=n == len(terms) - 1 and not more)
                        for q, (lhs, rhs) in enumerate(more):
                            cols = slice(NQ * q, NQ * q + NQ)
                            ins = pe.matmul(out[rows, c, cols], lhs[rows, c], rhs[rows, c, cols], start=not terms, stop=not terms or q == 3)
                return ins

            def back(b):
                pe.wait_ge(new_done, b + 1)
                if b < 2:
                    pe.wait_ge(u_out, 2)
                else:
                    pe.wait_ge(back_out, b - 1)
                each(bank(4 + b % 2)[:, 0], (stT[:, b], eye)).then_inc(back_mm, 1)

            pe.wait_ge(c_in, 16 * (2 * NB + 1))
            for g in range(4):
                for i in two:
                    ins = each(bank(g)[:, i], (sst[:, 2 * g + i], eye))
                ins.then_inc(turned, 1)
            each(bank(4)[:, 0], (st[0], eye)).then_inc(fin_mm, 1)
            pe.wait_ge(turned_a, 2)
            pe.wait_ge(turned_v, 2)
            for s in two:
                each(bank(6 + s)[:, 0], more=[(stT[:, 4 * s + q], va[s][:, 1]) for q in range(4)]).then_inc(ut_mm, 1)
            for s in two:
                pe.wait_ge(ut_out, s + 1)
                if s == 0:
                    pe.wait_ge(fin_out, 1)
                each(bank(4 + s)[:, 0], (ut[s], eye)).then_inc(u_mm, 1)
            for s in two:
                pe.wait_ge(u_out, s + 1)
                each(bank(6 + s)[:, 0], (u[s], qm[s][:, 1]), (tok[s][:, 3], qm[s][:, 2]),
                     more=[(stT[:, 4 * s + q], xin[s][:, 4]) for q in range(4)]).then_inc(y_mm, 1)
            for b in range(NB):
                pe.wait_ge(masked, b + 1)
                if b >= 4:
                    pe.wait_ge(new_sum, b - 3)
                each(bank(b % 4)[:, 0], (bk[b % 2][:, 0], u[b // 4]), (bk[b % 2][:, 1], tok[b // 4][:, 3])).then_inc(new_mm, 1)
                if b >= 1:
                    back(b - 1)
            back(NB - 1)


def rwkv_output(nc, t, S, R):
    with stage(nc, "ro_") as (ctx, sb, sem):
        ps = S["ps"]
        out = sb("out", [P, RT, TOK])
        in_, cent_mm, centred, squared, var_mm, rooted, chain, done, stored = (sem(n) for n in
            ("in_", "cent_mm", "centred", "squared", "var_mm", "rooted", "chain", "done", "stored"))
        block = ctx.enter_context(nc.Block())
        y, g, bonus, sq, root = R["a"], R["b"], R["k"], R["v"], R["r"]
        vec = lambda name, k: S["vec"][:, VEC_AT[name] + k:VEC_AT[name] + k + 1]
        third = lambda a: a.rearrange("p (n t) -> p n t", n=3)
        three = lambda i: ps[:, 3 * (i % 2):3 * (i % 2) + 3, 0:TOK // 3]

        @block.sync
        def _(sp):
            sp.dma_start(g[:, :, :], feature_tiles(t["gT"], 0, TOK)).then_inc(in_, 16)
            sp.dma_start(bonus[:, :, :], feature_tiles(t["bonusT"], 0, TOK)).then_inc(in_, 16)
            for c in range(RT):
                sp.wait_ge(done, c + 1)
                sp.dma_start(feature_tiles(t["rwT"], 0, TOK)[:, c], out[:, c]).then_inc(stored, 16)
            sp.wait_ge(stored, 16 * RT)

        @block.scalar
        def _(act):
            for c in range(RT):
                act.wait_ge(centred, c + 1)
                act.activation(sq[:, c], y[:, c], ACT.Square).then_inc(squared, 1)
            for c in range(RT):
                act.wait_ge(var_mm, c + 1)
                act.activation(third(root[:, c]), three(c), ACT.Sqrt, bias=S["lnx_eps"][:, 0:1], scale=1.0 / 64).then_inc(rooted, 1)

        @block.vector
        def _(dve):
            own = Chain(dve, chain)
            for c in range(RT):
                dve.wait_ge(cent_mm, c + 1)
                dve.scalar_tensor_tensor(third(y[:, c]), three(c), -1.0 / 64, third(y[:, c]), ALU.mult, ALU.add).then_inc(centred, 1)
            for c in range(RT):
                dve.wait_ge(rooted, c + 1)
                own.do(dve.reciprocal(root[:, c], root[:, c]))
                own.do(dve.scalar_tensor_tensor(out[:, c], y[:, c], vec("rwkv_lnx_g", c), root[:, c], ALU.mult, ALU.mult))
                dve.wait_ge(in_, 32)
                own.do(dve.scalar_tensor_tensor(out[:, c], out[:, c], vec("rwkv_lnx_b", c), bonus[:, c], ALU.add, ALU.add))
                dve.tensor_tensor(out[:, c], out[:, c], g[:, c], ALU.mult).then_inc(done, 1)

        @block.tensor
        def _(pe):
            for n, (x, of) in enumerate(((y, cent_mm), (sq, var_mm))):
                for c in range(RT):
                    if n == 1:
                        pe.wait_ge(squared, c + 1)
                        pe.wait_ge(centred, RT)
                    if n == 1 and c >= 2:
                        pe.wait_ge(rooted, c - 1)
                    elif n == 0 and c >= 2:
                        pe.wait_ge(centred, c - 1)
                    for b in range(3):
                        ins = pe.matmul(ps[:, 3 * (c % 2) + b, 0:TOK // 3], R["block"][:, :], x[:, c, b * (TOK // 3):(b + 1) * (TOK // 3)], start=True, stop=True)
                    ins.then_inc(of, 1)


def rwkv(nc, t, S):
    with ExitStack() as ctx:
        sb = lambda n, s: ctx.enter_context(nc.sbuf_tensor("rw_" + n, s, F32))
        R = {n: sb(n, [P, RT, TOK]) for n in ("r", "k", "v", "a", "b")}
        R["pend"] = sb("pend", [P, RT, SEQ // CHUNK + NB])
        R["block"] = sb("block", [P, P])
        rwkv_prepare(nc, t, S, R)
        rwkv_chunks(nc, t, S, R)
        rwkv_output(nc, t, S, R)


def shared(nc, ctx):
    sb = lambda n, s, d=F32: ctx.enter_context(nc.sbuf_tensor(n, s, d))
    return {"ident": sb("ident", [P, P]), "ones": sb("ones", [P, P]), "eps": sb("eps_col", [P, 1]),
            "lnx_eps": sb("lnx_eps_col", [P, 1]), "vec": sb("vec", [P, NVEC]),
            "neg_lam": sb("neg_lam", [P, 1]), "qk_sample": sb("qk_sample", [P, 8, NB * NQ]),
            "ps": ctx.enter_context(nc.psum_tensor("ps", [P, 8, 512], F32))}


def constants():
    f = np.float32
    pos = np.concatenate([np.arange(SEQ), np.tile(PAST + np.arange(NQ), NB)]).astype(f)
    inv = (f(10000.0) ** (-np.arange(32, dtype=f) / f(32))).astype(f)
    ang = (pos[None, :] * inv[:, None]).astype(f).astype(np.float64)
    rot = np.zeros((P, P), f)
    for d in range(P):
        rot[d + 32 if d % 64 < 32 else d - 32, d] = -1 if d % 64 < 32 else 1
    mask = np.zeros((1, P + CHUNK), f)
    mask[0, :CHUNK] = 1
    mask[0, P:] = -1e30
    pick, sign = np.zeros((P, 64), f), np.zeros((P, 2), f)
    for h in range(HEADS):
        for m in range(2):
            for q in range(NQ):
                row = h * 2 * NQ + m * NQ + q
                pick[row, h * NQ + q] = 1
                sign[row, m] = 1
    starts = np.ones((P, TOK), f)
    starts[:, 0:SEQ:CHUNK] = 0
    starts[:, SEQ::NQ] = 0
    row, col = np.arange(P)[:, None] % 64, np.arange(64)[None, :]
    same = row // NQ == col // NQ
    upper, lower = col > row, col < row
    diag = [upper & same, lower & same]
    kinds = [diag + [upper & ~same, lower & ~same, upper, upper | (col == row)],
             diag + [upper & False, lower & False, upper & same, (upper | (col == row)) & same]]
    masks = np.stack([np.stack([np.repeat(m[:, None], RT, 1) for m in k], 1) for k in kinds], 1).astype(f)
    eye = np.repeat((row == col)[:, None], RT, 1).astype(f)
    extra = {"c_starts": starts, "c_masks": masks.reshape(P, -1), "c_eye": eye.reshape(P, -1),
             "c_block": np.kron(np.eye(2, dtype=f), np.ones((64, 64), f)),
             "c_rmask": (row // NQ == np.arange(4)[None, :]).astype(f)}
    return {**extra, "c_ident": np.eye(P, dtype=f), "c_rot": rot, "c_cos": np.tile(np.cos(ang), (4, 1)).astype(f),
            "c_sin": np.tile(np.sin(ang), (4, 1)).astype(f), "c_mask": mask, "c_pick": pick, "c_sign": sign}


def store_output(nc, t, S):
    with stage(nc, "so_") as (ctx, sb, sem):
        ps = S["ps"]
        xfeat = sb("xfeat", [P, DT, TOK])
        xtok = sb("xtok", [P, TOK // P, D])
        x_in, half_t, copied_a, copied_v, stored = (sem(n) for n in ("x_in", "half_t", "copied_a", "copied_v", "stored"))
        block = ctx.enter_context(nc.Block())
        NT = TOK // P
        units = [(m, f) for m in range(NT) for f in range(2)]

        @block.sync
        def _(sp):
            sp.dma_start(xfeat[:, :, :], feature_tiles(t["res3"], 0, TOK)).then_inc(x_in, 16)
            for m in range(NT):
                sp.wait_ge(copied_a, m + 1)
                sp.wait_ge(copied_v, m + 1)
                dst = t["y_prompt"][0, m * P:(m + 1) * P] if m < NT - 1 else t["y_sample"].rearrange("b s d -> (b s) d")
                sp.dma_start(dst, xtok[:, m, :]).then_inc(stored, 16)
            sp.wait_ge(stored, 16 * NT)

        @block.tensor
        def _(pe):
            pe.wait_ge(x_in, 16)
            for n, (m, f) in enumerate(units):
                if n >= 4:
                    pe.wait_ge(copied_a if n % 2 == 0 else copied_v, (n - 4) // 2 + 1)
                for i in range(4):
                    ins = pe.transpose(ps[:, n % 4, i * P:(i + 1) * P], xfeat[:, 4 * f + i, m * P:(m + 1) * P], S["ident"][:, :])
                ins.then_inc(half_t, 1)

        @block.scalar
        def _(act):
            for m in range(NT):
                act.wait_ge(half_t, 2 * m + 1)
                act.activation(xtok[:, m, 0:512], ps[:, (2 * m) % 4, :], ACT.Copy).then_inc(copied_a, 1)

        @block.vector
        def _(dve):
            for m in range(NT):
                dve.wait_ge(half_t, 2 * m + 2)
                dve.tensor_copy(xtok[:, m, 512:1024], ps[:, (2 * m + 1) % 4, :]).then_inc(copied_v, 1)


SCRATCH = [("res0", (D, TOK)), ("res1", (D, TOK)), ("res2", (D, TOK)), ("res3", (D, TOK)), ("zT", (Z_TILES * P, TOK)),
           ("attT", (D // 2, TOK)), ("rwT", (D // 2, TOK)), ("gT", (D // 2, TOK)), ("bonusT", (D // 2, TOK))]


def program(nc, t):
    for name, shape in SCRATCH:
        t[name] = nc.dram_tensor(name + "_scratch", shape, F32, kind="Internal").ap()
    with ExitStack() as ctx:
        S = shared(nc, ctx)
        load_inputs(nc, t, S)
        for half in range(2):
            ffn_half(nc, t, S, f"fa{half}_", half, t["res0"], t["res1"], t["ffn1_w_in"], t["ffn1_w_out"], "ffn1_pre_g", "ffn1_post_g")
        in_projection(nc, t, S)
        prompt_attention(nc, t, S)
        sample_attention(nc, t, S)
        rwkv(nc, t, S)
        for half in range(2):
            out_projection_half(nc, t, S, f"op{half}_", half)
        for half in range(2):
            ffn_half(nc, t, S, f"fb{half}_", half, t["res2"], t["res3"], t["ffn2_w_in"], t["ffn2_w_out"], "ffn2_pre_g", "ffn2_post_g")
        store_output(nc, t, S)


INPUTS = ["x_prompt", "x_sample", "cache_att_k", "cache_att_v", "state_rwkv", "state_shift", "ffn1_pre_g", "ffn1_w_in",
          "ffn1_w_out", "ffn1_post_g", "mix_pre_g", "w_in", "att_lambda_q1", "att_lambda_k1", "att_lambda_q2",
          "att_lambda_k2", "att_subln_g", "rwkv_mu", "rwkv_w0", "rwkv_w2", "rwkv_a0", "rwkv_a2", "rwkv_g2", "rwkv_k_k",
          "rwkv_k_a", "rwkv_r_k", "rwkv_lnx_g", "rwkv_lnx_b", "w_o_att", "w_o_rwkv", "w_out", "mix_post_g",
          "ffn2_pre_g", "ffn2_w_in", "ffn2_w_out", "ffn2_post_g"]
AS = {"cache_att_k": (NB, PAST, D // 2), "cache_att_v": (NB, PAST, D // 2), "state_rwkv": (NB, 8, 64, 64),
      "ffn1_w_in": (D, 2 * FF), "ffn1_w_out": (FF, D), "w_in": (D, Z_TILES * P), "rwkv_w2": (64, D // 2),
      "rwkv_a2": (64, D // 2), "rwkv_g2": (P, D // 2), "w_o_att": (D // 2, D), "w_o_rwkv": (D // 2, D),
      "w_out": (D, D), "ffn2_w_in": (D, 2 * FF), "ffn2_w_out": (FF, D)}
OUTPUTS = [("y_prompt", (1, SEQ, D), (1, SEQ, D)), ("y_sample", (NB, NQ, D), (NB, NQ, D)),
           ("new_k_prompt", (SEQ, D // 2), (1, 1, SEQ, HEADS, 2, 64)), ("new_v_prompt", (SEQ, D // 2), (1, 1, SEQ, HEADS, P)),
           ("new_rwkv_prompt", (8, 64, 64), (1, 1, 8, 64, 64)), ("new_shift_prompt", (1, ZRT * P), (1, 1, 1, ZRT * P)),
           ("new_k_sample", (NB * NQ, D // 2), (1, NB, NQ, HEADS, 2, 64)), ("new_v_sample", (NB * NQ, D // 2), (1, NB, NQ, HEADS, P)),
           ("new_rwkv_sample", (NB, 8, 64, 64), (1, NB, 8, 64, 64)), ("new_shift_sample", (NB, ZRT * P), (1, NB, 1, ZRT * P))]


def kernel(**inputs):
    import concourse.bacc as bacc
    from concourse.bass_utils import run_bass_kernel_spmd

    nc = bacc.Bacc("TRN2", target_bir_lowering=False, num_devices=1)
    arrays, t = {}, {}
    shaped = {name: np.ascontiguousarray(inputs[name]).reshape(AS.get(name, inputs[name].shape)) for name in INPUTS}
    for name, a in {**shaped, **constants()}.items():
        arrays[f"in_{name}_dram"] = a
        t[name] = nc.dram_tensor(f"in_{name}_dram", a.shape, mybir.dt.from_np(a.dtype), kind="ExternalInput").ap()
    for i, (name, shape, _) in enumerate(OUTPUTS):
        t[name] = nc.dram_tensor(f"out_{i}_dram", shape, F32, kind="ExternalOutput").ap()
    program(nc, t)
    r = run_bass_kernel_spmd(nc, [arrays], core_ids=[0])
    return tuple(r.results[0][f"out_{i}_dram"].reshape(full) for i, (_, _, full) in enumerate(OUTPUTS))
```

```python
from contextlib import ExitStack, contextmanager

import numpy as np

import concourse.bass as bass
from concourse import mybir

F32 = mybir.dt.float32
F32R = mybir.dt.float32r
ALU = mybir.AluOpType
ACT = mybir.ActivationFunctionType
AX = mybir.AxisListType.X

P = 128
D = 1024
DT = D // P
SEQ = 1024
NB = 8
NQ = 16
TOK = SEQ + NB * NQ
HALF = TOK // 2
NN = HALF // 2
FF = 2816
FT = FF // P
KS = 4
EPS = 1e-6
Z_TILES = 42
Z_GATES = 16
ZQ, ZK, ZV, ZR = 0, 4, 8, 12
HEADS = 4
SCALE = 64 ** -0.5
CHUNK = 64
RT = 4
ZRT = 14
KAPPA = float(np.exp(-0.5))
LAM_INIT = 0.8 - 0.6
PAST = 1024

VECS = [("ffn1_pre_g", 8), ("ffn1_post_g", 8), ("mix_pre_g", 8), ("mix_post_g", 8), ("ffn2_pre_g", 8),
        ("ffn2_post_g", 8), ("rwkv_mu", 14), ("rwkv_w0", 4), ("rwkv_a0", 4), ("rwkv_k_k", 4),
        ("rwkv_k_a", 4), ("rwkv_r_k", 4), ("rwkv_lnx_g", 4), ("rwkv_lnx_b", 4), ("att_subln_g", 1)]
VEC_AT = {}
_at = 0
for _n, _k in VECS:
    VEC_AT[_n] = _at
    _at += _k
NVEC = _at


class Chain:

    def __init__(self, eng, sem):
        self.eng, self.sem, self.n = eng, sem, 0

    def mark(self, ins):
        ins.then_inc(self.sem, 1)
        self.n += 1

    def wait(self):
        self.eng.wait_ge(self.sem, self.n)

    def do(self, ins):
        self.mark(ins)
        self.wait()


@contextmanager
def stage(nc, tag):
    used = []
    with ExitStack() as buffers:
        sb = lambda n, s, d=F32: buffers.enter_context(nc.sbuf_tensor(tag + n, s, d))

        def sem(n):
            used.append(nc.alloc_semaphore(tag + n))
            return used[-1]

        with ExitStack() as ctx:
            yield ctx, sb, sem
        nc.clear_and_free_semaphores(used)
        nc.all_engine_barrier()


def feature_tiles(dram, t0, t1):
    return dram.rearrange("(k p) t -> p k t", p=P)[:, :, t0:t1]


def load_inputs(nc, t, S):
    with stage(nc, "li_") as (ctx, sb, sem):
        ps = S["ps"]
        rows = sb("rows", [NVEC, P])
        xtok = sb("xtok", [P, TOK // P, D])
        xfeat = sb("xfeat", [P, DT, TOK])
        consts_in, rows_in, x_in, stored = sem("consts_in"), sem("rows_in"), sem("x_in"), sem("stored")
        vec_t, vec_done, half_t, copied_a, copied_v = (sem(n) for n in ("vec_t", "vec_done", "half_t", "copied_a", "copied_v"))
        ones_set = sem("ones_set")
        block = ctx.enter_context(nc.Block())
        NT = TOK // P
        units = [(m, f) for m in range(NT) for f in range(2)]

        @block.sync
        def _(sp):
            sp.dma_start(S["ident"][:, :], t["c_ident"]).then_inc(consts_in, 16)
            at = 0
            for name, k in VECS:
                src = t[name].rearrange("a b c -> (a b c)") if len(t[name].shape) == 3 else t[name].rearrange("a b -> (a b)")
                sp.dma_start(rows[at:at + k, :], src.rearrange("(k p) -> k p", p=P)).then_inc(rows_in, 16)
                at += k
            sp.dma_start(xtok[:, 0:SEQ // P, :], t["x_prompt"].rearrange("b (n p) d -> p (b n) d", p=P)).then_inc(x_in, 16)
            sp.dma_start(xtok[:, SEQ // P, :], t["x_sample"].rearrange("b s d -> (b s) d")).then_inc(x_in, 16)
            sp.wait_ge(copied_a, len(units) // 2)
            sp.wait_ge(copied_v, len(units) // 2)
            sp.dma_start(feature_tiles(t["res0"], 0, TOK), xfeat[:, :, :]).then_inc(stored, 16)
            sp.wait_ge(stored, 16)

        @block.tensor
        def _(pe):
            pe.wait_ge(consts_in, 16)
            pe.wait_ge(rows_in, 16 * len(VECS))
            pe.transpose(ps[:, 7, 0:NVEC], rows[:, :], S["ident"][0:NVEC, 0:NVEC]).then_inc(vec_t, 1)
            pe.wait_ge(x_in, 32)
            for n, (m, f) in enumerate(units):
                if n >= 4:
                    pe.wait_ge(copied_a if n % 2 == 0 else copied_v, (n - 4) // 2 + 1)
                for i in range(4):
                    ins = pe.transpose(ps[:, n % 4, i * P:(i + 1) * P], xtok[:, m, (4 * f + i) * P:(4 * f + i + 1) * P], S["ident"][:, :])
                ins.then_inc(half_t, 1)

        def copy_out(n, m, f):
            return xfeat[:, 4 * f:4 * f + 4, m * P:(m + 1) * P], ps[:, n % 4, :].rearrange("p (i q) -> p i q", i=4)

        @block.scalar
        def _(act):
            for n, (m, f) in enumerate(units):
                if n % 2 == 0:
                    act.wait_ge(half_t, n + 1)
                    act.activation(*copy_out(n, m, f), ACT.Copy).then_inc(copied_a, 1)

        @block.vector
        def _(dve):
            dve.memset(S["ones"][:, :], 1.0).then_inc(ones_set, 1)
            dve.memset(S["eps"][:, :], EPS).then_inc(ones_set, 1)
            dve.memset(S["lnx_eps"][:, :], 64e-5).then_inc(ones_set, 1)
            dve.wait_ge(vec_t, 1)
            dve.tensor_copy(S["vec"][:, :], ps[:, 7, 0:NVEC]).then_inc(vec_done, 1)
            dve.wait_ge(vec_done, 1)
            for n in ("ffn1_post_g", "ffn2_post_g"):
                g = S["vec"][:, VEC_AT[n]:VEC_AT[n] + 8]
                dve.tensor_scalar(g, g, 0.5, None, ALU.mult).then_inc(vec_done, 1)
            for n, (m, f) in enumerate(units):
                if n % 2 == 1:
                    dve.wait_ge(half_t, n + 1)
                    dve.tensor_copy(*copy_out(n, m, f)).then_inc(copied_v, 1)


def ffn_half(nc, t, S, tag, half, res_in, res_out, w_in, w_out, pre, post):
    t0, t1 = half * HALF, (half + 1) * HALF
    with stage(nc, tag) as (ctx, sb, sem):
        ps = S["ps"]
        xn = {h: sb("xn" + h, [P, DT, HALF], F32R) for h in ("hi", "lo")}
        hid = {h: sb("hid" + h, [P, FT, HALF], F32R) for h in ("hi", "lo")}
        work = sb("work", [P, DT, HALF])
        tmp = sb("tmp", [P, 4, HALF])
        raw = sb("raw", [P, 4, KS, P])
        w = {h: sb("w" + h, [P, 4, KS, P], F32R) for h in ("hi", "lo")}
        sq, ssum, rstd = tmp[:, 0:2], tmp[:, 2], tmp[:, 3]
        x_in = [sem(f"x_in{i}") for i in range(DT // 2)]
        gscaled, upped = sem("gscaled"), sem("upped")
        squared, summed, sum_mm, rooted, xhi, xlo = (sem(n) for n in
            ("squared", "summed", "sum_mm", "rooted", "xhi", "xlo"))
        raw_in = [sem(f"raw_in{q}") for q in range(4)]
        whi, wlo, used, silu_done, prod_done, hhi, hlo, y_done, ysq, yadd, stored, dchain = (sem(n) for n in
            ("whi", "wlo", "used", "silu_done", "prod_done", "hhi", "hlo", "y_done", "ysq", "yadd", "stored", "dchain"))
        back_in, normed, added_v, added_p = (sem(n) for n in ("back_in", "normed", "added_v", "added_p"))
        back = xn["hi"][:, :, :].bitcast(F32)
        block = ctx.enter_context(nc.Block())
        w_in_v = w_in.rearrange("(k p) n -> p k n", p=P)
        w_out_v = w_out.rearrange("(k p) n -> p k n", p=P)
        UP = 4
        N_UP = UP * FT
        DOWN = [(k, min(KS, FT - k)) for k in range(0, FT, KS)]
        ND = len(DOWN)
        vec = lambda name, k: S["vec"][:, VEC_AT[name] + k:VEC_AT[name] + k + 1]
        flat = lambda a: a.rearrange("p (n t) -> p n t", n=2)
        bank = lambda b: ps[:, b:b + 2, 0:NN]

        @block.sync
        def _(sp):
            def load(i):
                sp.dma_start(work[:, 2 * i:2 * i + 2], feature_tiles(res_in, t0, t1)[:, 2 * i:2 * i + 2]).then_inc(x_in[i], 16)

            def up(j, r, qs=range(UP)):
                for q in qs:
                    if not (isinstance(j, int) and 2 * j + r == 0):
                        sp.wait_ge(wlo, (2 * j + r - 1) * UP + q + 1)
                    col = (2 * j + r) * P + (q // 2) * FF
                    sp.dma_start(raw[:, q], w_in_v[:, (q % 2) * KS:(q % 2) * KS + KS, bass.ds(col, P)]).then_inc(raw_in[q], 16)

            load(0)
            load(1)
            up(0, 0, [0])
            load(2)
            load(3)
            up(0, 0, range(1, UP))
            up(0, 1)
            with sp.Fori(1, FT // 2) as j:
                up(j, 0)
                up(j, 1)

            def down(j):
                for r in range(2):
                    for i, (k, n) in enumerate(DOWN):
                        s = r * ND + i
                        sp.wait_ge(wlo, N_UP + j * 2 * ND + s - 4 + 1)
                        sp.dma_start(raw[:, s % 4, 0:n], w_out_v[:, k:k + n, bass.ds((2 * j + r) * P, P)]).then_inc(raw_in[s % 4], 16)

            down(0)
            sp.wait_ge(used, N_UP)
            sp.dma_start(back, feature_tiles(res_in, t0, t1)).then_inc(back_in, 16)
            with sp.Fori(1, DT // 2) as j:
                down(j)
            for k in range(DT):
                sp.wait_ge((added_p, added_v)[k % 2], k // 2 + 1)
                sp.dma_start(feature_tiles(res_out, t0, t1)[:, k], work[:, k]).then_inc(stored, 16)
            sp.wait_ge(stored, 16 * DT)

        @block.gpsimd
        def _(pool):
            pool.wait_ge(back_in, 16)
            for k in range(0, DT, 2):
                pool.wait_ge(normed, k + 1)
                pool.tensor_tensor(work[:, k], work[:, k], back[:, k], ALU.add).then_inc(added_p, 1)

        @block.scalar
        def _(act):
            def take(k):
                act.wait_ge(x_in[k // 2], 16)
                act.activation(xn["hi"][:, k], work[:, k], ACT.Identity, scale=vec(pre, k)).then_inc(xhi, 1)

            def split(j, r, first=False, qs=range(UP)):
                for q in qs:
                    act.wait_ge(raw_in[q], 16 * (2 * j + r + 1))
                    if not first:
                        act.wait_ge(used, (2 * j + r - 1) * UP + q + 1)
                    act.activation(w["hi"][:, q], raw[:, q], ACT.Copy).then_inc(whi, 1)

            def finish(j, r):
                act.wait_ge(gscaled, 2 * j + r + 1)
                act.activation(work[:, r], work[:, r], ACT.Silu).then_inc(silu_done, 1)
                act.wait_ge(prod_done, 2 * j + r + 1)
                act.activation(hid["hi"][:, bass.ds(2 * j + r, 1)], work[:, 2 + r:3 + r], ACT.Copy).then_inc(hhi, 1)

            def split_down(j, s, n):
                i = 2 * ND * j + s
                act.wait_ge(raw_in[s % 4], 16 * (FT + 2 * ND // 4 * j + s // 4 + 1))
                act.wait_ge(used, N_UP + i - 4 + 1)
                act.activation(w["hi"][:, s % 4, 0:n], raw[:, s % 4, 0:n], ACT.Copy).then_inc(whi, 1)

            def finish_down(j, r):
                act.wait_ge(used, N_UP + (2 * j + r + 1) * ND)
                act.activation(flat2(work[:, bass.ds(2 * j + r, 1)]), bank(4 * r), ACT.Copy).then_inc(y_done, 1)
                if not (isinstance(j, int) and j == 0):
                    act.wait_ge(yadd, 2 * j + r - 1)
                act.activation(flat(sq[:, r]), bank(4 * r), ACT.Square).then_inc(ysq, 1)

            flat2 = lambda a: a.rearrange("p o (n t) -> p (o n) t", n=2)
            for k in range(KS):
                take(k)
            split(0, 0, True, [0])
            for k in range(KS, DT):
                take(k)
            split(0, 0, True, range(1, UP))
            for k in range(DT):
                if k >= 2:
                    act.wait_ge(summed, k - 1)
                act.activation(sq[:, k % 2], work[:, k], ACT.Square).then_inc(squared, 1)
            split(0, 1)
            act.wait_ge(sum_mm, 1)
            act.activation(flat(rstd), bank(4), ACT.Sqrt, bias=S["eps"][:, 0:1], scale=1.0 / D).then_inc(rooted, 1)
            finish(0, 0)
            with act.Fori(1, FT // 2) as j:
                split(j, 0)
                finish(j - 1, 1)
                split(j, 1)
                finish(j, 0)
            for i in range(4):
                split_down(0, i, DOWN[i][1])
            finish(FT // 2 - 1, 1)
            for i in range(4, 8):
                split_down(0, i, DOWN[i % ND][1])
            for s in range(8, 2 * ND):
                split_down(0, s, DOWN[s % ND][1])
            finish_down(0, 0)
            with act.Fori(1, DT // 2) as j:
                for s in range(4):
                    split_down(j, s, DOWN[s % ND][1])
                finish_down(j - 1, 1)
                for s in range(4, 2 * ND):
                    split_down(j, s, DOWN[s % ND][1])
                finish_down(j, 0)
            finish_down(DT // 2 - 1, 1)
            act.wait_ge(sum_mm, 2)
            act.activation(flat(rstd), bank(0), ACT.Sqrt, bias=S["eps"][:, 0:1], scale=1.0 / D).then_inc(rooted, 1)

        @block.vector
        def _(dve):
            own = Chain(dve, dchain)

            def take(k):
                dve.wait_ge(xhi, k + 1)
                dve.scalar_tensor_tensor(xn["lo"][:, k], work[:, k], vec(pre, k), xn["hi"][:, k].bitcast(F32), ALU.mult, ALU.subtract).then_inc(xlo, 1)

            def split(j, r, qs=range(UP)):
                for q in qs:
                    dve.wait_ge(whi, (2 * j + r) * UP + q + 1)
                    dve.tensor_tensor(w["lo"][:, q], raw[:, q], w["hi"][:, q].bitcast(F32), ALU.subtract).then_inc(wlo, 1)

            for k in range(KS):
                take(k)
            split(0, 0, [0])
            for k in range(KS, DT):
                take(k)
            split(0, 0, range(1, UP))
            dve.wait_ge(squared, 2)
            dve.tensor_tensor(ssum, sq[:, 0], sq[:, 1], ALU.add).then_inc(summed, 2)
            dve.wait_ge(summed, 2)
            for k in range(2, DT):
                dve.wait_ge(squared, k + 1)
                dve.tensor_tensor(ssum, ssum, sq[:, k % 2], ALU.add).then_inc(summed, 1)
                dve.wait_ge(summed, k + 1)
            def finish(j, r):
                dve.wait_ge(used, (2 * j + r) * UP + 2)
                dve.tensor_tensor(flat(work[:, r]), bank(4 * r), flat(rstd), ALU.mult).then_inc(gscaled, 1)
                dve.wait_ge(used, (2 * j + r + 1) * UP)
                if not (isinstance(j, int) and j == 0):
                    dve.wait_ge(hlo, 2 * j + r - 1)
                dve.tensor_tensor(flat(work[:, 2 + r]), bank(4 * r + 2), flat(rstd), ALU.mult).then_inc(upped, 1)
                dve.wait_ge(silu_done, 2 * j + r + 1)
                dve.wait_ge(upped, 2 * j + r + 1)
                dve.tensor_tensor(work[:, 2 + r], work[:, 2 + r], work[:, r], ALU.mult).then_inc(prod_done, 1)
                dve.wait_ge(hhi, 2 * j + r + 1)
                dve.tensor_tensor(hid["lo"][:, bass.ds(2 * j + r, 1)], work[:, 2 + r:3 + r],
                                  hid["hi"][:, bass.ds(2 * j + r, 1)].bitcast(F32), ALU.subtract).then_inc(hlo, 1)

            def split_down(j, s, n):
                dve.wait_ge(whi, N_UP + 2 * ND * j + s + 1)
                dve.tensor_tensor(w["lo"][:, s % 4, 0:n], raw[:, s % 4, 0:n], w["hi"][:, s % 4, 0:n].bitcast(F32), ALU.subtract).then_inc(wlo, 1)

            def finish_down(j, r):
                dve.wait_ge(ysq, 2 * j + r + 1)
                if isinstance(j, int) and 2 * j + r == 0:
                    dve.tensor_copy(ssum, sq[:, 0]).then_inc(yadd, 1)
                else:
                    dve.wait_ge(yadd, 2 * j + r)
                    dve.tensor_tensor(ssum, ssum, sq[:, r], ALU.add).then_inc(yadd, 1)

            split(0, 1)
            dve.wait_ge(rooted, 1)
            own.do(dve.reciprocal(rstd, rstd))
            finish(0, 0)
            with dve.Fori(1, FT // 2) as j:
                split(j, 0)
                finish(j - 1, 1)
                split(j, 1)
                finish(j, 0)
            for s in range(4):
                split_down(0, s, DOWN[s][1])
            finish(FT // 2 - 1, 1)
            for s in range(4, 2 * ND):
                split_down(0, s, DOWN[s % ND][1])
            finish_down(0, 0)
            with dve.Fori(1, DT // 2) as j:
                for s in range(4):
                    split_down(j, s, DOWN[s % ND][1])
                finish_down(j - 1, 1)
                for s in range(4, 2 * ND):
                    split_down(j, s, DOWN[s % ND][1])
                finish_down(j, 0)
            finish_down(DT // 2 - 1, 1)
            dve.wait_ge(rooted, 2)
            own.do(dve.reciprocal(rstd, rstd))
            dve.wait_ge(y_done, DT)
            dve.wait_ge(back_in, 16)
            for k in range(DT):
                dve.scalar_tensor_tensor(work[:, k], work[:, k], vec(post, k), rstd, ALU.mult, ALU.mult).then_inc(normed, 1)
                if k % 2:
                    dve.wait_ge(normed, k + 1)
                    dve.tensor_tensor(work[:, k], work[:, k], back[:, k], ALU.add).then_inc(added_v, 1)

        @block.tensor
        def _(pe):
            def sum_features(bank0):
                for b in range(2):
                    ins = pe.matmul(ps[:, bank0 + b, 0:NN], S["ones"][:, :], ssum[:, b * NN:(b + 1) * NN], start=True, stop=True)
                ins.then_inc(sum_mm, 1)

            def slab(slot, n, act_hi, act_lo, bank0, first, last):
                for k in range(n):
                    for wt, xt, f, l in (("hi", act_hi, first and k == 0, False), ("hi", act_lo, False, False),
                                         ("lo", act_hi, False, last and k == n - 1)):
                        for b in range(2):
                            ins = pe.matmul(ps[:, bank0 + b, 0:NN], w[wt][:, slot, k], xt[k][:, b * NN:(b + 1) * NN], start=f, stop=l)
                return ins

            def up(j, first=False):
                for r in range(2):
                    if not first:
                        pe.wait_ge(prod_done, 2 * j + r - 1)
                    elif r == 1:
                        pe.wait_ge(summed, DT)
                        sum_features(4)
                        pe.wait_ge(rooted, 1)
                    for q in range(UP):
                        if first and r == 0:
                            pe.wait_ge(xlo, DT if q else KS)
                        pe.wait_ge(wlo, (2 * j + r) * UP + q + 1)
                        ks = [(q % 2) * KS + k for k in range(KS)]
                        slab(q, KS, [xn["hi"][:, k] for k in ks], [xn["lo"][:, k] for k in ks],
                             4 * r + 2 * (q // 2), q % 2 == 0, q % 2 == 1).then_inc(used, 1)

            def down(j, first=False):
                for r in range(2):
                    if first:
                        pe.wait_ge(prod_done, FT - 1 + r)
                    else:
                        pe.wait_ge(ysq, 2 * j + r - 1)
                    for i, (k, n) in enumerate(DOWN):
                        s = r * ND + i
                        if first:
                            pe.wait_ge(hlo, k + n)
                        pe.wait_ge(wlo, N_UP + 2 * ND * j + s + 1)
                        slab(s % 4, n, [hid["hi"][:, k + x] for x in range(n)], [hid["lo"][:, k + x] for x in range(n)],
                             4 * r, i == 0, i == ND - 1).then_inc(used, 1)

            up(0, True)
            with pe.Fori(1, FT // 2) as j:
                up(j)
            down(0, True)
            with pe.Fori(1, DT // 2) as j:
                down(j)
            pe.wait_ge(yadd, DT)
            pe.wait_ge(ysq, DT)
            sum_features(0)


def in_projection(nc, t, S):
    with stage(nc, "ip_") as (ctx, sb, sem):
        ps = S["ps"]
        xn = {h: sb("xn" + h, [P, DT, TOK], F32R) for h in ("hi", "lo")}
        work = sb("work", [P, DT, TOK])
        sq, ssum, rstd = sb("sq", [P, 2, TOK]), sb("ssum", [P, TOK]), sb("rstd", [P, TOK])
        out = sq
        raw = sb("raw", [P, 4, KS, P])
        w = {h: sb("w" + h, [P, 4, KS, P], F32R) for h in ("hi", "lo")}
        x_in = [sem(f"x_in{i}") for i in range(DT // 2)]
        squared, summed, sum_mm, rooted, xhi, xlo, inv = (sem(n) for n in
            ("squared", "summed", "sum_mm", "rooted", "xhi", "xlo", "inv"))
        raw_in = [sem(f"raw_in{q}") for q in range(4)]
        z_out = [sem(f"z_out{q}") for q in range(2)]
        whi, wlo, used, out_a, out_v = (sem(n) for n in ("whi", "wlo", "used", "out_a", "out_v"))
        block = ctx.enter_context(nc.Block())
        w_in_v = t["w_in"].rearrange("(k p) n -> p k n", p=P)
        z_v = t["zT"].rearrange("(m p) t -> p m t", p=P)
        UP = 2
        NJ, NG = Z_TILES // 2, Z_GATES // 2
        vec = lambda k: S["vec"][:, VEC_AT["mix_pre_g"] + k:VEC_AT["mix_pre_g"] + k + 1]
        rows = lambda a, n0, n1: a.rearrange("p (n t) -> p n t", t=NN)[:, n0:n1]
        zero = lambda j: isinstance(j, int) and j == 0

        @block.sync
        def _(sp):
            def take(i):
                sp.dma_start(work[:, 2 * i:2 * i + 2], feature_tiles(t["res1"], 0, TOK)[:, 2 * i:2 * i + 2]).then_inc(x_in[i], 16)

            def load(j, r, qs=range(UP)):
                for q in qs:
                    slot = UP * r + q
                    if not zero(j):
                        sp.wait_ge(wlo, 4 * (j - 1) + slot + 1)
                    sp.dma_start(raw[:, slot], w_in_v[:, q * KS:(q + 1) * KS, bass.ds((2 * j + r) * P, P)]).then_inc(raw_in[slot], 16)

            take(0)
            load(0, 0, [0])
            take(1)
            take(2)
            load(0, 0, [1])
            take(3)
            load(0, 1)
            with sp.Fori(1, NJ) as j:
                load(j, 0)
                load(j, 1)

        @block.gpsimd
        def _(pool):
            def store(j, r, gate):
                if gate:
                    pool.wait_ge(out_a, 2 * (j - NJ + NG) + r + 1)
                else:
                    pool.wait_ge(out_v, 2 * j + r + 1)
                pool.dma_start(z_v[:, bass.ds(2 * j + r, 1)], out[:, r:r + 1]).then_inc(z_out[r], 16)

            with pool.Fori(0, NJ - NG) as j:
                store(j, 0, False)
                store(j, 1, False)
            with pool.Fori(NJ - NG, NJ) as j:
                store(j, 0, True)
                store(j, 1, True)
            for r in range(2):
                pool.wait_ge(z_out[r], 16 * NJ)

        @block.scalar
        def _(act):
            def take(k):
                act.wait_ge(x_in[k // 2], 16)
                act.activation(xn["hi"][:, k], work[:, k], ACT.Identity, scale=vec(k)).then_inc(xhi, 1)

            def split(j, r, qs=range(UP)):
                for q in qs:
                    slot = UP * r + q
                    act.wait_ge(raw_in[slot], 16 * (j + 1))
                    if not zero(j):
                        act.wait_ge(used, 4 * (j - 1) + slot + 1)
                    act.activation(w["hi"][:, slot], raw[:, slot], ACT.Copy).then_inc(whi, 1)

            def gate(j, r):
                act.wait_ge(out_v, 2 * j + r + 1)
                act.activation(out[:, r], out[:, r], ACT.Sigmoid).then_inc(out_a, 1)

            for k in range(KS):
                take(k)
            split(0, 0, [0])
            for k in range(KS, DT):
                take(k)
            split(0, 0, [1])
            for k in range(DT):
                if k >= 2:
                    act.wait_ge(summed, k - 1)
                act.activation(sq[:, k % 2], work[:, k], ACT.Square).then_inc(squared, 1)
            split(0, 1)
            act.wait_ge(sum_mm, 1)
            act.activation(rows(rstd, 0, 4), ps[:, 4:8, 0:NN], ACT.Sqrt, bias=S["eps"][:, 0:1], scale=1.0 / D).then_inc(rooted, 1)
            with act.Fori(1, NJ - NG) as j:
                split(j, 0)
                split(j, 1)
            split(NJ - NG, 0)
            split(NJ - NG, 1)
            gate(NJ - NG, 0)
            with act.Fori(NJ - NG + 1, NJ) as j:
                split(j, 0)
                gate(j - 1, 1)
                split(j, 1)
                gate(j, 0)
            gate(NJ - 1, 1)

        @block.vector
        def _(dve):
            def take(k):
                dve.wait_ge(xhi, k + 1)
                dve.scalar_tensor_tensor(xn["lo"][:, k], work[:, k], vec(k), xn["hi"][:, k].bitcast(F32), ALU.mult, ALU.subtract).then_inc(xlo, 1)

            def split(j, r, qs=range(UP)):
                for q in qs:
                    slot = UP * r + q
                    dve.wait_ge(whi, 4 * j + slot + 1)
                    dve.tensor_tensor(w["lo"][:, slot], raw[:, slot], w["hi"][:, slot].bitcast(F32), ALU.subtract).then_inc(wlo, 1)

            def finish(j, r):
                dve.wait_ge(used, (2 * j + r + 1) * UP)
                if not zero(j):
                    dve.wait_ge(z_out[r], 16 * j)
                dve.tensor_tensor(rows(out[:, r], 0, 4), ps[:, 4 * r:4 * r + 4, 0:NN], rows(rstd, 0, 4), ALU.mult).then_inc(out_v, 1)

            for k in range(KS):
                take(k)
            split(0, 0, [0])
            for k in range(KS, DT):
                take(k)
            split(0, 0, [1])
            dve.wait_ge(squared, 2)
            dve.tensor_tensor(ssum[:, :], sq[:, 0], sq[:, 1], ALU.add).then_inc(summed, 2)
            dve.wait_ge(summed, 2)
            for k in range(2, DT):
                dve.wait_ge(squared, k + 1)
                dve.tensor_tensor(ssum[:, :], ssum[:, :], sq[:, k % 2], ALU.add).then_inc(summed, 1)
                dve.wait_ge(summed, k + 1)
            split(0, 1)
            dve.wait_ge(rooted, 1)
            dve.reciprocal(rstd[:, :], rstd[:, :]).then_inc(inv, 1)
            dve.wait_ge(inv, 1)
            finish(0, 0)
            with dve.Fori(1, NJ) as j:
                split(j, 0)
                finish(j - 1, 1)
                split(j, 1)
                finish(j, 0)
            finish(NJ - 1, 1)

        @block.tensor
        def _(pe):
            def tile(j, first=False):
                for r in range(2):
                    if not first:
                        pe.wait_ge(out_v, 2 * j + r - 1)
                    elif r == 1:
                        pe.wait_ge(summed, DT)
                        for b in range(4):
                            ins = pe.matmul(ps[:, 4 + b, 0:NN], S["ones"][:, :], ssum[:, b * NN:(b + 1) * NN], start=True, stop=True)
                        ins.then_inc(sum_mm, 1)
                        pe.wait_ge(rooted, 1)
                    for q in range(UP):
                        slot = UP * r + q
                        pe.wait_ge(wlo, 4 * j + slot + 1)
                        for k in range(KS):
                            x = q * KS + k
                            if first and r == 0:
                                pe.wait_ge(xlo, x + 1)
                            for wt, xt, f, l in (("hi", "hi", x == 0, False), ("hi", "lo", False, False), ("lo", "hi", False, x == DT - 1)):
                                for b in range(4):
                                    ins = pe.matmul(ps[:, 4 * r + b, 0:NN], w[wt][:, slot, k], xn[xt][:, x, b * NN:(b + 1) * NN], start=f, stop=l)
                        ins.then_inc(used, 1)

            tile(0, True)
            with pe.Fori(1, NJ) as j:
                tile(j)


def out_projection_half(nc, t, S, tag, half):
    t0, t1 = half * HALF, (half + 1) * HALF
    with stage(nc, tag) as (ctx, sb, sem):
        ps = S["ps"]
        o_raw = sb("o_raw", [P, 2, KS, HALF])
        o = {h: sb("o" + h, [P, 2, KS, HALF], F32R) for h in ("hi", "lo")}
        m = {h: sb("m" + h, [P, DT, HALF], F32R) for h in ("hi", "lo")}
        y = sb("y", [P, DT, HALF])
        gate = sb("gate", [P, 2, 2, HALF])
        prod = sb("prod", [P, 2, 2, HALF])
        tmp = sb("tmp", [P, 4, HALF])
        sq, ssum, rstd = tmp[:, 0:2], tmp[:, 2], tmp[:, 3]
        raw = sb("raw", [P, 4, KS, P])
        w = {h: sb("w" + h, [P, 4, KS, P], F32R) for h in ("hi", "lo")}
        raw_in = [sem(f"raw_in{q}") for q in range(4)]
        gate_in = [sem(f"gate_in{q}") for q in range(2)]
        o_in = [sem(f"o_in{q}") for q in range(2)]
        back_in, added_v, added_p = (sem(n) for n in ("back_in", "added_v", "added_p"))
        back = o_raw[:, :, :, :].rearrange("p i k t -> p (i k) t")
        ohi, olo, whi, wlo, used, gated, merged, mhi, mlo, y_done, ysq, yadd, sum_mm, rooted, inv, normed, stored = (sem(n) for n in
            ("ohi", "olo", "whi", "wlo", "used", "gated", "merged", "mhi", "mlo", "y_done", "ysq", "yadd", "sum_mm", "rooted", "inv", "normed", "stored"))
        block = ctx.enter_context(nc.Block())
        w_att = t["w_o_att"].rearrange("(k p) n -> p k n", p=P)
        w_rw = t["w_o_rwkv"].rearrange("(k p) n -> p k n", p=P)
        w_out = t["w_out"].rearrange("(k p) n -> p k n", p=P)
        z_v = t["zT"].rearrange("(m p) t -> p m t", p=P)
        vec = lambda k: S["vec"][:, VEC_AT["mix_post_g"] + k:VEC_AT["mix_post_g"] + k + 1]
        flat = lambda a: a.rearrange("p (n t) -> p n t", n=2)
        bank = lambda b: ps[:, b:b + 2, 0:NN]
        G0 = Z_TILES - Z_GATES

        @block.sync
        def _(sp):
            for i, src in enumerate(("attT", "rwT")):
                sp.dma_start(o_raw[:, i], feature_tiles(t[src], t0, t1)).then_inc(o_in[i], 16)
            for s in range(4 * DT):
                u, q = s % (2 * DT) // 2, s % 2
                if s >= 4:
                    sp.wait_ge(wlo, s - 3)
                cols = slice(u * P, (u + 1) * P)
                src = (w_att[:, :, cols], w_rw[:, :, cols])[q] if s < 2 * DT else w_out[:, q * KS:(q + 1) * KS, cols]
                sp.dma_start(raw[:, s % 4], src).then_inc(raw_in[s % 4], 16)
            sp.wait_ge(olo, 2 * KS)
            sp.dma_start(back, feature_tiles(t["res1"], t0, t1)).then_inc(back_in, 16)
            for k in range(DT):
                sp.wait_ge((added_p, added_v)[k % 2], k // 2 + 1)
                sp.dma_start(feature_tiles(t["res2"], t0, t1)[:, k], y[:, k]).then_inc(stored, 16)
            sp.wait_ge(stored, 16 * DT)

        @block.gpsimd
        def _(pool):
            for u in range(DT):
                if u >= 2:
                    pool.wait_ge(merged, u - 1)
                pool.dma_start(gate[:, u % 2], z_v[:, G0 + u:Z_TILES:DT, t0:t1]).then_inc(gate_in[u % 2], 16)
            pool.wait_ge(back_in, 16)
            for k in range(0, DT, 2):
                pool.wait_ge(normed, k + 1)
                pool.tensor_tensor(y[:, k], y[:, k], back[:, k], ALU.add).then_inc(added_p, 1)

        @block.scalar
        def _(act):
            def take(i):
                for k in range(KS):
                    act.wait_ge(o_in[i], 16)
                    act.activation(o["hi"][:, i, k], o_raw[:, i, k], ACT.Copy).then_inc(ohi, 1)

            def split(s):
                act.wait_ge(raw_in[s % 4], 16 * (s // 4 + 1))
                if s >= 4:
                    act.wait_ge(used, s - 3)
                act.activation(w["hi"][:, s % 4], raw[:, s % 4], ACT.Copy).then_inc(whi, 1)

            for s in range(2):
                take(s)
                split(s)
            for u in range(DT):
                for s in (2 * u + 2, 2 * u + 3):
                    split(s)
                act.wait_ge(merged, u + 1)
                act.activation(m["hi"][:, u], prod[:, u % 2, 0], ACT.Copy).then_inc(mhi, 1)
            for u in range(DT):
                if u < DT - 1:
                    for s in (2 * (DT + u) + 2, 2 * (DT + u) + 3):
                        split(s)
                act.wait_ge(used, 2 * (DT + u + 1))
                act.activation(flat(y[:, u]), bank(4 * (u % 2)), ACT.Copy).then_inc(y_done, 1)
                if u >= 2:
                    act.wait_ge(yadd, u - 1)
                act.activation(flat(sq[:, u % 2]), bank(4 * (u % 2)), ACT.Square).then_inc(ysq, 1)
            act.wait_ge(sum_mm, 1)
            act.activation(flat(rstd), bank(0), ACT.Sqrt, bias=S["eps"][:, 0:1], scale=1.0 / D).then_inc(rooted, 1)

        @block.vector
        def _(dve):
            def take(i):
                for k in range(KS):
                    dve.wait_ge(ohi, KS * i + k + 1)
                    dve.tensor_tensor(o["lo"][:, i, k], o_raw[:, i, k], o["hi"][:, i, k].bitcast(F32), ALU.subtract).then_inc(olo, 1)

            def split(s):
                dve.wait_ge(whi, s + 1)
                dve.tensor_tensor(w["lo"][:, s % 4], raw[:, s % 4], w["hi"][:, s % 4].bitcast(F32), ALU.subtract).then_inc(wlo, 1)

            for s in range(2):
                take(s)
                split(s)
            for u in range(DT):
                for s in (2 * u + 2, 2 * u + 3):
                    split(s)
                dve.wait_ge(used, 2 * u + 2)
                dve.wait_ge(gate_in[u % 2], 16 * (u // 2 + 1))
                if u >= 2:
                    dve.wait_ge(mlo, u - 1)
                for i in range(2):
                    dve.tensor_tensor(flat(prod[:, u % 2, i]), flat(gate[:, u % 2, i]), bank(4 * (u % 2) + 2 * i), ALU.mult).then_inc(gated, 1)
                dve.wait_ge(gated, 2 * u + 2)
                dve.tensor_tensor(prod[:, u % 2, 0], prod[:, u % 2, 0], prod[:, u % 2, 1], ALU.add).then_inc(merged, 1)
                dve.wait_ge(mhi, u + 1)
                dve.tensor_tensor(m["lo"][:, u], prod[:, u % 2, 0], m["hi"][:, u].bitcast(F32), ALU.subtract).then_inc(mlo, 1)
            for u in range(DT):
                if u < DT - 1:
                    for s in (2 * (DT + u) + 2, 2 * (DT + u) + 3):
                        split(s)
                dve.wait_ge(ysq, u + 1)
                if u == 0:
                    dve.tensor_copy(ssum, sq[:, 0]).then_inc(yadd, 1)
                else:
                    dve.wait_ge(yadd, u)
                    dve.tensor_tensor(ssum, ssum, sq[:, u % 2], ALU.add).then_inc(yadd, 1)
            dve.wait_ge(rooted, 1)
            dve.reciprocal(rstd, rstd).then_inc(inv, 1)
            dve.wait_ge(inv, 1)
            dve.wait_ge(back_in, 16)
            for k in range(DT):
                dve.scalar_tensor_tensor(y[:, k], y[:, k], vec(k), rstd, ALU.mult, ALU.mult).then_inc(normed, 1)
                if k % 2:
                    dve.wait_ge(normed, k + 1)
                    dve.tensor_tensor(y[:, k], y[:, k], back[:, k], ALU.add).then_inc(added_v, 1)

        @block.tensor
        def _(pe):
            def slab(slot, xt, bank0, first, last):
                for k in range(KS):
                    for wt, h, f, l in (("hi", "hi", first and k == 0, False), ("hi", "lo", False, False), ("lo", "hi", False, last and k == KS - 1)):
                        for b in range(2):
                            ins = pe.matmul(ps[:, bank0 + b, 0:NN], w[wt][:, slot, k], xt(h, k)[:, b * NN:(b + 1) * NN], start=f, stop=l)
                ins.then_inc(used, 1)

            for u in range(DT):
                if u >= 2:
                    pe.wait_ge(gated, 2 * (u - 1))
                for i in range(2):
                    if u == 0:
                        pe.wait_ge(olo, KS * (i + 1))
                    pe.wait_ge(wlo, 2 * u + i + 1)
                    slab((2 * u + i) % 4, lambda h, k: o[h][:, i, k], 4 * (u % 2) + 2 * i, True, True)
            for u in range(DT):
                if u < 2:
                    pe.wait_ge(gated, 2 * (DT - 1 + u))
                else:
                    pe.wait_ge(ysq, u - 1)
                for i in range(2):
                    s = 2 * (DT + u) + i
                    if u == 0:
                        pe.wait_ge(mlo, 4 * i + 4)
                    pe.wait_ge(wlo, s + 1)
                    slab(s % 4, lambda h, k: m[h][:, 4 * i + k], 4 * (u % 2), i == 0, i == 1)
            pe.wait_ge(yadd, DT)
            for b in range(2):
                ins = pe.matmul(ps[:, b, 0:NN], S["ones"][:, :], ssum[:, b * NN:(b + 1) * NN], start=True, stop=True)
            ins.then_inc(sum_mm, 1)


SPIN_P, SPIN_S, SPIN_R = 2, 1, 3


def spin(pe, free, S, rhs, n):
    for _ in range(n):
        pe.matmul(free, S["ones"][:, :], rhs, start=True, stop=True)


def prompt_attention(nc, t, S):
    with stage(nc, "pa_") as (ctx, sb, sem):
        ps = S["ps"]
        qk = sb("qk", [P, 8, TOK])
        vf = sb("vf", [P, HEADS, TOK])
        ktok, vtok = sb("ktok", [P, TOK // P, HEADS * P]), sb("vtok", [P, TOK // P, HEADS * P])
        cos, sin, rot = sb("cos", [P, TOK]), sb("sin", [P, TOK]), sb("rot", [P, P])
        turn = sb("turn", [P, TOK])
        mask = sb("mask", [1, P + CHUNK])
        lamr, lamc = sb("lamr", [1, 4, 64]), sb("lamc", [1, 8])
        ex = sb("ex", [P, 2, SEQ])
        aw = sb("aw", [P, SEQ])
        awT = sb("awT", [P, SEQ // P, P])
        stat = sb("stat", [P, 8])
        z_in = [sem(f"z_in{i}") for i in range(4)]
        c_in, turned, cosed, roped, sined = (sem(n) for n in ("c_in", "turned", "cosed", "roped", "sined"))
        moved, moved_a, stored, lam_s, lam_e, lam_mm, chain = (sem(n) for n in ("moved", "moved_a", "stored", "lam_s", "lam_e", "lam_mm", "chain"))
        scored, maxed, exped, mixed, flipped, flipped_out, valued, out_done = (sem(n) for n in
            ("scored", "maxed", "exped", "mixed", "flipped", "flipped_out", "valued", "out_done"))
        osq, osum, oroot, onorm = (sem(n) for n in ("osq", "osum", "oroot", "onorm"))
        block = ctx.enter_context(nc.Block())
        NK = SEQ // P
        units = [(h, b) for h in range(HEADS) for b in range(NK)]
        z_v = t["zT"].rearrange("(m p) t -> p m t", p=P)
        NT = TOK // P
        flips = [("v", m) for m in range(NT)] + [("k", m) for m in range(NT)]
        third = lambda a: a.rearrange("p (n t) -> p n t", n=3)
        three = lambda b: ps[:, b:b + 3, 0:TOK // 3]
        halves = [(0, 512), (512, 1024)]
        cols = lambda b: [(a, min(e, (b + 1) * P)) for a, e in halves if a < (b + 1) * P]

        @block.sync
        def _(sp):
            for k, n in (("q1", 0), ("k1", 1), ("q2", 2), ("k2", 3)):
                sp.dma_start(lamr[:, n], t["att_lambda_" + k]).then_inc(c_in, 16)
            for dst, n in ((rot, "c_rot"), (cos, "c_cos"), (sin, "c_sin"), (mask, "c_mask")):
                sp.dma_start(dst[:, :], t[n]).then_inc(c_in, 16)
            for i in range(4):
                dst = vf[:, :, :] if i == 1 else qk[:, 4 * (i // 2):4 * (i // 2) + 4]
                if i < 3:
                    sp.dma_start(dst, z_v[:, {0: ZQ, 1: ZV, 2: ZK}[i]:{0: ZQ, 1: ZV, 2: ZK}[i] + 4]).then_inc(z_in[i], 16)
            sp.wait_ge(moved, NT)
            sp.dma_start(t["new_v_prompt"].rearrange("(m p) c -> p m c", p=P), vtok[:, 0:NK]).then_inc(stored, 16)
            sp.dma_start(t["new_v_sample"], vtok[:, NK]).then_inc(stored, 16)
            sp.wait_ge(moved, 2 * NT)
            sp.dma_start(t["new_k_prompt"].rearrange("(m p) c -> p m c", p=P), ktok[:, 0:NK]).then_inc(stored, 16)
            sp.dma_start(t["new_k_sample"], ktok[:, NK]).then_inc(stored, 16)
            sp.wait_ge(onorm, 2 * HEADS)
            sp.dma_start(feature_tiles(t["attT"], 0, SEQ), vf[:, :, 0:SEQ]).then_inc(stored, 16)
            sp.wait_ge(stored, 16 * 5)

        @block.gpsimd
        def _(pool):
            pool.wait_ge(c_in, 16 * 8)
            for i in range(8):
                pool.wait_ge(turned, i + 1)
                pool.tensor_tensor(qk[:, i], qk[:, i], cos[:, :], ALU.mult).then_inc(cosed, 1)

        @block.scalar
        def _(act):
            act.wait_ge(lam_s, 2)
            act.activation(lamc[:, 2:4], lamc[:, 0:2], ACT.Exp).then_inc(lam_e, 1)
            for n, (h, b) in enumerate(units):
                N = (b + 1) * P
                for m in range(2):
                    act.wait_ge(maxed, 2 * n + m + 1)
                    if n >= 1:
                        act.wait_ge(mixed, 2 * n)
                    act.activation(ex[:, m, 0:N], ps[:, 2 * m:2 * m + 2, :].rearrange("p b c -> p (b c)")[:, 0:N], ACT.Exp,
                                   bias=stat[:, 4 * m + 1:4 * m + 2], scale=SCALE, accum_out=stat[:, 4 * m + 2:4 * m + 3]).then_inc(exped, 1)
                for g in range(len(cols(b))):
                    act.wait_ge(flipped, sum(len(cols(bb)) for _, bb in units[:n]) + g + 1)
                    if n >= 1:
                        act.wait_ge(valued, n)
                    k = min(4, b + 1 - 4 * g)
                    act.activation(awT[:, 4 * g:4 * g + k], ps[:, 4 + g, 0:k * P].rearrange("p (k q) -> p k q", k=k), ACT.Copy).then_inc(flipped_out, 1)
            for h in range(HEADS):
                if h == 0:
                    act.wait_ge(out_done, len(units))
                else:
                    act.wait_ge(oroot, h)
                    act.wait_ge(osum, h)
                act.activation(turn[:, 0:SEQ], vf[:, h, 0:SEQ], ACT.Square).then_inc(osq, 1)
                act.wait_ge(osum, h + 1)
                if h >= 1:
                    act.wait_ge(onorm, 2 * h)
                act.activation(sin[:, 0:SEQ], ps[:, 0:2, :].rearrange("p b c -> p (b c)"), ACT.Sqrt, bias=S["eps"][:, 0:1], scale=1.0 / P).then_inc(oroot, 1)

        def take_out(dve, n):
            h, b = units[n]
            dve.wait_ge(valued, n + 1)
            dve.tensor_copy(vf[:, h, b * P:(b + 1) * P], ps[:, 6 + n % 2, 0:P]).then_inc(out_done, 1)

        @block.vector
        def _(dve):
            own = Chain(dve, chain)
            dve.wait_ge(c_in, 16 * 8)
            for i in range(2):
                dve.tensor_tensor_reduce(out=lamr[:, 2 * i], in0=lamr[:, 2 * i], in1=lamr[:, 2 * i + 1], scale=1.0, scalar=0.0,
                                         op0=ALU.mult, op1=ALU.add, accum_out=lamc[:, i:i + 1]).then_inc(lam_s, 1)
            dve.wait_ge(lam_e, 1)
            own.do(dve.tensor_tensor(lamc[:, 4:5], lamc[:, 3:4], lamc[:, 2:3], ALU.subtract))
            own.do(dve.tensor_scalar(lamc[:, 5:6], lamc[:, 4:5], -LAM_INIT, None, ALU.add))
            dve.tensor_copy(lamc[:, 6:7], lamc[:, 5:6]).then_inc(lam_s, 1)
            dve.wait_ge(lam_mm, 1)
            own.do(dve.tensor_copy(S["neg_lam"][:, :], ps[:, 7, 0:1]))

            def rope(i):
                dve.wait_ge(turned, i + 1)
                if i >= 1:
                    dve.wait_ge(roped, i)
                dve.tensor_tensor(third(turn[:, :]), three(3 * (i % 2)), third(sin[:, :]), ALU.mult).then_inc(sined, 1)
                dve.wait_ge(sined, i + 1)
                dve.wait_ge(cosed, i + 1)
                dve.tensor_tensor(qk[:, i], qk[:, i], turn[:, :], ALU.add).then_inc(roped, 1)

            for i in range(8):
                rope(i)
            dve.wait_ge(roped, 8)
            dve.tensor_copy(S["qk_sample"][:, :, :], qk[:, :, SEQ:TOK]).then_inc(chain, 1)
            own.n += 1
            for n, (what, m) in enumerate(flips):
                dve.wait_ge(moved_a, n + 1)
                dve.tensor_copy((vtok if what == "v" else ktok)[:, m], ps[:, 6 + n % 2, :]).then_inc(moved, 1)
            for n, (h, b) in enumerate(units):
                N = (b + 1) * P
                for m in range(2):
                    dve.wait_ge(scored, n + 1)
                    own.do(dve.tensor_reduce(stat[:, 4 * m:4 * m + 1], ps[:, 2 * m:2 * m + 2, :].rearrange("p b c -> p (b c)")[:, 0:N], AX, ALU.max, negate=True))
                    dve.tensor_scalar(stat[:, 4 * m + 1:4 * m + 2], stat[:, 4 * m:4 * m + 1], SCALE, None, ALU.mult).then_inc(maxed, 1)
                for m in range(2):
                    dve.wait_ge(exped, 2 * n + m + 1)
                    own.do(dve.reciprocal(stat[:, 4 * m + 3:4 * m + 4], stat[:, 4 * m + 2:4 * m + 3]))
                    if m == 0:
                        if n >= 1:
                            dve.wait_ge(flipped, sum(len(cols(bb)) for _, bb in units[:n]))
                        dve.tensor_scalar(aw[:, 0:N], ex[:, 0, 0:N], stat[:, 3:4], None, ALU.mult).then_inc(mixed, 1)
                    else:
                        own.do(dve.tensor_tensor(stat[:, 7:8], stat[:, 7:8], S["neg_lam"][:, :], ALU.mult))
                        dve.wait_ge(mixed, 2 * n + 1)
                        dve.scalar_tensor_tensor(aw[:, 0:N], ex[:, 1, 0:N], stat[:, 7:8], aw[:, 0:N], ALU.mult, ALU.add).then_inc(mixed, 1)
                if n >= 1:
                    take_out(dve, n - 1)
            take_out(dve, len(units) - 1)
            for h in range(HEADS):
                dve.wait_ge(oroot, h + 1)
                own.do(dve.reciprocal(sin[:, 0:SEQ], sin[:, 0:SEQ]))
                dve.scalar_tensor_tensor(vf[:, h, 0:SEQ], vf[:, h, 0:SEQ], S["vec"][:, NVEC - 1:NVEC], sin[:, 0:SEQ], ALU.mult, ALU.mult).then_inc(onorm, 1)
                dve.wait_ge(onorm, 2 * h + 1)
                dve.tensor_scalar(vf[:, h, 0:SEQ], vf[:, h, 0:SEQ], 1.0 - LAM_INIT, None, ALU.mult).then_inc(onorm, 1)

        @block.tensor
        def _(pe):
            pe.wait_ge(c_in, 16 * 8)
            pe.wait_ge(lam_s, 3)
            pe.matmul(ps[:, 7, 0:1], S["ones"][0:1, :], lamc[:, 6:7], start=True, stop=True).then_inc(lam_mm, 1)
            for i in range(8):
                pe.wait_ge(z_in[0 if i < 4 else 2], 16)
                if i >= 2:
                    pe.wait_ge(sined, i - 1)
                for b in range(3):
                    ins = pe.matmul(ps[:, 3 * (i % 2) + b, 0:TOK // 3], rot[:, :], qk[:, i, b * (TOK // 3):(b + 1) * (TOK // 3)], start=True, stop=True)
                ins.then_inc(turned, 1)
            pe.wait_ge(z_in[1], 16)
            pe.wait_ge(roped, 8)
            pe.wait_ge(chain, 3)
            for n, (what, m) in enumerate(flips):
                if n >= 2:
                    pe.wait_ge(moved, n - 1)
                for h in range(HEADS):
                    src = vf[:, h, m * P:(m + 1) * P] if what == "v" else qk[:, 4 + h, m * P:(m + 1) * P]
                    ins = pe.transpose(ps[:, 6 + n % 2, h * P:(h + 1) * P], src, S["ident"][:, :])
                ins.then_inc(moved_a, 1)

            def scores(n):
                h, b = units[n]
                N = (b + 1) * P
                if n >= 1:
                    pe.wait_ge(exped, 2 * n)
                for i, (a, e) in enumerate(cols(b)):
                    last = e == N
                    for m in range(2):
                        rows = slice(64 * m, 64 * m + 64)
                        pe.matmul(ps[:, 2 * m + i, 0:e - a], qk[rows, h, b * P:(b + 1) * P], qk[rows, 4 + h, a:e], start=True, stop=not last)
                    if last:
                        for m in range(2):
                            ins = pe.matmul(ps[:, 2 * m + i, e - a - CHUNK:e - a], mask[:, 0:P], mask[:, P:P + CHUNK], start=False, stop=True)
                ins.then_inc(scored, 1)

            def flip(n):
                h, b = units[n]
                spin(pe, ps[:, 4, 0:256], S, qk[:, 0, 0:256], SPIN_P)
                pe.wait_ge(mixed, 2 * n + 2)
                for g in range(len(cols(b))):
                    if n >= 1:
                        pe.wait_ge(flipped_out, sum(len(cols(bb)) for _, bb in units[:n]))
                    for k in range(min(4, b + 1 - 4 * g)):
                        ins = pe.transpose(ps[:, 4 + g, k * P:(k + 1) * P], aw[:, (4 * g + k) * P:(4 * g + k + 1) * P], S["ident"][:, :])
                    ins.then_inc(flipped, 1)

            def values(n):
                h, b = units[n]
                if n >= 2:
                    pe.wait_ge(out_done, n - 1)
                for k in range(b + 1):
                    if k % 4 == 0:
                        pe.wait_ge(flipped_out, sum(len(cols(bb)) for _, bb in units[:n]) + k // 4 + 1)
                    ins = pe.matmul(ps[:, 6 + n % 2, 0:P], vtok[:, k, h * P:(h + 1) * P], awT[:, k], start=k == 0, stop=k == b)
                ins.then_inc(valued, 1)

            pe.wait_ge(moved, 2 * NT)
            scores(0)
            for n in range(len(units)):
                if n + 1 < len(units):
                    scores(n + 1)
                flip(n)
                values(n)
            for h in range(HEADS):
                pe.wait_ge(osq, h + 1)
                if h >= 1:
                    pe.wait_ge(oroot, h)
                for b in range(2):
                    ins = pe.matmul(ps[:, b, :], S["ones"][:, :], turn[:, b * 512:(b + 1) * 512], start=True, stop=True)
                ins.then_inc(osum, 1)


def sample_attention(nc, t, S):
    with stage(nc, "sa_") as (ctx, sb, sem):
        ps = S["ps"]
        CK = 1024 // P
        NS = 1024 + NQ
        kc, vc = sb("kc", [P, 2, CK, HEADS * P]), sb("vc", [P, 2, CK, HEADS * P])
        vnew = sb("vnew", [NQ, 2, HEADS * P])
        kT = sb("kT", [P, 2, HEADS, CK * P])
        qbd = sb("qbd", [P, 2, HEADS, 2 * NQ])
        knew = sb("knew", [P, 2, HEADS, NQ])
        ex = sb("ex", [P, NS])
        pick, coef, sign = sb("pick", [P, 64]), sb("coef", [P, 64]), sb("sign", [P, 2])
        stat = sb("stat", [P, 8])
        awT = sb("awT", [P, CK + 1, 64])
        av = sb("av", [64, HEADS * P])
        out, sq, root = sb("out", [P, HEADS, P]), sb("sq", [P, HEADS * P]), sb("root", [P, HEADS * P])
        k_in, v_in = [sem(f"k_in{i}") for i in range(2)], [sem(f"v_in{i}") for i in range(2)]
        c_in, qset, flipped, out_a, out_v, scored, maxed, exped, weighed, mixed, mixed_out, valued, out_done, chain = (sem(n) for n in
            ("c_in", "qset", "flipped", "out_a", "out_v", "scored", "maxed", "exped", "weighed", "mixed", "mixed_out", "valued", "out_done", "chain"))
        av_out, turned = sem("av_out"), sem("turned")
        osq, osum, oroot, onorm, stored = (sem(n) for n in ("osq", "osum", "oroot", "onorm", "stored"))
        block = ctx.enter_context(nc.Block())
        k_v = t["cache_att_k"].rearrange("b (p k) c -> b p k c", k=CK)
        v_v = t["cache_att_v"].rearrange("b (p k) c -> b p k c", k=CK)
        vn_v = t["new_v_sample"].rearrange("(b q) c -> b q c", b=NB)
        zero = lambda j: isinstance(j, int) and j == 0
        GROUPS = [(h, g) for h in range(HEADS) for g in range(2)]
        flat3 = ps[:, 0:3, :].rearrange("p b c -> p (b c)")
        after = lambda j, r: (j, 1) if r == 0 else (j + 1, 0)
        one = lambda a: a.rearrange("b p k c -> p (b k) c")

        @block.sync
        def _(sp):
            sp.dma_start(pick[:, :], t["c_pick"]).then_inc(c_in, 16)
            sp.dma_start(sign[:, :], t["c_sign"]).then_inc(c_in, 16)

            def load(j, r):
                if not zero(j):
                    sp.wait_ge(flipped, 8 * (2 * j + r - 1))
                sp.dma_start(kc[:, r], one(k_v[bass.ds(2 * j + r, 1)])).then_inc(k_in[r], 16)
                if not zero(j):
                    sp.wait_ge(valued, 2 * j + r - 1)
                sp.dma_start(vc[:, r], one(v_v[bass.ds(2 * j + r, 1)])).then_inc(v_in[r], 16)
                sp.dma_start(vnew[:, r], vn_v[bass.ds(2 * j + r, 1)].rearrange("b q c -> q (b c)")).then_inc(v_in[r], 16)

            load(0, 0)
            load(0, 1)
            with sp.Fori(1, NB // 2) as j:
                load(j, 0)
                load(j, 1)
            sp.wait_ge(onorm, 2)
            sp.dma_start(feature_tiles(t["attT"], SEQ, TOK), out[:, :, :]).then_inc(stored, 16)
            sp.wait_ge(stored, 16)

        def copy_group(r, g):
            h, half = GROUPS[g]
            return kT[:, r, h, half * 512:half * 512 + 512], ps[:, 3 + g % 2, :]

        @block.scalar
        def _(act):
            def keys(j, r):
                n = 2 * j + r
                for g in range(0, 8, 2):
                    act.wait_ge(flipped, 8 * n + g + 1)
                    if not zero(j):
                        act.wait_ge(scored, n - 1)
                    act.activation(*copy_group(r, g), ACT.Copy).then_inc(out_a, 1)

            def seq(j, r, last=False):
                n = 2 * j + r
                act.wait_ge(maxed, n + 1)
                if not (zero(j) and r == 0):
                    act.wait_ge(mixed, n)
                act.activation(ex[:, :], flat3[:, 0:NS], ACT.Exp, bias=stat[:, 1:2], scale=SCALE, accum_out=stat[:, 2:3]).then_inc(exped, 1)
                if not last:
                    keys(*after(j, r))
                act.wait_ge(valued, n + 1)
                if not (zero(j) and r == 0):
                    act.wait_ge(turned, n)
                act.activation(av[:, :], ps[0:64, 7, :], ACT.Copy).then_inc(av_out, 1)

            keys(0, 0)
            seq(0, 0)
            seq(0, 1)
            with act.Fori(1, NB // 2 - 1) as j:
                seq(j, 0)
                seq(j, 1)
            seq(NB // 2 - 1, 0)
            seq(NB // 2 - 1, 1, True)
            act.wait_ge(out_done, NB)
            act.activation(sq[:, :], out[:, :, :].rearrange("p h t -> p (h t)"), ACT.Square).then_inc(osq, 1)
            act.wait_ge(osum, 1)
            act.activation(root[:, :], ps[:, 0, :], ACT.Sqrt, bias=S["eps"][:, 0:1], scale=1.0 / P).then_inc(oroot, 1)

        @block.vector
        def _(dve):
            dve.memset(qbd[:, :, :, :], 0.0).then_inc(chain, 1)
            dve.wait_ge(c_in, 32)
            dve.tensor_tensor(stat[:, 4:5], sign[:, 1:2], S["neg_lam"][:, :], ALU.mult).then_inc(chain, 1)
            dve.wait_ge(chain, 2)
            dve.tensor_tensor(stat[:, 5:6], stat[:, 4:5], sign[:, 0:1], ALU.add).then_inc(chain, 1)
            dve.wait_ge(chain, 3)

            def keys(j, r):
                n = 2 * j + r
                if not zero(j):
                    dve.wait_ge(scored, n - 1)
                for m in range(2):
                    rows = slice(64 * m, 64 * m + 64)
                    dve.tensor_copy(qbd[rows, r, :, m * NQ:(m + 1) * NQ], S["qk_sample"][rows, 0:HEADS, bass.ds(n * NQ, NQ)]).then_inc(qset, 1)
                dve.tensor_copy(knew[:, r], S["qk_sample"][:, HEADS:8, bass.ds(n * NQ, NQ)]).then_inc(qset, 1)
                for g in range(1, 8, 2):
                    dve.wait_ge(flipped, 8 * n + g + 1)
                    dve.tensor_copy(*copy_group(r, g)).then_inc(out_v, 1)

            def take_out(n):
                dve.wait_ge(turned, n + 1)
                dve.tensor_copy(out[:, :, bass.ds(n * NQ, NQ)], ps[:, 6, 64:128].rearrange("p (h q) -> p h q", h=HEADS)).then_inc(out_done, 1)

            def seq(j, r, last=False):
                n = 2 * j + r
                first = zero(j) and r == 0
                dve.wait_ge(scored, n + 1)
                if not first:
                    dve.wait_ge(exped, n)
                dve.tensor_reduce(stat[:, 0:1], flat3[:, 0:NS], AX, ALU.max, negate=True).then_inc(chain, 1)
                dve.wait_ge(chain, 3 + 3 * n + 1)
                dve.tensor_scalar(stat[:, 1:2], stat[:, 0:1], SCALE, None, ALU.mult).then_inc(maxed, 1)
                if not first:
                    take_out(n - 1)
                if not last:
                    keys(*after(j, r))
                dve.wait_ge(exped, n + 1)
                dve.reciprocal(stat[:, 3:4], stat[:, 2:3]).then_inc(chain, 1)
                dve.wait_ge(chain, 3 + 3 * n + 2)
                dve.tensor_tensor(stat[:, 6:7], stat[:, 3:4], stat[:, 5:6], ALU.mult).then_inc(chain, 1)
                dve.wait_ge(chain, 3 + 3 * n + 3)
                dve.tensor_scalar(coef[:, :], pick[:, :], stat[:, 6:7], None, ALU.mult).then_inc(weighed, 1)
                dve.wait_ge(mixed, n + 1)
                dve.tensor_copy(awT[:, 0:CK], ps[:, 5, :].rearrange("p (k c) -> p k c", k=CK)).then_inc(mixed_out, 1)
                dve.tensor_copy(awT[0:NQ, CK], ps[0:NQ, 6, 0:64]).then_inc(mixed_out, 1)

            keys(0, 0)
            seq(0, 0)
            seq(0, 1)
            with dve.Fori(1, NB // 2 - 1) as j:
                seq(j, 0)
                seq(j, 1)
            seq(NB // 2 - 1, 0)
            seq(NB // 2 - 1, 1, True)
            take_out(NB - 1)
            dve.wait_ge(oroot, 1)
            dve.reciprocal(root[:, :], root[:, :]).then_inc(chain, 1)
            dve.wait_ge(chain, 3 + 3 * NB + 1)
            o = out[:, :, :].rearrange("p h t -> p (h t)")
            dve.scalar_tensor_tensor(o, o, S["vec"][:, NVEC - 1:NVEC], root[:, :], ALU.mult, ALU.mult).then_inc(onorm, 1)
            dve.wait_ge(onorm, 1)
            dve.tensor_scalar(o, o, 1.0 - LAM_INIT, None, ALU.mult).then_inc(onorm, 1)

        @block.tensor
        def _(pe):
            def keys(j, r):
                n = 2 * j + r
                first = zero(j) and r == 0
                pe.wait_ge(k_in[r], 16 * (j + 1))
                for g, (h, half) in enumerate(GROUPS):
                    if g >= 2 or not first:
                        pe.wait_ge(out_v if g % 2 else out_a, 4 * n + g // 2)
                    for k in range(4):
                        ins = pe.transpose(ps[:, 3 + g % 2, k * P:(k + 1) * P], kc[:, r, 4 * half + k, h * P:(h + 1) * P], S["ident"][:, :])
                    ins.then_inc(flipped, 1)

            def turn(n, first):
                pe.wait_ge(av_out, n + 1)
                if not first:
                    pe.wait_ge(out_done, n)
                for h in range(HEADS):
                    ins = pe.matmul(ps[:, 6, 64 + h * NQ:64 + (h + 1) * NQ], av[:, h * P:(h + 1) * P], S["ident"][0:64, h * NQ:(h + 1) * NQ], start=True, stop=True)
                ins.then_inc(turned, 1)

            def seq(j, r, last=False):
                n = 2 * j + r
                first = zero(j) and r == 0
                pe.wait_ge(qset, 3 * n + 3)
                pe.wait_ge(out_a, 4 * n + 4)
                pe.wait_ge(out_v, 4 * n + 4)
                if not first:
                    pe.wait_ge(exped, n)
                for c in range(2):
                    for h in range(HEADS):
                        pe.matmul(ps[32 * h:32 * h + 32, c, :], qbd[:, r, h], kT[:, r, h, c * 512:(c + 1) * 512], start=True, stop=True, tile_position=(0, 32 * h))
                for h in range(HEADS):
                    ins = pe.matmul(ps[32 * h:32 * h + 32, 2, 0:NQ], qbd[:, r, h], knew[:, r, h], start=True, stop=True, tile_position=(0, 32 * h))
                ins.then_inc(scored, 1)
                if not first:
                    turn(n - 1, zero(j))
                if not last:
                    keys(*after(j, r))
                spin(pe, ps[:, 7, 0:256], S, S["qk_sample"][:, 0:2], SPIN_S)
                pe.wait_ge(weighed, n + 1)
                if not first:
                    pe.wait_ge(mixed_out, 2 * n)
                for k in range(CK):
                    pe.matmul(ps[:, 5, k * 64:(k + 1) * 64], ex[:, k * P:(k + 1) * P], coef[:, :], start=True, stop=True)
                pe.matmul(ps[0:NQ, 6, 0:64], ex[:, CK * P:NS], coef[:, :], start=True, stop=True).then_inc(mixed, 1)
                spin(pe, ps[:, 7, 0:256], S, S["qk_sample"][:, 0:2], SPIN_S)
                pe.wait_ge(mixed_out, 2 * n + 2)
                pe.wait_ge(v_in[r], 32 * (j + 1))
                if not first:
                    pe.wait_ge(av_out, n)
                for k in range(CK):
                    pe.matmul(ps[0:64, 7, :], awT[:, k], vc[:, r, k], start=k == 0, stop=False)
                pe.matmul(ps[0:64, 7, :], awT[0:NQ, CK], vnew[:, r], start=False, stop=True).then_inc(valued, 1)

            keys(0, 0)
            seq(0, 0)
            seq(0, 1)
            with pe.Fori(1, NB // 2 - 1) as j:
                seq(j, 0)
                seq(j, 1)
            seq(NB // 2 - 1, 0)
            seq(NB // 2 - 1, 1, True)
            turn(NB - 1, False)
            pe.wait_ge(osq, 1)
            pe.matmul(ps[:, 0, :], S["ones"][:, :], sq[:, :], start=True, stop=True).then_inc(osum, 1)


def rwkv_prepare(nc, t, S, R):
    with stage(nc, "rp_") as (ctx, sb, sem):
        ps = S["ps"]
        lora = sb("lora", [P, 2, TOK])
        diff = sb("diff", [P, 2, TOK])
        sw, aa = sb("sw", [P, RT, TOK]), sb("aa", [P, RT, TOK])
        gg = sb("gg", [P, RT, TOK])
        cum = sb("cum", [P, TOK])
        e = [sb(f"e{i}", [P, TOK]) for i in range(2)]
        starts = sb("starts", [P, TOK])
        wl, g2 = sb("wl", [P, RT * P]), sb("g2", [P, RT * P])
        rows = sb("rows", [NB + 1, ZRT * P])
        shift_cols = sb("shift_cols", [P, ZRT, NB])
        last_cols = sb("last_cols", [P, ZRT, NB + 1])
        tri = [R["r"], R["k"], R["v"]]
        z = lambda i: tri[i // RT][:, i % RT] if i < 3 * RT else lora[:, i - 3 * RT]
        z_in = [sem(f"z_in{i}") for i in range(4)]
        c_in, flip, flipped, diffed, shifted, stored, chain, cols_kept, rows_kept, rows_mm = (sem(n) for n in
            ("c_in", "flip", "flipped", "diffed", "shifted", "stored", "chain", "cols_kept", "rows_kept", "rows_mm"))
        acts, lora_mm, lora_out, sum_mm, sum_out, expd, used, pooled = (sem(n) for n in
            ("acts", "lora_mm", "lora_out", "sum_mm", "sum_out", "expd", "used", "pooled"))
        block = ctx.enter_context(nc.Block())
        z_v = t["zT"].rearrange("(m p) t -> p m t", p=P)
        vec = lambda name, k: S["vec"][:, VEC_AT[name] + k:VEC_AT[name] + k + 1]
        third = lambda a: a.rearrange("p (n t) -> p n t", n=3)
        three = lambda b: ps[:, b:b + 3, 0:TOK // 3]
        C3 = [(b, b * (TOK // 3), (b + 1) * (TOK // 3)) for b in range(3)]
        order = [12, 13] + list(range(12))
        sample = lambda a: a[:, SEQ:TOK].rearrange("p (b q) -> p b q", b=NB)

        @block.sync
        def _(sp):
            sp.dma_start(rows[0:NB, :], t["state_shift"].rearrange("a b c d -> (a b c) d")).then_inc(c_in, 16)
            sp.dma_start(starts[:, :], t["c_starts"]).then_inc(c_in, 16)
            sp.dma_start(R["block"][:, :], t["c_block"]).then_inc(c_in, 16)
            sp.dma_start(wl[0:64, :], t["rwkv_w2"]).then_inc(c_in, 16)
            sp.dma_start(wl[64:P, :], t["rwkv_a2"]).then_inc(c_in, 16)
            sp.dma_start(g2[:, :], t["rwkv_g2"]).then_inc(c_in, 16)
            sp.dma_start(lora[:, :, :], z_v[:, ZR + 12:ZR + 14]).then_inc(z_in[3], 16)
            for i in range(3):
                sp.dma_start(tri[i][:, :, :], z_v[:, ZR + RT * i:ZR + RT * (i + 1)]).then_inc(z_in[i], 16)
            sp.wait_ge(rows_kept, 4)
            sp.dma_start(t["new_shift_prompt"], rows[0:1, :]).then_inc(stored, 16)
            sp.dma_start(t["new_shift_sample"], rows[1:NB + 1, :]).then_inc(stored, 16)
            sp.wait_ge(lora_out, 3 * RT)
            sp.dma_start(feature_tiles(t["gT"], 0, TOK), gg[:, :, :]).then_inc(stored, 16)
            sp.wait_ge(chain, R_DONE[RT - 1])
            sp.dma_start(feature_tiles(t["bonusT"], 0, TOK), sw[:, :, :]).then_inc(stored, 16)
            sp.wait_ge(stored, 16 * 4)

        @block.gpsimd
        def _(pool):
            pool.wait_ge(flipped, 1)
            for n, i in enumerate(order):
                pool.wait_ge(z_in[i // RT if i < 12 else 3], 16)
                if n >= 2:
                    pool.wait_ge(shifted, n - 1)
                d, x = diff[:, n % 2], z(i)
                pool.tensor_tensor(d[:, 1:TOK], x[:, 0:TOK - 1], x[:, 1:TOK], ALU.subtract).then_inc(pooled, 1)
                pool.tensor_copy(last_cols[:, i, 0:1], x[:, SEQ - 1:SEQ]).then_inc(cols_kept, 1)
                pool.tensor_copy(last_cols[:, i, 1:NB + 1], sample(x)[:, :, NQ - 1]).then_inc(cols_kept, 1)
                pool.tensor_scalar(d[:, 0:1], x[:, 0:1], -1.0, None, ALU.mult).then_inc(diffed, 1)
                pool.wait_ge(pooled, n + 1)
                pool.tensor_tensor(sample(d)[:, :, 0], shift_cols[:, i], sample(x)[:, :, 0], ALU.subtract).then_inc(diffed, 1)

        @block.scalar
        def _(act):
            act.wait_ge(shifted, 2)
            act.activation(lora[0:64, 0], lora[0:64, 0], ACT.Tanh).then_inc(acts, 1)
            act.activation(lora[:, 1], lora[:, 1], ACT.Sigmoid).then_inc(acts, 1)
            for c in range(RT):
                for n, (dst, bias) in enumerate(((sw[:, c], "rwkv_w0"), (aa[:, c], "rwkv_a0"), (gg[:, c], None))):
                    act.wait_ge(lora_mm, 3 * c + n + 1)
                    src = three(3 * ((3 * c + n) % 2))
                    if bias:
                        act.activation(third(dst), src, ACT.Sigmoid, bias=vec(bias, c)).then_inc(lora_out, 1)
                    else:
                        act.activation(third(dst), src, ACT.Copy).then_inc(lora_out, 1)
            for c in range(RT):
                act.wait_ge(used, c + 1)
                act.activation(e[1][:, :], R["a"][:, c], ACT.Square).then_inc(acts, 1)
                act.wait_ge(sum_mm, c + 1)
                act.activation(third(R["b"][:, c]), three(3 * (c % 2)), ACT.Sqrt).then_inc(sum_out, 1)
            for c in range(RT):
                act.wait_ge(chain, R_CUM[c])
                act.activation(e[0][:, :], cum[:, :], ACT.Exp, scale=KAPPA).then_inc(expd, 1)
                act.activation(e[1][:, :], cum[:, :], ACT.Exp, scale=-KAPPA).then_inc(expd, 1)
                act.wait_ge(chain, R_PREV[c])
                act.activation(diff[:, 0], diff[:, 0], ACT.Exp, scale=-KAPPA).then_inc(expd, 1)

        @block.vector
        def _(dve):
            own = Chain(dve, chain)
            dve.wait_ge(flip, 1)
            dve.tensor_copy(shift_cols[:, :, :], ps[:, 7, 0:ZRT * NB].rearrange("p (i b) -> p i b", b=NB)).then_inc(flipped, 1)
            for n, i in enumerate(order):
                dve.wait_ge(diffed, 2 * n + 2)
                dve.wait_ge(cols_kept, 2 * n + 2)
                dve.scalar_tensor_tensor(z(i), diff[:, n % 2], vec("rwkv_mu", i), z(i), ALU.mult, ALU.add).then_inc(shifted, 1)
            for b in range(4):
                dve.wait_ge(rows_mm, b + 1)
                n = min(4, ZRT - 4 * b)
                dve.tensor_copy(rows[:, 4 * b * P:(4 * b + n) * P], ps[0:NB + 1, 6 + b % 2, 0:n * P]).then_inc(rows_kept, 1)
            dve.wait_ge(shifted, ZRT)
            for c in range(RT):
                dve.tensor_scalar(R["a"][:, c], R["k"][:, c], vec("rwkv_k_k", c), None, ALU.mult).then_inc(used, 1)
            for c in range(RT):
                dve.wait_ge(lora_out, 3 * c + 2)
                own.do(dve.tensor_scalar(diff[:, 1], aa[:, c], -1.0, vec("rwkv_k_a", c), ALU.add, ALU.mult))
                own.do(dve.scalar_tensor_tensor(R["k"][:, c], diff[:, 1], 1.0, R["k"][:, c], ALU.add, ALU.mult))
            for c in range(RT):
                dve.wait_ge(sum_out, c + 1)
                own.do(dve.tensor_scalar(R["b"][:, c], R["b"][:, c], 1e-12, None, ALU.max))
                own.do(dve.reciprocal(R["b"][:, c], R["b"][:, c]))
                own.do(dve.tensor_tensor(R["a"][:, c], R["a"][:, c], R["b"][:, c], ALU.mult))
                own.do(dve.tensor_tensor(R["b"][:, c], R["a"][:, c], aa[:, c], ALU.mult))
                own.do(dve.scalar_tensor_tensor(aa[:, c], R["r"][:, c], vec("rwkv_r_k", c), R["k"][:, c], ALU.mult, ALU.mult))
            for c in range(RT):
                own.do(dve.tensor_tensor_scan(cum[:, :], starts[:, :], sw[:, c], 0.0, ALU.mult, ALU.add))
                assert own.n == R_CUM[c]
                own.do(dve.tensor_tensor(diff[:, 0], cum[:, :], sw[:, c], ALU.subtract))
                assert own.n == R_PREV[c]
                dve.wait_ge(expd, 3 * c + 1)
                own.do(dve.tensor_tensor(R["b"][:, c], R["b"][:, c], e[0][:, :], ALU.mult))
                own.do(dve.tensor_tensor(R["k"][:, c], R["k"][:, c], e[0][:, :], ALU.mult))
                dve.wait_ge(expd, 3 * c + 2)
                own.do(dve.tensor_tensor(R["r"][:, c], R["r"][:, c], e[1][:, :], ALU.mult))
                own.do(dve.tensor_copy(R["pend"][:, c, 0:SEQ // CHUNK], e[1][:, CHUNK - 1:SEQ:CHUNK]))
                own.do(dve.tensor_copy(R["pend"][:, c, SEQ // CHUNK:], e[1][:, SEQ + NQ - 1:TOK:NQ]))
                dve.wait_ge(expd, 3 * c + 3)
                own.do(dve.scalar_tensor_tensor(R["a"][:, c], R["a"][:, c], -1.0, diff[:, 0], ALU.mult, ALU.mult))
                dve.wait_ge(sum_mm, RT + c + 1)
                own.do(dve.tensor_tensor(third(sw[:, c]), third(R["v"][:, c]), three(3 * (c % 2)), ALU.mult))
                assert own.n == R_DONE[c]

        @block.tensor
        def _(pe):
            pe.wait_ge(c_in, 16 * 6)
            for i in range(ZRT):
                ins = pe.transpose(ps[:, 7, i * NB:(i + 1) * NB], rows[0:NB, i * P:(i + 1) * P], S["ident"][0:NB, 0:NB])
            ins.then_inc(flip, 1)
            pe.wait_ge(acts, 2)
            for c in range(RT):
                for n in range(3):
                    i = 3 * c + n
                    if i >= 2:
                        pe.wait_ge(lora_out, i - 1)
                    for b, c0, c1 in C3:
                        w = (wl[0:64, c * P:(c + 1) * P], wl[64:P, c * P:(c + 1) * P], g2[:, c * P:(c + 1) * P])[n]
                        x = (lora[0:64, 0, c0:c1], lora[64:P, 0, c0:c1], lora[:, 1, c0:c1])[n]
                        ins = pe.matmul(ps[:, 3 * (i % 2) + b, 0:TOK // 3], w, x, start=True, stop=True)
                    ins.then_inc(lora_mm, 1)
            pe.wait_ge(cols_kept, 2 * ZRT)
            pe.wait_ge(flipped, 1)
            for b in range(4):
                if b >= 2:
                    pe.wait_ge(rows_kept, b - 1)
                for n in range(min(4, ZRT - 4 * b)):
                    ins = pe.transpose(ps[0:NB + 1, 6 + b % 2, n * P:(n + 1) * P], last_cols[:, 4 * b + n], S["ident"][:, :])
                ins.then_inc(rows_mm, 1)
            for c in range(RT):
                pe.wait_ge(acts, 2 + c + 1)
                if c < 2:
                    pe.wait_ge(lora_out, 3 * RT)
                else:
                    pe.wait_ge(sum_out, c - 1)
                for b, c0, c1 in C3:
                    ins = pe.matmul(ps[:, 3 * (c % 2) + b, 0:TOK // 3], R["block"][:, :], e[1][:, c0:c1], start=True, stop=True)
                ins.then_inc(sum_mm, 1)
            for c in range(RT):
                if c < 2:
                    pe.wait_ge(sum_out, RT)
                    pe.wait_ge(chain, R_CUM[0] - 1)
                else:
                    pe.wait_ge(chain, R_DONE[c - 2])
                for b, c0, c1 in C3:
                    ins = pe.matmul(ps[:, 3 * (c % 2) + b, 0:TOK // 3], R["block"][:, :], aa[:, c, c0:c1], start=True, stop=True)
                ins.then_inc(sum_mm, 1)


R_CUM = [7 * RT + 9 * c + 1 for c in range(RT)]
R_PREV = [n + 1 for n in R_CUM]
R_DONE = [n + 8 for n in R_CUM]


def plain_waits(eng, name, over, count_over):
    awaited = eng.alloc_register(name)

    def wait_count(sem, count):
        if isinstance(count, int):
            eng.wait_ge(sem, count)
        else:
            eng.reg_mov(awaited, count)
            eng.wait_ge(over, count_over)
            eng.wait_ge(sem, awaited)

    return wait_count


def operands(term, c, h):
    rows = slice(0, P) if any(isinstance(x, tuple) for x in term) else slice(64 * h, 64 * h + 64)
    pick = [x[h] if isinstance(x, tuple) else x for x in term]
    return [x[rows, c] if len(x.shape) == 3 else x[rows] for x in pick]


def rwkv_chunks(nc, t, S, R):
    with stage(nc, "rc_") as (ctx, sb, sem):
        ps = S["ps"]
        two = range(2)
        G = [P, RT, CHUNK]
        xin = [sb(f"xin{s}", [P, 8, RT, CHUNK]) for s in two]
        tok = [sb(f"tok{s}", [P, 4, RT, CHUNK]) for s in two]
        dg = [sb(f"dg{s}", [P, 2, RT, CHUNK]) for s in two]
        od = [sb(f"od{s}", [P, 2, RT, CHUNK]) for s in two]
        qm = [sb(f"qm{s}", [P, 3, RT, CHUNK]) for s in two]
        sq2, sq4 = ([sb(f"{n}{s}", [P, 2, RT, CHUNK]) for s in two] for n in ("sqa", "sqb"))
        m8 = [sb(f"m8{s}", G) for s in two]
        xb = [sb(f"x{s}", [P, 2, RT, CHUNK]) for s in two]
        x = [(xb[s][:, 0], xb[s][:, 1]) for s in two]
        r = [sb(f"r{s}", G) for s in two]
        hty = [sb(f"hty{s}", [P, 2, RT, CHUNK]) for s in two]
        w = [sb(f"w{s}", G) for s in two]
        mv = [sb(f"mv{s}", G) for s in two]
        va = [sb(f"va{s}", [P, 2, RT, CHUNK]) for s in two]
        u = [sb(f"u{s}", G) for s in two]
        st = [sb(f"st{s}", G) for s in two]
        eyes = sb("eyes", [P, 2, CHUNK])
        eye = (eyes[:, 0], eyes[:, 1])
        ones_on = sb("ones_on", G)
        masks = sb("masks", [P, 2, 6, RT, CHUNK])
        c_in, zeroed = sem("c_in"), sem("zeroed")
        fed, prod, kept_v, kept_a = ([sem(f"{n}{s}") for s in two] for n in ("fed", "prod", "kept_v", "kept_a"))
        NC = SEQ // CHUNK
        NJ = NC // 2
        at, bt, rt = ([(xin[s][:, 2 * i], xin[s][:, 2 * i + 1]) for s in two] for i in range(3))
        kt, vt = ([xin[s][:, i] for s in two] for i in (6, 7))
        feeds = [("a", 0, 0), ("a", 1, 1), ("b", 2, 0), ("b", 3, 1), ("k", 6, None), ("v", 7, None), ("r", 4, 0), ("r", 5, 1)]
        NF = len(feeds)
        on_head = lambda h: R["block"][:, 64 * h:64 * h + 1]
        bank = lambda s, b: ps[:, 4 * s + b, :].rearrange("p (x c t) -> p x c t", x=2, c=RT)
        zero = lambda j: isinstance(j, int) and j == 0
        NP, NA, NV = 21, 10, 14
        (TAB, TKV, MAB, QAR, QKR, SQ2, X2, SQ4, X3, SQ8, X4, HH, HTY, R2, R3, WW, MV, VA, UU, SS, YY) = range(NP)
        UD, UO, US, UI = 0, 2, 4, 5

        with nc.Block() as block:
            @block.sync
            def _(sp):
                sp.dma_start(masks[:, :, :, :, :], t["c_masks"].rearrange("p (a b c d) -> p a b c d", a=2, b=6, c=RT)).then_inc(c_in, 16)
                for c in range(RT):
                    sp.dma_start(ones_on[:, c], t["c_eye"][:, P:P + CHUNK]).then_inc(c_in, 16)
                sp.dma_start(eyes[:, :, :], t["c_eye"][:, 0:P].rearrange("p (h d) -> p h d", h=2)).then_inc(c_in, 16)

            @block.gpsimd
            def _(pool):
                wait_count = plain_waits(pool, "pool_awaited", c_in, 16 * (2 + RT))

                def feed(j, s):
                    for n, (src, i, h) in enumerate(feeds):
                        if not zero(j):
                            wait_count(prod[s], NP * (j - 1) + QKR + 1 if n < 6 else NP * j)
                        tokens = R[src][:, :, bass.ds((2 * j + s) * CHUNK, CHUNK)]
                        if h is None:
                            ins = pool.tensor_copy(xin[s][:, i], tokens)
                        else:
                            ins = pool.tensor_tensor(xin[s][:, i], tokens, on_head(h).unsqueeze(1).broadcast_to([P, RT, CHUNK]), ALU.mult)
                        ins.then_inc(fed[s], 1)
                feed(0, 0)
                feed(0, 1)
                with pool.Fori(1, NJ + 1) as j:
                    feed(j, 0)
                    feed(j, 1)

            @block.scalar
            def _(act):
                def keep(j, s, p, dst, frm):
                    act.wait_ge(prod[s], NP * j + p + 1)
                    act.activation(dst, frm, ACT.Copy).then_inc(kept_a[s], 1)

                def chunks(j):
                    for s in two:
                        keep(j, s, TAB, tok[s][:, 0:2], bank(s, 0))
                    for s in two:
                        keep(j, s, TKV, tok[s][:, 2:4], bank(s, 1))
                    for s in two:
                        keep(j, s, SQ2, sq2[s][:, :], bank(s, 1))
                    for s in two:
                        keep(j, s, SQ4, sq4[s][:, :], bank(s, 3))
                    for s in two:
                        keep(j, s, SQ8, m8[s][:, :], bank(s, 1)[:, 0])
                    for s in two:
                        keep(j, s, HTY, hty[s][:, :], bank(s, 0))
                    for s in two:
                        keep(j, s, WW, w[s][:, :], bank(s, 3)[:, 0])
                    for s in two:
                        keep(j, s, MV, mv[s][:, :], bank(s, 0)[:, 0])
                    for s in two:
                        keep(j, s, VA, va[s][:, :], bank(s, 1))

                with act.Fori(0, NJ) as j:
                    chunks(j)
                    for s in two:
                        keep(j, s, YY, R["a"][:, :, bass.ds((2 * j + s) * CHUNK, CHUNK)], bank(s, 0)[:, 0])
                chunks(NJ)

            @block.vector
            def _(dve):
                def chunks(j, kind):
                    mk = masks[:, kind]
                    for s in two:
                        dve.wait_ge(prod[s], NP * j + MAB + 1)
                        dve.tensor_tensor(dg[s][:, :], bank(s, 2), mk[:, UD:UD + 2], ALU.mult).then_inc(kept_v[s], 1)
                        dve.tensor_tensor(od[s][:, :], bank(s, 2), mk[:, UO:UO + 2], ALU.mult).then_inc(kept_v[s], 1)
                    for s in two:
                        dve.wait_ge(prod[s], NP * j + QAR + 1)
                        dve.tensor_tensor(qm[s][:, 0:2], bank(s, 3), mk[:, US:US + 2], ALU.mult).then_inc(kept_v[s], 1)
                    for s in two:
                        dve.wait_ge(prod[s], NP * j + QKR + 1)
                        dve.tensor_tensor(qm[s][:, 2], bank(s, 0)[:, 0], mk[:, UI], ALU.mult).then_inc(kept_v[s], 1)
                        dve.wait_ge(kept_v[s], NV * j + 1)
                        for h in two:
                            ins = dve.scalar_tensor_tensor(x[s][h], dg[s][:, 0], on_head(h), eye[h].unsqueeze(1).broadcast_to([P, RT, CHUNK]), ALU.mult, ALU.add)
                        ins.then_inc(kept_v[s], 1)
                    for n, (p, b) in enumerate(((X2, 2), (X3, 0), (X4, 2))):
                        for s in two:
                            dve.wait_ge(prod[s], NP * j + p + 1)
                            dve.wait_ge(kept_v[s], NV * j + 5 + n)
                            for h in two:
                                ins = dve.scalar_tensor_tensor(x[s][h], bank(s, b)[:, 0], on_head(h), x[s][h], ALU.mult, ALU.add)
                            ins.then_inc(kept_v[s], 1)
                    for p, b in ((HH, 3), (R2, 1), (R3, 2)):
                        for s in two:
                            dve.wait_ge(prod[s], NP * j + p + 1)
                            dve.tensor_tensor(r[s][:, :], bank(s, b)[:, 0], ones_on[:, :, :], ALU.add).then_inc(kept_v[s], 1)

                def states(j):
                    for s in two:
                        dve.wait_ge(prod[s], NP * j + UU + 1)
                        dve.wait_ge(kept_a[s], NA * j + 9)
                        dve.tensor_tensor(u[s][:, :], bank(s, 2)[:, 0], va[s][:, 0], ALU.add).then_inc(kept_v[s], 1)
                        dve.wait_ge(prod[s], NP * j + SS + 1)
                        if s == 1:
                            dve.wait_ge(prod[0], NP * (j + 1))
                        elif not zero(j):
                            dve.wait_ge(prod[1], NP * j)
                        nxt = st[1 - s]
                        dve.tensor_tensor(nxt[:, :], bank(s, 3)[:, 0], st[s][:, :], ALU.add).then_inc(kept_v[s], 1)
                        dve.wait_ge(kept_v[s], NV * j + 13)
                        dve.tensor_tensor(nxt[:, :], nxt[:, :], R["pend"][:, :, bass.ds(2 * j + s, 1)].broadcast_to([P, RT, CHUNK]), ALU.mult).then_inc(kept_v[s], 1)
                        dve.wait_ge(kept_v[s], NV * j + 14)

                dve.wait_ge(c_in, 16 * (2 + RT))
                dve.memset(st[0][:, :, :], 0.0).then_inc(zeroed, 1)
                dve.wait_ge(zeroed, 1)
                chunks(0, 0)
                states(0)
                with dve.Fori(1, NJ) as j:
                    chunks(j, 0)
                    states(j)
                chunks(NJ, 1)

            @block.tensor
            def _(pe):
                def each(s, b, g, *terms, inc=False):
                    for c in range(RT):
                        for h in range(2):
                            rows = slice(64 * h, 64 * h + 64)
                            for n, term in enumerate(terms):
                                lhs, rhs = operands(term, c, h)
                                ins = pe.matmul(bank(s, b)[rows, g, c], lhs, rhs, start=n == 0, stop=n == len(terms) - 1)
                    if inc:
                        ins.then_inc(prod[s], 1)

                def idle(s):
                    spin(pe, bank(s, 1)[:, 0], S, masks[:, 0, 0], SPIN_R)

                wait_count = plain_waits(pe, "pe_awaited", c_in, 16 * (2 + RT))

                def after(s, j, v=0, a=0, before_v=0, before_a=0, first=False):
                    if v:
                        wait_count(kept_v[s], NV * j + v)
                    if a:
                        wait_count(kept_a[s], NA * j + a)
                    if before_v and not first:
                        wait_count(kept_v[s], NV * (j - 1) + before_v)
                    if before_a and not first:
                        wait_count(kept_a[s], NA * (j - 1) + before_a)

                def chunks(j, first=False):
                    for s in two:
                        wait_count(fed[s], NF * j + 4)
                        after(s, j, before_a=10, first=first)
                        each(s, 0, 0, (at[s], eye))
                        each(s, 0, 1, (bt[s], eye), inc=True)
                    for s in two:
                        wait_count(fed[s], NF * j + 6)
                        after(s, j, before_a=9, first=first)
                        each(s, 1, 0, (kt[s], eye))
                        each(s, 1, 1, (vt[s], eye), inc=True)
                    for s in two:
                        after(s, j, before_v=12, first=first)
                        each(s, 2, 0, (bt[s], at[s]))
                        each(s, 2, 1, (at[s], bt[s]), inc=True)
                    for s in two:
                        wait_count(fed[s], NF * j + 8)
                        after(s, j, before_v=13, first=first)
                        each(s, 3, 0, (kt[s], at[s]))
                        each(s, 3, 1, (bt[s], rt[s]), inc=True)
                    for s in two:
                        after(s, j, a=1)
                        each(s, 0, 0, (kt[s], rt[s]), inc=True)
                    up, low = 0, 1
                    for s in two:
                        after(s, j, v=1, a=2)
                        each(s, 1, 0, (dg[s][:, low], dg[s][:, up]))
                        each(s, 1, 1, (dg[s][:, up], dg[s][:, low]), inc=True)
                    for s in two:
                        after(s, j, v=5, a=3)
                        each(s, 2, 0, (sq2[s][:, low], x[s]), inc=True)
                    for s in two:
                        each(s, 3, 0, (sq2[s][:, low], sq2[s][:, up]))
                        each(s, 3, 1, (sq2[s][:, up], sq2[s][:, low]), inc=True)
                    for s in two:
                        after(s, j, v=6, a=4)
                        each(s, 0, 0, (sq4[s][:, low], x[s]), inc=True)
                    for s in two:
                        each(s, 1, 0, (sq4[s][:, up], sq4[s][:, low]), inc=True)
                    for s in two:
                        after(s, j, v=7, a=5)
                        each(s, 2, 0, (m8[s], x[s]), inc=True)
                    for s in two:
                        after(s, j, v=8)
                        each(s, 3, 0, (od[s][:, low], x[s]), inc=True)
                    for s in two:
                        each(s, 0, 0, (x[s], od[s][:, low]))
                        each(s, 0, 1, (x[s], eye), inc=True)
                    for s in two:
                        after(s, j, v=9, a=6)
                        each(s, 1, 0, (hty[s][:, 0], r[s]), inc=True)
                    for s in two:
                        after(s, j, v=10)
                        each(s, 2, 0, (hty[s][:, 0], r[s]), inc=True)
                    for s in two:
                        after(s, j, v=11)
                        idle(s)
                        each(s, 3, 0, (hty[s][:, 1], r[s]), inc=True)
                    for s in two:
                        each(s, 0, 0, (qm[s][:, 0], tok[s][:, 3]), inc=True)
                    for s in two:
                        after(s, j, a=8)
                        each(s, 1, 0, (w[s], mv[s]))
                        each(s, 1, 1, (tok[s][:, 0], w[s]), inc=True)

                def states(j, first=False):
                    for s in two:
                        after(s, j, a=9)
                        idle(s)
                        if s == 1:
                            wait_count(kept_v[0], NV * (j + 1))
                        elif not first:
                            wait_count(kept_v[1], NV * j)
                        each(s, 2, 0, (va[s][:, 1], st[s]), inc=True)
                        idle(s)
                        after(s, j, v=12)
                        each(s, 3, 0, (tok[s][:, 1], u[s]), (tok[s][:, 2], tok[s][:, 3]), inc=True)
                        each(s, 0, 0, (st[s], rt[s]), (u[s], qm[s][:, 1]), (tok[s][:, 3], qm[s][:, 2]), inc=True)
                        idle(s)

                pe.wait_ge(c_in, 16 * (2 + RT))
                pe.wait_ge(zeroed, 1)
                for _ in range(4):
                    idle(1)
                chunks(0, True)
                states(0, True)
                with pe.Fori(1, NJ) as j:
                    chunks(j)
                    states(j)
                chunks(NJ)

        rwkv_states(nc, t, S, R, sb, sem, eye, rt, tok, qm, va, u, st)


def rwkv_states(nc, t, S, R, sb, sem, eye, rt, tok, qm, va, u, st):
    ps = S["ps"]
    two = range(2)
    sst = sb("sst", [P, NB, RT, CHUNK])
    stT = sb("stT", [P, NB, RT, CHUNK])
    ut = [sb(f"ut{s}", [P, RT, CHUNK]) for s in two]
    bk = [sb(f"bk{s}", [P, 2, RT, CHUNK]) for s in two]
    fin = sb("fin", [P, RT, CHUNK])
    rmask = sb("rmask", [P, 4])
    c_in, stored, turned, turned_a, turned_v, fin_mm, fin_out, ut_mm, ut_out, u_mm, u_out, y_mm, y_out = (sem(n) for n in
        ("s_c_in", "s_stored", "turned", "turned_a", "turned_v", "fin_mm", "fin_out", "ut_mm", "ut_out", "u_mm", "u_out", "y_mm", "y_out"))
    masked, new_mm, new_sum, new_done, back_mm, back_out = (sem(n) for n in ("masked", "new_mm", "new_sum", "new_done", "back_mm", "back_out"))
    bank = lambda b: ps[:, b, :].rearrange("p (x c t) -> p x c t", x=2, c=RT)
    heads_of = lambda a: a.rearrange("(c h) i j -> h i c j", h=2)
    with nc.Block() as block:
        @block.sync
        def _(sp):
            sp.dma_start(rmask[:, :], t["c_rmask"]).then_inc(c_in, 16)
            for b in range(NB):
                for h in range(2):
                    sp.dma_start(sst[64 * h:64 * h + 64, b], heads_of(t["state_rwkv"][b])[h]).then_inc(c_in, 16)
            sp.wait_ge(fin_out, 1)
            for h in range(2):
                sp.dma_start(heads_of(t["new_rwkv_prompt"])[h], fin[64 * h:64 * h + 64]).then_inc(stored, 16)
            for b in range(NB):
                sp.wait_ge(back_out, b + 1)
                for h in range(2):
                    sp.dma_start(heads_of(t["new_rwkv_sample"][b])[h], sst[64 * h:64 * h + 64, b]).then_inc(stored, 16)
            sp.wait_ge(stored, 16 * 2 * (NB + 1))

        @block.scalar
        def _(act):
            for g in (0, 2):
                act.wait_ge(turned, g + 1)
                act.activation(stT[:, 2 * g:2 * g + 2], bank(g), ACT.Copy).then_inc(turned_a, 1)
            for s in two:
                act.wait_ge(ut_mm, s + 1)
                act.activation(ut[s][:, :], bank(6 + s)[:, 0], ACT.Copy).then_inc(ut_out, 1)
            for s in two:
                act.wait_ge(y_mm, s + 1)
                act.activation(R["a"][:, :, SEQ + s * CHUNK:SEQ + (s + 1) * CHUNK], bank(6 + s)[:, 0], ACT.Copy).then_inc(y_out, 1)
            for b in range(NB):
                act.wait_ge(back_mm, b + 1)
                act.activation(sst[:, b], bank(4 + b % 2)[:, 0], ACT.Copy).then_inc(back_out, 1)

        @block.vector
        def _(dve):
            def update(b):
                dve.wait_ge(new_mm, b + 1)
                dve.tensor_tensor(stT[:, b], bank(b % 4)[:, 0], stT[:, b], ALU.add).then_inc(new_sum, 1)
                dve.wait_ge(new_sum, b + 1)
                pend = R["pend"][:, :, SEQ // CHUNK + b:SEQ // CHUNK + b + 1]
                dve.tensor_tensor(stT[:, b], stT[:, b], pend.broadcast_to([P, RT, CHUNK]), ALU.mult).then_inc(new_done, 1)

            for n, g in enumerate((1, 3)):
                dve.wait_ge(turned, g + 1)
                dve.tensor_copy(stT[:, 2 * g:2 * g + 2], bank(g)).then_inc(turned_v, 1)
            dve.wait_ge(fin_mm, 1)
            dve.tensor_copy(fin[:, :], bank(4)[:, 0]).then_inc(fin_out, 1)
            for s in two:
                dve.wait_ge(u_mm, s + 1)
                dve.tensor_tensor(u[s][:, :], bank(4 + s)[:, 0], va[s][:, 0], ALU.add).then_inc(u_out, 1)
            for b in range(NB):
                dve.wait_ge(c_in, 16 * (2 * NB + 1))
                if b >= 2:
                    dve.wait_ge(new_mm, b - 1)
                dve.tensor_scalar(bk[b % 2][:, :], tok[b // 4][:, 1:3], rmask[:, b % 4:b % 4 + 1], None, ALU.mult).then_inc(masked, 1)
                if b >= 1:
                    update(b - 1)
            update(NB - 1)

        @block.tensor
        def _(pe):
            def each(out, *terms, more=()):
                for c in range(RT):
                    for h in range(2):
                        rows = slice(64 * h, 64 * h + 64)
                        for n, term in enumerate(terms):
                            lhs, rhs = operands(term, c, h)
                            ins = pe.matmul(out[rows, c], lhs, rhs, start=n == 0, stop=n == len(terms) - 1 and not more)
                        for q, term in enumerate(more):
                            lhs, rhs = operands(term, c, h)
                            cols = slice(NQ * q, NQ * q + NQ)
                            ins = pe.matmul(out[rows, c, cols], lhs, rhs[:, cols], start=not terms, stop=not terms or q == 3)
                return ins

            def back(b):
                pe.wait_ge(new_done, b + 1)
                if b < 2:
                    pe.wait_ge(u_out, 2)
                else:
                    pe.wait_ge(back_out, b - 1)
                each(bank(4 + b % 2)[:, 0], (stT[:, b], eye)).then_inc(back_mm, 1)

            pe.wait_ge(c_in, 16 * (2 * NB + 1))
            for g in range(4):
                for i in two:
                    ins = each(bank(g)[:, i], (sst[:, 2 * g + i], eye))
                ins.then_inc(turned, 1)
            each(bank(4)[:, 0], (st[0], eye)).then_inc(fin_mm, 1)
            pe.wait_ge(turned_a, 2)
            pe.wait_ge(turned_v, 2)
            for s in two:
                each(bank(6 + s)[:, 0], more=[(stT[:, 4 * s + q], va[s][:, 1]) for q in range(4)]).then_inc(ut_mm, 1)
            for s in two:
                pe.wait_ge(ut_out, s + 1)
                if s == 0:
                    pe.wait_ge(fin_out, 1)
                each(bank(4 + s)[:, 0], (ut[s], eye)).then_inc(u_mm, 1)
            for s in two:
                pe.wait_ge(u_out, s + 1)
                each(bank(6 + s)[:, 0], (u[s], qm[s][:, 1]), (tok[s][:, 3], qm[s][:, 2]),
                     more=[(stT[:, 4 * s + q], rt[s]) for q in range(4)]).then_inc(y_mm, 1)
            for b in range(NB):
                pe.wait_ge(masked, b + 1)
                if b >= 4:
                    pe.wait_ge(new_sum, b - 3)
                each(bank(b % 4)[:, 0], (bk[b % 2][:, 0], u[b // 4]), (bk[b % 2][:, 1], tok[b // 4][:, 3])).then_inc(new_mm, 1)
                if b >= 1:
                    back(b - 1)
            back(NB - 1)


def rwkv_output(nc, t, S, R):
    with stage(nc, "ro_") as (ctx, sb, sem):
        ps = S["ps"]
        out = sb("out", [P, RT, TOK])
        in_, cent_mm, centred, squared, scaled, shifted, summed, var_mm, rooted, chain, done, stored = (sem(n) for n in
            ("in_", "cent_mm", "centred", "squared", "scaled", "shifted", "summed", "var_mm", "rooted", "chain", "done", "stored"))
        block = ctx.enter_context(nc.Block())
        y, g, bonus, sq, root = R["a"], R["b"], R["k"], R["v"], R["r"]
        vec = lambda name, k: S["vec"][:, VEC_AT[name] + k:VEC_AT[name] + k + 1]
        third = lambda a: a.rearrange("p (n t) -> p n t", n=3)
        three = lambda i: ps[:, 3 * (i % 2):3 * (i % 2) + 3, 0:TOK // 3]

        @block.sync
        def _(sp):
            sp.dma_start(g[:, :, :], feature_tiles(t["gT"], 0, TOK)).then_inc(in_, 16)
            sp.dma_start(bonus[:, :, :], feature_tiles(t["bonusT"], 0, TOK)).then_inc(in_, 16)
            for c in range(RT):
                sp.wait_ge(done, c + 1)
                sp.dma_start(feature_tiles(t["rwT"], 0, TOK)[:, c], out[:, c]).then_inc(stored, 16)
            sp.wait_ge(stored, 16 * RT)

        @block.scalar
        def _(act):
            def square(c):
                act.wait_ge(centred, c + 1)
                act.activation(sq[:, c], y[:, c], ACT.Square).then_inc(squared, 1)

            def take_root(c):
                act.wait_ge(var_mm, c + 1)
                act.activation(third(root[:, c]), three(c), ACT.Sqrt, bias=S["lnx_eps"][:, 0:1], scale=1.0 / 64).then_inc(rooted, 1)

            def shift(c):
                act.wait_ge(scaled, c + 1)
                act.activation(out[:, c], out[:, c], ACT.Identity, bias=vec("rwkv_lnx_b", c), scale=vec("rwkv_lnx_g", c)).then_inc(shifted, 1)

            square(0)
            square(1)
            take_root(0)
            take_root(1)
            square(2)
            shift(0)
            square(3)
            take_root(2)
            take_root(3)
            for c in range(1, RT):
                shift(c)

        @block.gpsimd
        def _(pool):
            pool.wait_ge(in_, 32)
            for c in range(RT):
                pool.wait_ge(shifted, c + 1)
                pool.tensor_tensor(out[:, c], out[:, c], bonus[:, c], ALU.add).then_inc(summed, 1)
                pool.wait_ge(summed, c + 1)
                pool.tensor_tensor(out[:, c], out[:, c], g[:, c], ALU.mult).then_inc(done, 1)

        @block.vector
        def _(dve):
            own = Chain(dve, chain)

            def centre(c):
                dve.wait_ge(cent_mm, c + 1)
                dve.scalar_tensor_tensor(third(y[:, c]), three(c), -1.0 / 64, third(y[:, c]), ALU.mult, ALU.add).then_inc(centred, 1)

            centre(0)
            centre(1)
            for c in range(RT):
                dve.wait_ge(rooted, c + 1)
                own.do(dve.reciprocal(root[:, c], root[:, c]))
                dve.tensor_tensor(out[:, c], y[:, c], root[:, c], ALU.mult).then_inc(scaled, 1)
                if c + 2 < RT:
                    centre(c + 2)

        @block.tensor
        def _(pe):
            def head_sums(x, c, to):
                for b in range(3):
                    ins = pe.matmul(ps[:, 3 * (c % 2) + b, 0:TOK // 3], R["block"][:, :], x[:, c, b * (TOK // 3):(b + 1) * (TOK // 3)], start=True, stop=True)
                ins.then_inc(to, 1)

            for c in (0, 2):
                for i in (c, c + 1):
                    if i >= 2:
                        pe.wait_ge(rooted, i - 1)
                    head_sums(y, i, cent_mm)
                for i in (c, c + 1):
                    pe.wait_ge(centred, i + 1)
                    pe.wait_ge(squared, i + 1)
                    head_sums(sq, i, var_mm)


def rwkv(nc, t, S):
    with ExitStack() as ctx:
        sb = lambda n, s: ctx.enter_context(nc.sbuf_tensor("rw_" + n, s, F32))
        R = {n: sb(n, [P, RT, TOK]) for n in ("r", "k", "v", "a", "b")}
        R["pend"] = sb("pend", [P, RT, SEQ // CHUNK + NB])
        R["block"] = sb("block", [P, P])
        rwkv_prepare(nc, t, S, R)
        rwkv_chunks(nc, t, S, R)
        rwkv_output(nc, t, S, R)


def shared(nc, ctx):
    sb = lambda n, s, d=F32: ctx.enter_context(nc.sbuf_tensor(n, s, d))
    return {"ident": sb("ident", [P, P]), "ones": sb("ones", [P, P]), "eps": sb("eps_col", [P, 1]),
            "lnx_eps": sb("lnx_eps_col", [P, 1]), "vec": sb("vec", [P, NVEC]),
            "neg_lam": sb("neg_lam", [P, 1]), "qk_sample": sb("qk_sample", [P, 8, NB * NQ]),
            "ps": ctx.enter_context(nc.psum_tensor("ps", [P, 8, 512], F32))}


def constants():
    f = np.float32
    pos = np.concatenate([np.arange(SEQ), np.tile(PAST + np.arange(NQ), NB)]).astype(f)
    inv = (f(10000.0) ** (-np.arange(32, dtype=f) / f(32))).astype(f)
    ang = (pos[None, :] * inv[:, None]).astype(f).astype(np.float64)
    rot = np.zeros((P, P), f)
    for d in range(P):
        rot[d + 32 if d % 64 < 32 else d - 32, d] = -1 if d % 64 < 32 else 1
    mask = np.zeros((1, P + CHUNK), f)
    mask[0, :CHUNK] = 1
    mask[0, P:] = -1e30
    pick, sign = np.zeros((P, 64), f), np.zeros((P, 2), f)
    for h in range(HEADS):
        for m in range(2):
            for q in range(NQ):
                row = h * 2 * NQ + m * NQ + q
                pick[row, h * NQ + q] = 1
                sign[row, m] = 1
    starts = np.ones((P, TOK), f)
    starts[:, 0:SEQ:CHUNK] = 0
    starts[:, SEQ::NQ] = 0
    row, col = np.arange(P)[:, None] % 64, np.arange(64)[None, :]
    same = row // NQ == col // NQ
    upper, lower = col > row, col < row
    diag = [upper & same, lower & same]
    kinds = [diag + [upper & ~same, lower & ~same, upper, upper | (col == row)],
             diag + [upper & False, lower & False, upper & same, (upper | (col == row)) & same]]
    masks = np.stack([np.stack([np.repeat(m[:, None], RT, 1) for m in k], 1) for k in kinds], 1).astype(f)
    eye = np.eye(P, dtype=f)
    extra = {"c_starts": starts, "c_masks": masks.reshape(P, -1), "c_eye": np.concatenate([eye, eye[:, :CHUNK] + eye[:, CHUNK:]], 1),
             "c_block": np.kron(np.eye(2, dtype=f), np.ones((64, 64), f)),
             "c_rmask": (row // NQ == np.arange(4)[None, :]).astype(f)}
    return {**extra, "c_ident": np.eye(P, dtype=f), "c_rot": rot, "c_cos": np.tile(np.cos(ang), (4, 1)).astype(f),
            "c_sin": np.tile(np.sin(ang), (4, 1)).astype(f), "c_mask": mask, "c_pick": pick, "c_sign": sign}


def store_output(nc, t, S):
    with stage(nc, "so_") as (ctx, sb, sem):
        ps = S["ps"]
        xfeat = sb("xfeat", [P, DT, TOK])
        xtok = sb("xtok", [P, TOK // P, D])
        x_in, half_t, copied_a, copied_v, stored = (sem(n) for n in ("x_in", "half_t", "copied_a", "copied_v", "stored"))
        block = ctx.enter_context(nc.Block())
        NT = TOK // P
        units = [(m, f) for m in range(NT) for f in range(2)]

        @block.sync
        def _(sp):
            sp.dma_start(xfeat[:, :, :], feature_tiles(t["res3"], 0, TOK)).then_inc(x_in, 16)
            for m in range(NT):
                sp.wait_ge(copied_a, m + 1)
                sp.wait_ge(copied_v, m + 1)
                dst = t["y_prompt"][0, m * P:(m + 1) * P] if m < NT - 1 else t["y_sample"].rearrange("b s d -> (b s) d")
                sp.dma_start(dst, xtok[:, m, :]).then_inc(stored, 16)
            sp.wait_ge(stored, 16 * NT)

        @block.tensor
        def _(pe):
            pe.wait_ge(x_in, 16)
            for n, (m, f) in enumerate(units):
                if n >= 4:
                    pe.wait_ge(copied_a if n % 2 == 0 else copied_v, (n - 4) // 2 + 1)
                for i in range(4):
                    ins = pe.transpose(ps[:, n % 4, i * P:(i + 1) * P], xfeat[:, 4 * f + i, m * P:(m + 1) * P], S["ident"][:, :])
                ins.then_inc(half_t, 1)

        @block.scalar
        def _(act):
            for m in range(NT):
                act.wait_ge(half_t, 2 * m + 1)
                act.activation(xtok[:, m, 0:512], ps[:, (2 * m) % 4, :], ACT.Copy).then_inc(copied_a, 1)

        @block.vector
        def _(dve):
            for m in range(NT):
                dve.wait_ge(half_t, 2 * m + 2)
                dve.tensor_copy(xtok[:, m, 512:1024], ps[:, (2 * m + 1) % 4, :]).then_inc(copied_v, 1)


SCRATCH = [("res0", (D, TOK)), ("res1", (D, TOK)), ("res2", (D, TOK)), ("res3", (D, TOK)), ("zT", (Z_TILES * P, TOK)),
           ("attT", (D // 2, TOK)), ("rwT", (D // 2, TOK)), ("gT", (D // 2, TOK)), ("bonusT", (D // 2, TOK))]


def program(nc, t):
    for name, shape in SCRATCH:
        t[name] = nc.dram_tensor(name + "_scratch", shape, F32, kind="Internal").ap()
    with ExitStack() as ctx:
        S = shared(nc, ctx)
        load_inputs(nc, t, S)
        for half in range(2):
            ffn_half(nc, t, S, f"fa{half}_", half, t["res0"], t["res1"], t["ffn1_w_in"], t["ffn1_w_out"], "ffn1_pre_g", "ffn1_post_g")
        in_projection(nc, t, S)
        prompt_attention(nc, t, S)
        sample_attention(nc, t, S)
        rwkv(nc, t, S)
        for half in range(2):
            out_projection_half(nc, t, S, f"op{half}_", half)
        for half in range(2):
            ffn_half(nc, t, S, f"fb{half}_", half, t["res2"], t["res3"], t["ffn2_w_in"], t["ffn2_w_out"], "ffn2_pre_g", "ffn2_post_g")
        store_output(nc, t, S)


INPUTS = ["x_prompt", "x_sample", "cache_att_k", "cache_att_v", "state_rwkv", "state_shift", "ffn1_pre_g", "ffn1_w_in",
          "ffn1_w_out", "ffn1_post_g", "mix_pre_g", "w_in", "att_lambda_q1", "att_lambda_k1", "att_lambda_q2",
          "att_lambda_k2", "att_subln_g", "rwkv_mu", "rwkv_w0", "rwkv_w2", "rwkv_a0", "rwkv_a2", "rwkv_g2", "rwkv_k_k",
          "rwkv_k_a", "rwkv_r_k", "rwkv_lnx_g", "rwkv_lnx_b", "w_o_att", "w_o_rwkv", "w_out", "mix_post_g",
          "ffn2_pre_g", "ffn2_w_in", "ffn2_w_out", "ffn2_post_g"]
AS = {"cache_att_k": (NB, PAST, D // 2), "cache_att_v": (NB, PAST, D // 2), "state_rwkv": (NB, 8, 64, 64),
      "ffn1_w_in": (D, 2 * FF), "ffn1_w_out": (FF, D), "w_in": (D, Z_TILES * P), "rwkv_w2": (64, D // 2),
      "rwkv_a2": (64, D // 2), "rwkv_g2": (P, D // 2), "w_o_att": (D // 2, D), "w_o_rwkv": (D // 2, D),
      "w_out": (D, D), "ffn2_w_in": (D, 2 * FF), "ffn2_w_out": (FF, D)}
OUTPUTS = [("y_prompt", (1, SEQ, D), (1, SEQ, D)), ("y_sample", (NB, NQ, D), (NB, NQ, D)),
           ("new_k_prompt", (SEQ, D // 2), (1, 1, SEQ, HEADS, 2, 64)), ("new_v_prompt", (SEQ, D // 2), (1, 1, SEQ, HEADS, P)),
           ("new_rwkv_prompt", (8, 64, 64), (1, 1, 8, 64, 64)), ("new_shift_prompt", (1, ZRT * P), (1, 1, 1, ZRT * P)),
           ("new_k_sample", (NB * NQ, D // 2), (1, NB, NQ, HEADS, 2, 64)), ("new_v_sample", (NB * NQ, D // 2), (1, NB, NQ, HEADS, P)),
           ("new_rwkv_sample", (NB, 8, 64, 64), (1, NB, 8, 64, 64)), ("new_shift_sample", (NB, ZRT * P), (1, NB, 1, ZRT * P))]


def kernel(**inputs):
    import concourse.bacc as bacc
    from concourse.bass_utils import run_bass_kernel_spmd

    nc = bacc.Bacc("TRN2", target_bir_lowering=False, num_devices=1)
    arrays, t = {}, {}
    shaped = {name: np.ascontiguousarray(inputs[name]).reshape(AS.get(name, inputs[name].shape)) for name in INPUTS}
    for name, a in {**shaped, **constants()}.items():
        arrays[f"in_{name}_dram"] = a
        t[name] = nc.dram_tensor(f"in_{name}_dram", a.shape, mybir.dt.from_np(a.dtype), kind="ExternalInput").ap()
    for i, (name, shape, _) in enumerate(OUTPUTS):
        t[name] = nc.dram_tensor(f"out_{i}_dram", shape, F32, kind="ExternalOutput").ap()
    program(nc, t)
    r = run_bass_kernel_spmd(nc, [arrays], core_ids=[0])
    return tuple(r.results[0][f"out_{i}_dram"].reshape(full) for i, (_, _, full) in enumerate(OUTPUTS))
```
